# Optimizing a Trainium2 kernel written in Bass

```python
import math
import jax, jax.numpy as jnp
from jax import lax
import numpy as np

D_MODEL = 2048
BATCH = 1
SEQ = 256
DEPTH = 1

GDN_HEADS = 8
GDN_DK = 128
GDN_DV = 128
GDN_CONV = 5
GDN_CHUNK = 64
DIFF_HEADS = 8
DIFF_DH = 64
DIFF_DV = 2 * DIFF_DH
Q_BLOCK = 128
N_GROUPS = 4
EXPERTS_PER_GROUP = 8
N_EXPERTS = N_GROUPS * EXPERTS_PER_GROUP
TOP_K = 2
D_EXPERT = 512
MOE_TOKEN_BLOCK = 1024
EPS = 1e-6

GDN_QK = GDN_HEADS * GDN_DK
GDN_V = GDN_HEADS * GDN_DV
DIFF_QK = DIFF_HEADS * 2 * DIFF_DH
DIFF_V = DIFF_HEADS * DIFF_DV
SPLITS = [GDN_QK, GDN_QK, GDN_V, GDN_V, 2 * GDN_HEADS, 2 * GDN_HEADS,
          DIFF_QK, DIFF_QK, DIFF_V, D_MODEL, D_MODEL]
D_IN = sum(SPLITS)

kernel_name = "hybrid_gdn_diffattn_hiermoe_encoder"

F32 = jnp.float32

def rms_norm(x, g):
    xf = x.astype(F32)
    y = xf * lax.rsqrt(jnp.mean(xf * xf, axis=-1, keepdims=True) + EPS)
    return (y * g.astype(F32)).astype(x.dtype)

def l2norm(t):
    return t * lax.rsqrt(jnp.sum(t * t, axis=-1, keepdims=True) + EPS)

def centred_depthwise_conv(x, w):
    K, C = w.shape
    pad = K // 2
    return lax.conv_general_dilated(
        x, w[:, None, :].astype(x.dtype), window_strides=(1,), padding=[(pad, pad)],
        dimension_numbers=("NWC", "WIO", "NWC"), feature_group_count=C)

def gated_delta_chunked(q, k, v, g, beta):
    B_, H, S, dk = q.shape
    dv = v.shape[-1]
    C = GDN_CHUNK
    N = S // C
    q = q.reshape(B_, H, N, C, dk)
    k = k.reshape(B_, H, N, C, dk)
    v = v.reshape(B_, H, N, C, dv)
    g_cum = jnp.cumsum(g.reshape(B_, H, N, C), axis=-1)
    beta = beta.reshape(B_, H, N, C)
    lower = jnp.tril(jnp.ones((C, C), bool))
    strict = jnp.tril(jnp.ones((C, C), bool), -1)
    decay = jnp.exp(jnp.where(lower, g_cum[..., :, None] - g_cum[..., None, :], -jnp.inf))
    k_beta = k * beta[..., None]
    L = jnp.where(strict, jnp.einsum("bhncd,bhnsd->bhncs", k_beta, k) * decay, 0.0)
    A = L + jnp.eye(C, dtype=F32)
    u = lax.linalg.triangular_solve(A, v * beta[..., None], left_side=True, lower=True, unit_diagonal=True)
    w = lax.linalg.triangular_solve(A, k_beta * jnp.exp(g_cum)[..., None], left_side=True, lower=True,
                                    unit_diagonal=True)
    attn = jnp.einsum("bhncd,bhnsd->bhncs", q, k) * decay

    def step(state, inp):
        q_c, k_c, u_c, w_c, attn_c, gc = inp
        v_new = u_c - jnp.einsum("bhcd,bhde->bhce", w_c, state)
        o = (jnp.einsum("bhcd,bhde->bhce", q_c * jnp.exp(gc)[..., None], state)
             + jnp.einsum("bhcs,bhse->bhce", attn_c, v_new))
        g_last = gc[..., -1]
        state = (state * jnp.exp(g_last)[..., None, None]
                 + jnp.einsum("bhcd,bhce->bhde", k_c * jnp.exp(g_last[..., None] - gc)[..., None], v_new))
        return state, o

    xs = tuple(jnp.moveaxis(t, 2, 0) for t in (q, k, u, w, attn, g_cum))
    state0 = jnp.zeros((B_, H, dk, dv), F32)
    _, o = lax.scan(step, state0, xs)
    return jnp.moveaxis(o, 0, 2).reshape(B_, H, S, dv)

def diff_attention(q, k, v, lam):
    B_, H, _, S, dh = q.shape
    dv = v.shape[-1]
    nb = S // Q_BLOCK
    scale = dh ** -0.5
    slopes = jnp.exp2(-8.0 * (jnp.arange(H, dtype=F32) + 1.0) / H)
    kpos = jnp.arange(S)
    qb = jnp.moveaxis(q.reshape(B_, H, 2, nb, Q_BLOCK, dh), 3, 0)

    def block(args):
        qi, start = args
        s = jnp.einsum("bhmqd,bhmkd->bhmqk", qi, k).astype(F32) * scale
        qpos = start + jnp.arange(Q_BLOCK)
        dist = jnp.abs(qpos[:, None] - kpos[None, :]).astype(F32)
        s = s - slopes[None, :, None, None, None] * dist
        p = jax.nn.softmax(s, axis=-1)
        pd = p[:, :, 0] - lam * p[:, :, 1]
        return jnp.einsum("bhqk,bhkd->bhqd", pd.astype(v.dtype), v)

    out = lax.map(block, (qb, jnp.arange(nb) * Q_BLOCK))
    return out.transpose(1, 2, 0, 3, 4).reshape(B_, H, S, dv)

def token_mixers(h, layer, w_in, conv_w, a_log, dt_bias, gdn_norm_w, diff_lambda, diff_norm_w,
                 w_branch_a, w_branch_d, w_out):
    B_, S, _ = h.shape
    p = h @ w_in
    idx = np.cumsum(SPLITS)[:-1].tolist()
    q_a, k_a, v_a, z_a, a_a, b_a, q_d, k_d, v_d, gate_a, gate_d = jnp.split(p, idx, axis=-1)

    qkv = jax.nn.silu(centred_depthwise_conv(jnp.concatenate([q_a, k_a, v_a], axis=-1), conv_w))
    q_a, k_a, v_a = jnp.split(qkv.astype(F32), [GDN_QK, 2 * GDN_QK], axis=-1)
    to_heads = lambda t, d: t.reshape(B_, S, GDN_HEADS, d).transpose(0, 2, 1, 3)
    q_a = l2norm(to_heads(q_a, GDN_DK)) * (GDN_DK ** -0.5)
    k_a = l2norm(to_heads(k_a, GDN_DK))
    v_a = to_heads(v_a, GDN_DV)
    a_a = a_a.astype(F32).reshape(B_, S, 2, GDN_HEADS).transpose(2, 0, 3, 1)
    b_a = b_a.astype(F32).reshape(B_, S, 2, GDN_HEADS).transpose(2, 0, 3, 1)
    g = -jnp.exp(a_log.astype(F32))[:, None, :, None] * jax.nn.softplus(
        a_a + dt_bias.astype(F32)[:, None, :, None])
    beta = jax.nn.sigmoid(b_a)
    flip = lambda t: jnp.flip(t, axis=2)
    o_fwd = gated_delta_chunked(q_a, k_a, v_a, g[0], beta[0])
    o_bwd = flip(gated_delta_chunked(flip(q_a), flip(k_a), flip(v_a), flip(g[1]), flip(beta[1])))
    o = (o_fwd + o_bwd).transpose(0, 2, 1, 3)
    z = z_a.astype(F32).reshape(B_, S, GDN_HEADS, GDN_DV)
    y_a = (rms_norm(o, gdn_norm_w) * jax.nn.silu(z)).reshape(B_, S, GDN_V).astype(h.dtype)

    lam_init = 0.8 - 0.6 * math.exp(-0.3 * layer)
    lf = diff_lambda.astype(F32)
    lam = jnp.exp(jnp.sum(lf[0] * lf[1])) - jnp.exp(jnp.sum(lf[2] * lf[3])) + lam_init
    qd = q_d.reshape(B_, S, DIFF_HEADS, 2, DIFF_DH).transpose(0, 2, 3, 1, 4)
    kd = k_d.reshape(B_, S, DIFF_HEADS, 2, DIFF_DH).transpose(0, 2, 3, 1, 4)
    vd = v_d.reshape(B_, S, DIFF_HEADS, DIFF_DV).transpose(0, 2, 1, 3)
    od = diff_attention(qd, kd, vd, lam).transpose(0, 2, 1, 3)
    y_d = (rms_norm(od, diff_norm_w) * (1.0 - lam_init)).reshape(B_, S, DIFF_V).astype(h.dtype)

    merged = (jax.nn.sigmoid(gate_a) * (y_a @ w_branch_a)
              + jax.nn.sigmoid(gate_d) * (y_d @ w_branch_d))
    return merged @ w_out

def hier_moe(h, w_group, b_group, w_router, b_router, w_gate, w_up, w_down):
    B_, S, D = h.shape
    t = h.reshape(-1, D)
    T = t.shape[0]
    g_logits = (t @ w_group).astype(F32) + b_group.astype(F32)
    g_probs = jax.nn.softmax(g_logits, axis=-1)
    g_idx = jnp.argmax(g_logits, axis=-1)
    g_w = jnp.take_along_axis(g_probs, g_idx[:, None], axis=-1)
    e_logits = ((t @ w_router).astype(F32) + b_router.astype(F32)).reshape(T, N_GROUPS, EXPERTS_PER_GROUP)
    e_sel = jnp.take_along_axis(e_logits, g_idx[:, None, None], axis=1)[:, 0]
    top_v, top_i = lax.top_k(jax.nn.softmax(e_sel, axis=-1), TOP_K)
    weights = top_v / jnp.sum(top_v, axis=-1, keepdims=True) * g_w
    expert_id = g_idx[:, None] * EXPERTS_PER_GROUP + top_i
    combine = jnp.sum(jax.nn.one_hot(expert_id, N_EXPERTS, dtype=F32) * weights[..., None], axis=1)

    blk = math.gcd(T, MOE_TOKEN_BLOCK)
    nb = T // blk

    def expert_block(args):
        tb, cb = args
        hid = jax.nn.silu(jnp.einsum("td,edf->tef", tb, w_gate)) * jnp.einsum("td,edf->tef", tb, w_up)
        return jnp.einsum("tef,efd->td", hid * cb[..., None].astype(hid.dtype), w_down)

    y = lax.map(expert_block, (t.reshape(nb, blk, D), combine.reshape(nb, blk, N_EXPERTS)))
    return y.reshape(B_, S, D)

def setup_inputs(seed: int = 0) -> dict:
    key = jax.random.key(seed)
    ks = jax.random.split(key, 24)
    nrm = lambda k, shape, scale: jax.random.normal(k, shape, F32) * scale
    gain = lambda k, shape: 1.0 + 0.01 * jax.random.normal(k, shape, F32)
    dt = jnp.exp(jax.random.uniform(ks[5], (DEPTH, 2, GDN_HEADS), F32, math.log(1e-3), math.log(1e-1)))
    return {
        "x": nrm(ks[0], (BATCH, SEQ, D_MODEL), 1.0),
        "g_mix": gain(ks[1], (DEPTH, D_MODEL)),
        "w_in": nrm(ks[2], (DEPTH, D_MODEL, D_IN), D_MODEL ** -0.5),
        "conv_w": nrm(ks[3], (DEPTH, GDN_CONV, 2 * GDN_QK + GDN_V), GDN_CONV ** -0.5),
        "a_log": jnp.log(jax.random.uniform(ks[4], (DEPTH, 2, GDN_HEADS), F32, 1.0, 16.0)),
        "dt_bias": dt + jnp.log(-jnp.expm1(-dt)),
        "gdn_norm_w": gain(ks[6], (DEPTH, GDN_DV)),
        "diff_lambda": nrm(ks[7], (DEPTH, 4, DIFF_DH), 0.1),
        "diff_norm_w": gain(ks[8], (DEPTH, DIFF_DV)),
        "w_branch_a": nrm(ks[9], (DEPTH, GDN_V, D_MODEL), GDN_V ** -0.5),
        "w_branch_d": nrm(ks[10], (DEPTH, DIFF_V, D_MODEL), DIFF_V ** -0.5),
        "w_out": nrm(ks[11], (DEPTH, D_MODEL, D_MODEL), D_MODEL ** -0.5),
        "g_ffn": gain(ks[12], (DEPTH, D_MODEL)),
        "w_group": nrm(ks[13], (DEPTH, D_MODEL, N_GROUPS), D_MODEL ** -0.5),
        "b_group": nrm(ks[14], (DEPTH, N_GROUPS), 0.01),
        "w_router": nrm(ks[15], (DEPTH, D_MODEL, N_EXPERTS), D_MODEL ** -0.5),
        "b_router": nrm(ks[16], (DEPTH, N_EXPERTS), 0.01),
        "w_exp_gate": nrm(ks[17], (DEPTH, N_EXPERTS, D_MODEL, D_EXPERT), D_MODEL ** -0.5),
        "w_exp_up": nrm(ks[18], (DEPTH, N_EXPERTS, D_MODEL, D_EXPERT), D_MODEL ** -0.5),
        "w_exp_down": nrm(ks[19], (DEPTH, N_EXPERTS, D_EXPERT, D_MODEL), D_EXPERT ** -0.5),
        "g_final": gain(ks[20], (D_MODEL,)),
    }

def reference(x, g_mix, w_in, conv_w, a_log, dt_bias, gdn_norm_w, diff_lambda, diff_norm_w,
              w_branch_a, w_branch_d, w_out, g_ffn, w_group, b_group, w_router, b_router,
              w_exp_gate, w_exp_up, w_exp_down, g_final):
    for layer in range(DEPTH):
        h = rms_norm(x, g_mix[layer])
        x = x + token_mixers(h, layer, w_in[layer], conv_w[layer], a_log[layer], dt_bias[layer],
                             gdn_norm_w[layer], diff_lambda[layer], diff_norm_w[layer],
                             w_branch_a[layer], w_branch_d[layer], w_out[layer])
        h = rms_norm(x, g_ffn[layer])
        x = x + hier_moe(h, w_group[layer], b_group[layer], w_router[layer], b_router[layer],
                         w_exp_gate[layer], w_exp_up[layer], w_exp_down[layer])
    return rms_norm(x, g_final)


_drawn_inputs = setup_inputs


def setup_inputs(seed=0):
    import zlib

    import numpy as np

    out = dict(_drawn_inputs(seed))
    spreads = {}
    factors = {'g_mix': 2.763,
     'gdn_norm_w': 3.866,
     'diff_norm_w': 5.784,
     'g_ffn': 3.082,
     'b_group': 3.436,
     'b_router': 3.916,
     'g_final': 5.763}
    for name, (base, spread) in spreads.items():
        noise = np.random.default_rng([zlib.crc32(name.encode()), seed]).standard_normal(out[name].shape)
        drawn = base * np.exp(spread * noise) if base else spread * noise
        out[name] = __import__('jax').numpy.asarray(drawn.astype(out[name].dtype))
    for name, factor in factors.items():
        out[name] = (out[name] * factor).astype(out[name].dtype)
    return out
```

```python
import math
from contextlib import ExitStack

import concourse.bass as bass
from concourse import mybir

F32 = mybir.dt.float32
I32 = mybir.dt.int32
ALU = mybir.AluOpType
ACT = mybir.ActivationFunctionType
AX = mybir.AxisListType

P = 128
D = 2048
T = 256
TT = T // P
KC = D // P
HEADS = 8
DK = 128
CH = 64
DH = 64
NG, EPG = 4, 8
NE = NG * EPG
FE = 512
SLOTS = 64
ROUNDS = T // SLOTS
EPS = 1e-6
LAM_INIT = 0.8 - 0.6 * math.exp(-0.3 * 0)

QK = HEADS * DK
OFF_Q, OFF_K, OFF_V, OFF_Z = 0, QK, 2 * QK, 3 * QK
OFF_AB = 4 * QK
OFF_AQ = OFF_AB + 4 * HEADS
OFF_AK, OFF_AV = OFF_AQ + QK, OFF_AQ + 2 * QK
OFF_GA = OFF_AQ + 3 * QK
OFF_GD = OFF_GA + D
NB = 512

BLOCKS = [("q", OFF_Q, 0), ("k", OFF_K, 0), ("v", OFF_V, 0), ("z", OFF_Z, 0),
          ("q", OFF_Q + NB, 1), ("k", OFF_K + NB, 1), ("v", OFF_V + NB, 1), ("z", OFF_Z + NB, 1),
          ("aq", OFF_AQ, 0), ("aq", OFF_AQ + NB, 1), ("ak", OFF_AK, 0), ("ak", OFF_AK + NB, 1),
          ("av", OFF_AV, 0), ("av", OFF_AV + NB, 1)]
BLOCKS += [("ga", OFF_GA + NB * i, i) for i in range(4)] + [("gd", OFF_GD + NB * i, i) for i in range(4)]
CONV = ("q", "k", "v")
TOKEN_MAJOR = ("z", "av")

LEVELS = 6
GDN = {"norm": (3, 2, 2), "decay": (4, 3, 2), "gram": (5, 0, 5), "first": (4, 1, 2)}
for _l in range(1, LEVELS):
    GDN[f"lt{_l}"] = (0, 1, 0)
    GDN[f"sub{_l}"] = (2, 0, 2) if _l < LEVELS - 1 else (1, 0, 0)
GDN |= {"uw": (1, 1, 2), "s0": (2, 0, 0), "v1": (2, 0, 0), "s1": (4, 0, 0), "v2": (2, 0, 0),
        "s2": (4, 0, 0), "v3": (2, 0, 0), "out": (6, 1, 2), "turn": (0, 1, 0)}
ATT = {"score": (10, 4, 0), "pT": (0, 1, 0), "pv": (1, 0, 0)}
ATT_END = {"norm": (4, 1, 1), "turn": (0, 1, 0)}
GDN_BATCHES = HEADS // 2

SET_ACT, XN_READY = 12, (5, 7)
HT_READY, AB_X, G_READY, GC_READY, COLS_READY = 11, 18, 20, 27, 28
SMALL_ALL = 16 * 10
H2_READY, ROUTE_ACT = (5, 7), 9
H2T_READY, GROUP_MAX, TOP_TWO, MASK_READY, ROUTE_FLAG = 9, 16, 32, 45, 50
FINAL_ROWS = 5


def conv_blocks(b):
    return sum(kind in CONV for kind, _, _ in BLOCKS[:b + 1])


def chunk_of(direction, step):
    return divmod(step if direction == 0 else T // CH - 1 - step, 2)


class StageCounts:

    def __init__(self, stages):
        self.before = {}
        at = [0, 0, 0, 0]
        for key, ops in stages:
            self.before[key] = tuple(at)
            at = [a + b for a, b in zip(at, (*ops, 1))]
        self.total = tuple(at)

    def value(self, engine, key, k=0):
        return self.before[key][("dve", "act", "pool", "pe").index(engine)] + k


GDN_STAGES = [((b, s), ops) for b in range(GDN_BATCHES) for s, ops in GDN.items()]
ATT_STAGES = [((a, s), ops) for a in range(HEADS) for s, ops in ATT.items()]
ATT_STAGES += [((HEADS, s), ops) for s, ops in ATT_END.items()]


def stage_order():
    gdn = [("gdn", *key) for key, _ in GDN_STAGES]
    att = [("att", *key) for key, _ in ATT_STAGES]
    order = []
    for b in range(len(BLOCKS)):
        for s in range(KC // 2):
            order.append(("pair", b, s))
            if b >= 3 and gdn and not (gdn[0][1] >= 2 and b < 8):
                order.append(gdn.pop(0))
            elif b >= 14 and not gdn and att:
                order.append(att.pop(0))
        order.append(("end", b, 0))
    return order + gdn + att


ORDER = stage_order()

SLOT = 4096
RING = 0
G_E, G_EG, G_AT, G_LT, G_UT, G_T, G_TT, G_Z, G_XK, G_S = (1024 * i for i in range(10))
G_KTM = G_S + 1536
G_VTM = G_KTM + 512
G_KTN = G_VTM + 512
A_OD = 8192
A_TMP = A_OD + 2048
HT = 6 * SLOT
MERGED = HT
QKV = HT + 4096
GATES = QKV
ZS = QKV + 6144
AQK = ZS + 2048
X2 = AQK
YA = AQK + 6144
YD = YA + 2048
CONST = YD + 2048
H2 = GATES
XE = HT
Y_SB = GATES + 4096
MOE = X2 + 4096
WORDS = 53200

C_IDENT, C_TRI, C_LEVEL = 0, 128, 128 + 512
C_DIST = C_LEVEL + 2 * LEVELS * 128
C_BEFORE = C_DIST + 512
C_ONES = C_BEFORE + 128
C_IOTA = C_ONES + 128
C_TWICE = C_IOTA + 64
N_CONST = C_TWICE + 64


def constants():
    import numpy as np
    c = np.zeros((P, N_CONST), np.float32)
    i = np.arange(P)
    r, n = i[:, None], i[None, :]
    same = (r // CH) == (n // CH)
    c[:, C_IDENT:C_IDENT + 128] = r == n
    for k, m in enumerate([r <= n, r >= n, r > n, r < n]):
        c[:, C_TRI + 128 * k:C_TRI + 128 * (k + 1)] = same & m
    for lv in range(LEVELS):
        m = 1 << lv
        block = (r // (2 * m)) == (n // (2 * m))
        low_r, low_n = (r // m) % 2 == 0, (n // m) % 2 == 0
        for d, mask in enumerate([low_r & ~low_n, ~low_r & low_n]):
            at = C_LEVEL + (lv * 2 + d) * 128
            c[:, at:at + 128] = block & mask
    for t in range(TT):
        c[:, C_DIST + 256 * t:C_DIST + 256 * (t + 1)] = np.abs(i[:, None] + 128 * t - np.arange(T)[None, :])
    c[:, C_BEFORE:C_BEFORE + 128] = r < n
    c[:, C_ONES:C_ONES + 128] = 1.0
    c[:, C_IOTA:C_IOTA + 64] = np.arange(64)[None, :]
    c[:, C_TWICE:C_TWICE + 64] = (i % 64)[:, None] == np.arange(64)[None, :]
    return c


def encoder(nc, x, g_mix, w_in, conv_w, a_log, dt_bias, gdn_norm_w, diff_lambda, diff_norm_w,
            w_branch_a, w_branch_d, w_out, g_ffn, w_group, b_group, w_router, b_router,
            w_exp_gate, w_exp_up, w_exp_down, g_final, const_tables, out):
    ctx = ExitStack()
    with ctx:
        def sem(name):
            return ctx.enter_context(nc.semaphore(name))

        arena = ctx.enter_context(nc.sbuf_tensor("arena", [P, WORDS], F32))
        banks = ctx.enter_context(nc.psum_tensor("banks", [P, 8, 512], F32))
        PROJ, MIX = 0, 4

        def at(off, *shape):
            n = math.prod(shape)
            v = arena[:, off:off + n]
            names = "abcde"[:len(shape)]
            if len(shape) > 1:
                v = v.rearrange(f"p ({' '.join(names)}) -> p {' '.join(names)}",
                                **dict(zip(names[:-1], shape[:-1])))
            return v

        def bank(i):
            return banks[:, i, :]

        def spread(ap, *shape):
            return ap.unsqueeze(len(shape)).broadcast_to([P, *shape])

        ident = at(CONST + C_IDENT, 128)
        tri = at(CONST + C_TRI, 4, 128)
        level = at(CONST + C_LEVEL, LEVELS, 2, 128)
        dist = at(CONST + C_DIST, TT, T)
        before = at(CONST + C_BEFORE, 128)
        ones = at(CONST + C_ONES, 128)
        iota = at(CONST + C_IOTA, 64)
        twice = at(CONST + C_TWICE, 64)
        small = [CONST + N_CONST]

        def take(*shape):
            v = at(small[0], *shape)
            small[0] += math.prod(shape)
            assert small[0] <= WORDS
            return v

        gmix_c, gffn_c = take(KC), take(KC)
        conv_rows, conv_c = take(P), take(5 * 24)
        dtb, alog = take(16), take(16)
        gdn_w, diff_w = take(DK), take(DK)
        lam_in = take(4, 64)
        w_ab = take(KC, 32)
        bias_r = take(NG + NE)
        eps_c, one_c, nlam = take(1), take(1), take(1)
        ss, rstd = take(2), take(2)
        ab_x, ab_t, ab_u = take(TT, 16), take(TT, 16), take(TT, 16)
        g_log, beta = take(TT, 16), take(TT, 16)
        gc, begc, esfx, bcol = (take(HEADS, 2, 2) for _ in range(4))
        lam_p, lam_s = take(2, 64), take(2)
        rn, rr = take(8), take(8)
        glast = take(2, 2, 2, 2)
        o_ss, o_r = take(4), take(4)
        mx, nmx, sums, rs, rl = take(4), take(4), take(4), take(4), take(2)
        od_ss, od_r = take(16), take(16)
        w_route = at(GATES + 4096, KC, NG + NE)

        x_sb = at(X2, TT, D)
        xn = at(RING, TT, KC, P)
        hT = at(HT, KC, T)
        qT, kT, vT = (at(QKV + 2048 * i, HEADS, T) for i in range(3))
        gates = [at(GATES, KC, T), at(GATES + 4096, KC, T)]
        zs = at(ZS, TT, QK)
        aq, ak = at(AQK, HEADS, T), at(AQK + 2048, HEADS, T)
        av = at(AQK + 4096, TT, QK)
        ya, yd = at(YA, HEADS, T), at(YD, HEADS, T)
        merged = at(MERGED, KC, T)

        g_sq = at(G_Z, 2, 2, T)
        g_E, g_EG, g_AT, g_LT, g_UT, g_T, g_TT, g_Z, g_XK = (
            at(o, 2, 2, 2, P) for o in (G_E, G_EG, G_AT, G_LT, G_UT, G_T, G_TT, G_Z, G_XK))
        g_XV, g_U, g_WT, g_KS = g_E, g_T, g_Z, g_UT
        g_S = at(G_S, 2, 2, 3, P)
        g_k, g_v = at(G_KTM, 2, 2, P), at(G_VTM, 2, 2, P)
        g_kT = at(G_KTN, 2, T)
        g_o, g_osq = at(G_E, 2, 2, P), at(G_E + 512, 2, 2, P)

        a_od = at(A_OD, TT, HEADS, P)
        a_s = at(A_TMP, TT, 2, T)
        a_p, a_pT = at(A_TMP + 1024, TT, T), at(A_TMP + 1536, 2, TT, P)
        a_sq = at(A_TMP, TT * HEADS, P)

        h2 = at(H2, TT, KC, P)
        h2T = at(HT, KC, T)
        xe = at(XE, KC, 2 * SLOTS)
        y_sb = at(Y_SB, 4, 512)
        moe_at = [MOE]

        def moe(*shape):
            v = at(moe_at[0], *shape)
            moe_at[0] += math.prod(shape)
            assert moe_at[0] <= CONST
            return v

        g_part, u_part = moe(FE), moe(FE)
        silu_g, hid = moe(4, SLOTS), moe(4, SLOTS)
        pick, pick_w = moe(TT, 2, SLOTS), moe(TT, 2, SLOTS)
        ws = moe(T)
        logits = moe(TT, NG + NE)
        rt = moe(8, TT, NE)
        rs1 = moe(16, TT)
        m_mask, m_weight, m_rank = moe(TT, NE), moe(TT, NE), moe(TT, NE)
        fin_ss = moe(TT)
        over_f, over_i = moe(1), moe(1).bitcast(I32)
        g_last = moe(D)

        x_in, table_in, small_in, wab_in = sem("x_in"), sem("table_in"), sem("small_in"), sem("wab_in")
        set_act, set_dve, set_pe = sem("set_act"), sem("set_dve"), sem("set_pe")
        unit_in = [sem(f"unit_in{i}") for i in range(3)]
        unit_used = sem("unit_used")
        conv_read = sem("conv_read")
        block_out = sem("block_out")
        gdn_sem = {e: sem(f"gdn_{e}") for e in ("dve", "act", "pool", "pe")}
        att_sem = {e: sem(f"att_{e}") for e in ("dve", "act", "pool", "pe")}
        merge_dve, merge_pool = sem("merge_dve"), sem("merge_pool")
        x_again, out_dve = sem("x_again"), sem("out_dve")
        route_in = sem("route_in")
        route_pe, route_dve, route_act = sem("route_pe"), sem("route_dve"), sem("route_act")
        full = [sem(f"expert_unit_in{i}") for i in range(6)]
        expert_unit_used = sem("expert_unit_used")
        pick_ready, ws_turned, ws_ready = sem("pick_ready"), sem("ws_turned"), sem("ws_ready")
        gathered, gather_read = sem("gathered"), sem("gather_read")
        gu_copied, gu_turned = sem("gu_copied"), sem("gu_turned")
        silu_done, hid_ready, y_copied = sem("silu_done"), sem("hid_ready"), sem("y_copied")
        scatter_done, added = sem("scatter_done"), sem("added")
        next_round = sem("next_round")
        final_in, fin_act, fin_dve, stored = sem("final_in"), sem("fin_act"), sem("fin_dve"), sem("stored")

        gdn_count = StageCounts(GDN_STAGES)
        att_count = StageCounts(ATT_STAGES)

        def wait_part(eng, sems, counts, me, key, offsets=()):
            off = dict(offsets)
            for e in ("dve", "act", "pool", "pe"):
                n = counts.value(e, key, off.get(e, 0))
                if n > 0:
                    eng.wait_ge(sems[e], n)

        class Line:

            def __init__(self, eng, s):
                self.eng, self.sem, self.n = eng, s, 0

            def __call__(self, ins):
                self.n += 1
                ins.then_inc(self.sem, 1)
                self.eng.wait_ge(self.sem, self.n)

        block = ctx.enter_context(nc.Block())

        wi = w_in[0].rearrange("(u p c) n -> u p c n", u=2, c=8)
        wa, wd = (w[0].rearrange("(c p) n -> p c n", p=P) for w in (w_branch_a, w_branch_d))
        wo = w_out[0].rearrange("(u c p) n -> u p c n", u=2, p=P)
        xt = x[0].rearrange("(t p) d -> p t d", p=P)
        UNITS_A = 2 * len(BLOCKS)
        UNITS = UNITS_A + 8 + 8

        def unit_source(n):
            if n < UNITS_A:
                col = BLOCKS[n // 2][1]
                return wi[n % 2, :, :, col:col + NB]
            n -= UNITS_A
            if n < 8:
                return (wa, wd)[n % 2][:, :, NB * (n // 2):NB * (n // 2 + 1)]
            n -= 8
            return wo[n % 2, :, :, NB * (n // 2):NB * (n // 2 + 1)]

        def unit(n):
            return at(RING + SLOT * (3 + n % 3), 8, NB)

        eg = w_exp_gate[0].rearrange("e (u p c) f -> e u p c f", u=2, c=8)
        eu = w_exp_up[0].rearrange("e (u p c) f -> e u p c f", u=2, c=8)
        ed = w_exp_down[0].rearrange("e (u k p) d -> e u p k d", u=2, p=P)

        def expert_unit(s, *shape):
            return at(RING + SLOT * s, *shape)

        def expert_source(e, s):
            return (eg, eu, ed)[s // 2][e, s % 2]

        def expert_target(s):
            return expert_unit(s, 8, FE) if s < 4 else expert_unit(s, 2, D)

        @block.sync
        def _(sp):
            sp.dma_start(x_sb[:, 0], xt[:, 0]).then_inc(x_in, 16)
            sp.dma_start(x_sb[:, 1], xt[:, 1]).then_inc(x_in, 16)
            sp.dma_start(at(CONST, N_CONST), const_tables).then_inc(table_in, 16)
            for n in range(UNITS):
                if n >= 3:
                    sp.wait_ge(unit_used, n - 2)
                sp.dma_start(unit(n), unit_source(n)).then_inc(unit_in[n % 3], 16)
                if n == UNITS_A + 2:
                    sp.wait_ge(att_sem["pe"], att_count.total[3])
                    sp.dma_start(x_sb, xt).then_inc(x_again, 16)
                if n == UNITS_A + 8:
                    for e in ("dve", "act", "pool", "pe"):
                        sp.wait_ge(gdn_sem[e], gdn_count.total[("dve", "act", "pool", "pe").index(e)])
                        sp.wait_ge(att_sem[e], att_count.total[("dve", "act", "pool", "pe").index(e)])
                    for s in range(3):
                        sp.dma_start(expert_target(s), expert_source(0, s)).then_inc(full[s], 16)
            sp.wait_ge(merge_pool, 4)
            for w, a, b in ((w_group, 0, NG), (w_router, NG, NG + NE)):
                for u in range(2):
                    sp.dma_start(w_route[:, 8 * u:8 * u + 8, a:b], w[0].rearrange("(u p c) n -> u p c n", u=2, c=8)[u]).then_inc(route_in, 16)
            sp.dma_start(g_last, g_final.partition_broadcast(P)).then_inc(final_in, 16)
            for s in range(3, 6):
                sp.wait_ge(unit_used, UNITS - 5 + s)
                sp.dma_start(expert_target(s), expert_source(0, s)).then_inc(full[s], 16)

            def load_expert(n, e):
                for s in range(6):
                    sp.wait_ge(expert_unit_used, 6 * n + (s - 5))
                    sp.dma_start(expert_target(s), expert_source(e, s)).then_inc(full[s], 16)

            with sp.Fori(1, NE) as e:
                load_expert(e, e)
            sp.wait_ge(route_dve, ROUTE_FLAG)
            sp_over = sp.value_load(over_i[0:1, 0:1], min_val=0, max_val=1)
            with sp.If(sp_over > 0):
                with sp.Fori(1, ROUNDS) as r:
                    with sp.Fori(0, NE) as e:
                        load_expert(r * NE + e, e)
            for t in range(TT):
                sp.wait_ge(fin_dve, FINAL_ROWS - 1 + t)
                sp.dma_start(out[0].rearrange("(t p) d -> p t d", p=P)[:, t], x_sb[:, t]).then_inc(stored, 16)
            sp.wait_ge(stored, 32)

        @block.tensor
        def _(pe):
            mm = nc.tensor.matmul
            turn = nc.tensor.transpose

            pe.wait_ge(table_in, 16)
            for t in range(TT):
                pe.wait_ge(set_act, XN_READY[t])
                for c in range(KC):
                    last = turn(bank(c // 2)[:, (c % 2) * T + t * P:(c % 2) * T + t * P + P], xn[:, t, c, :], ident)
            last.then_inc(set_pe, 1)
            pe.wait_ge(small_in, SMALL_ALL)
            pe.wait_ge(set_dve, HT_READY)
            turn(bank(4)[:, 0:120], conv_rows[0:120, :], ident[0:120, 0:120]).then_inc(set_pe, 1)
            pe.wait_ge(wab_in, 32)
            for t in range(TT):
                for c in range(KC):
                    last = mm(bank(5)[:, 32 * t:32 * t + 32], hT[:, c, t * P:(t + 1) * P], w_ab[:, c, :],
                              start=(c == 0), stop=(c == KC - 1))
            last.then_inc(set_pe, 1)

            def decay_sums():
                pe.wait_ge(set_dve, G_READY)
                for k in range(4):
                    for t in range(TT):
                        last = mm(bank(6)[:, (k * 2 + t) * 8:(k * 2 + t) * 8 + 8], tri[:, k, :],
                                  g_log[:, t, (k % 2) * 8:(k % 2) * 8 + 8], start=True, stop=True)
                last.then_inc(set_pe, 1)

            def wait_unit(n):
                pe.wait_ge(unit_in[n % 3], 16 * (n // 3 + 1))

            def pair(b, s):
                kind = BLOCKS[b][0]
                b0 = PROJ + 2 * (b % 2)
                if s == 0 and b >= 2:
                    if BLOCKS[b - 2][0] in CONV:
                        pe.wait_ge(conv_read, 20 * conv_blocks(b - 2))
                    else:
                        pe.wait_ge(block_out, b - 1)
                for c in (2 * s, 2 * s + 1):
                    if c % 8 == 0:
                        wait_unit(2 * b + c // 8)
                    w = unit(2 * b + c // 8)[:, c % 8, :]
                    if kind in TOKEN_MAJOR:
                        for t in range(TT):
                            last = mm(bank(b0 + t), hT[:, c, t * P:(t + 1) * P], w, start=(c == 0), stop=(c == KC - 1))
                    else:
                        for j in range(4):
                            last = mm(bank(b0 + j // 2)[:, (j % 2) * T:(j % 2 + 1) * T], w[:, j * P:(j + 1) * P],
                                      hT[:, c, :], start=(c == 0 and j % 2 == 0), stop=(c == KC - 1),
                                      skip_group_check=True)
                    if c % 8 == 7:
                        last.then_inc(unit_used, 1)

            HDT = [(h, d, t) for h in range(2) for d in range(2) for t in range(2)]

            def mix(i, j=0, n=P):
                return bank(MIX + i)[:, P * j:P * j + n]

            def gdn_stage(b, s):
                wait_part(pe, gdn_sem, gdn_count, "pe", (b, s), {"pool": 2} if s == "norm" else {})
                heads = (2 * b, 2 * b + 1)
                single = dict(start=True, stop=True)
                if s == "norm":
                    pe.wait_ge(block_out, 3 if b < 2 else 7)
                    for k, src in enumerate((kT, vT)):
                        for h in range(2):
                            for t in range(2):
                                turn(mix(k, 2 * h + t), src[:, heads[h], t * P:(t + 1) * P], ident)
                    for qk in range(2):
                        for h in range(2):
                            for t in range(2):
                                n = qk * 4 + h * 2 + t
                                last = mm(mix(2)[:, n:n + 1], g_sq[:, qk, h, t * P:(t + 1) * P], ones[:, 0:1], **single)
                elif s == "decay":
                    if b == 0:
                        pe.wait_ge(set_dve, COLS_READY)
                    for h in range(2):
                        for t in range(2):
                            turn(mix(0, 2 * h + t), g_k[:, h, t, :], ident)
                    for h, d, t in HDT:
                        col = g_log[:, t, d * 8 + heads[h]:d * 8 + heads[h] + 1]
                        last = mm(mix(2 + h, 2 * d + t), col.broadcast_to([P, P]), tri[:, d, :], **single)
                elif s == "gram":
                    for h in range(2):
                        for t in range(2):
                            kk = g_kT[:, h, t * P:(t + 1) * P]
                            mm(mix(0, 2 * h + t), kk, kk, **single)
                            mm(mix(1, 2 * h + t), kk, qT[:, heads[h], t * P:(t + 1) * P], **single)
                    for h, d, t in HDT:
                        last = mm(mix(2 + h, 2 * d + t), bcol[:, heads[h], d, t:t + 1].broadcast_to([P, P]), ident, **single)
                elif s == "first":
                    for h, d, t in HDT:
                        last = turn(mix(2 + h, 2 * d + t), g_TT[:, h, d, t, :], ident)
                elif s[:2] == "lt":
                    for h, d, t in HDT:
                        last = mm(mix(h, 2 * d + t), g_UT[:, h, d, t, :], g_T[:, h, d, t, :], **single)
                elif s[:3] == "sub":
                    for h, d, t in HDT:
                        if s != f"sub{LEVELS - 1}":
                            mm(mix(h, 2 * d + t), g_TT[:, h, d, t, :], g_Z[:, h, d, t, :], **single)
                        last = mm(mix(2 + h, 2 * d + t), g_Z[:, h, d, t, :], g_TT[:, h, d, t, :], **single)
                elif s == "uw":
                    for h, d, t in HDT:
                        mm(mix(h, 2 * d + t), g_TT[:, h, d, t, :], g_XV[:, h, d, t, :], **single)
                        last = mm(mix(2 + h, 2 * d + t), g_XK[:, h, d, t, :], g_TT[:, h, d, t, :], **single)
                elif s[0] == "s":
                    for d in range(2):
                        tile, r = chunk_of(d, int(s[1]))
                        for h in range(2):
                            last = mm(mix(2 * d, h), g_KS[64 * r:64 * r + 64, h, d, tile, :],
                                      g_U[64 * r:64 * r + 64, h, d, tile, :], **single)
                elif s[0] == "v":
                    step = int(s[1])
                    for d in range(2):
                        tile, r = chunk_of(d, step)
                        for h in range(2):
                            last = mm(mix(1, h)[64 * r:64 * r + 64, :], g_WT[:, h, d, tile, 64 * r:64 * r + 64],
                                      g_S[:, h, d, step - 1, :], **single)
                elif s == "out":
                    for t in range(2):
                        for h in range(2):
                            o = mix(2 * t, h)
                            mm(o, g_AT[:, h, 0, t, :], g_U[:, h, 0, t, :], start=True, stop=False, skip_group_check=True)
                            mm(o, g_AT[:, h, 1, t, :], g_U[:, h, 1, t, :], start=False, stop=False, skip_group_check=True)
                            for d in range(2):
                                for r in range(2):
                                    step = 2 * t + r if d == 0 else 3 - 2 * t - r
                                    if step:
                                        last = mm(o[64 * r:64 * r + 64, :], g_EG[:, h, d, t, 64 * r:64 * r + 64],
                                                  g_S[:, h, d, step - 1, :], start=False, stop=True, skip_group_check=True)
                elif s == "turn":
                    for t in range(2):
                        for h in range(2):
                            last = turn(mix(0, 2 * h + t), g_o[:, t, h, :], ident)
                last.then_inc(gdn_sem["pe"], 1)

            def att_stage(a, s):
                if (a, s) == (0, "score"):
                    for e in ("dve", "act", "pool"):
                        pe.wait_ge(gdn_sem[e], gdn_count.total[("dve", "act", "pool").index(e)])
                    pe.wait_ge(block_out, 14)
                wait_part(pe, att_sem, att_count, "pe", (a, s))
                if s == "score":
                    for t in range(TT):
                        for m in range(2):
                            rows = slice(DH * m, DH * m + DH)
                            last = mm(bank(MIX + 2 * t + m)[:, 0:T], aq[rows, a, t * P:(t + 1) * P], ak[rows, a, :],
                                      start=True, stop=True)
                elif s == "pT":
                    for k in range(2):
                        for t in range(TT):
                            last = turn(mix(0, 2 * k + t), a_p[:, t, k * P:(k + 1) * P], ident)
                elif s == "pv":
                    for t in range(TT):
                        for k in range(2):
                            last = mm(mix(1, t), a_pT[:, k, t, :], av[:, k, a * P:(a + 1) * P], start=(k == 0), stop=(k == 1))
                elif s == "norm":
                    last = turn(mix(0), ident, ident)
                elif s == "turn":
                    for h in range(HEADS):
                        for t in range(TT):
                            last = turn(bank(MIX + h // 2)[:, (h % 2) * T + t * P:(h % 2) * T + t * P + P],
                                        a_od[:, t, h, :], ident)
                last.then_inc(att_sem["pe"], 1)

            for what, i, s in ORDER:
                if what == "pair":
                    pair(i, s)
                    if (i, s) == (0, KC // 2 - 1):
                        decay_sums()
                elif what == "gdn":
                    gdn_stage(i, s)
                elif what == "att":
                    att_stage(i, s)

            pe.wait_ge(att_sem["act"], att_count.total[1])
            for k in range(4):
                b0 = 4 * (k % 2)
                if k == 0:
                    pe.wait_ge(block_out, len(BLOCKS))
                if k >= 2:
                    pe.wait_ge(merge_dve, 4 * (k - 1))
                for br, y in enumerate((ya, yd)):
                    n = UNITS_A + 2 * k + br
                    wait_unit(n)
                    for c in range(HEADS):
                        for j in range(4):
                            last = mm(bank(b0 + 2 * br + j // 2)[:, (j % 2) * T:(j % 2 + 1) * T],
                                      unit(n)[:, c, j * P:(j + 1) * P], y[:, c, :],
                                      start=(c == 0 and j % 2 == 0), stop=(c == HEADS - 1), skip_group_check=True)
                    last.then_inc(unit_used, 1)
            pe.wait_ge(merge_pool, 4)
            pe.wait_ge(merge_dve, 16)
            for k in range(4):
                if k >= 2:
                    pe.wait_ge(out_dve, 2 * (k - 1))
                for c in range(KC):
                    n = UNITS_A + 8 + 2 * k + c // 8
                    if c % 8 == 0:
                        wait_unit(n)
                    for t in range(TT):
                        last = mm(bank(2 * (k % 2) + t), merged[:, c, t * P:(t + 1) * P], unit(n)[:, c % 8, :],
                                  start=(c == 0), stop=(c == KC - 1))
                    if c % 8 == 7:
                        last.then_inc(unit_used, 1)
            pe.wait_ge(out_dve, 8)
            for t in range(TT):
                pe.wait_ge(route_act, H2_READY[t])
                for c in range(KC):
                    last = turn(bank(c // 2)[:, (c % 2) * T + t * P:(c % 2) * T + t * P + P], h2[:, t, c, :], ident)
            last.then_inc(route_pe, 1)
            pe.wait_ge(route_in, 64)
            pe.wait_ge(route_dve, H2T_READY)
            for t in range(TT):
                for c in range(KC):
                    last = mm(bank(0)[:, 36 * t:36 * t + 36], h2T[:, c, t * P:(t + 1) * P], w_route[:, c, :],
                              start=(c == 0), stop=(c == KC - 1))
            last.then_inc(route_pe, 1)
            pe.wait_ge(route_dve, MASK_READY)
            mm(bank(1)[:, 0:NE], before, m_mask[:, 0, :], start=True, stop=True)
            mm(bank(1)[:, NE:2 * NE], before, m_mask[:, 1, :], start=True, stop=False)
            mm(bank(1)[:, NE:2 * NE], ones, m_mask[:, 0, :], start=False, stop=True)
            mm(bank(1)[:, 2 * NE:3 * NE], ones, m_mask[:, 0, :], start=True, stop=False)
            mm(bank(1)[:, 2 * NE:3 * NE], ones, m_mask[:, 1, :], start=False, stop=True).then_inc(route_pe, 1)

            def experts_pair(n):
                pe.wait_ge(pick_ready, 4 * n + 4)
                pe.wait_ge(hid_ready, 2 * n + 1)
                for t in range(TT):
                    last = turn(bank(4)[:, t * P:(t + 1) * P], pick_w[:, t].rearrange("p a b -> p (a b)"), ident)
                last.then_inc(ws_turned, 1)
                pe.wait_ge(added, 8 * n + 2)
                for k in range(4):
                    pe.wait_ge(gather_read, 4 * n + k + 1)
                    for c in range(4 * k, 4 * k + 4):
                        for t in range(TT):
                            last = mm(bank(k % 2)[:, (c % 4) * P:(c % 4 + 1) * P], h2[:, t, c, :],
                                      pick[:, t].rearrange("p a b -> p (a b)"), start=(t == 0), stop=(t == TT - 1))
                    last.then_inc(gathered, 1)
                pe.wait_ge(gather_read, 4 * n + 6)
                for e in range(2):
                    X = 2 * n + e
                    pe.wait_ge(gu_copied, 2 * X + 1)
                    for m in range(2):
                        for u in range(2):
                            pe.wait_ge(full[2 * m + u], 16 * X + 16)
                            for c in range(8):
                                g = c % 2
                                last = mm(bank(2 + m)[64 * g:64 * g + 64, :],
                                          xe[:, 8 * u + c, SLOTS * e:SLOTS * e + SLOTS],
                                          expert_unit(2 * m + u, 8, FE)[:, c, :],
                                          start=(u == 0 and c < 2), stop=(u == 1 and c >= 6))
                            last.then_inc(expert_unit_used, 1)
                    pe.wait_ge(ws_ready, n + 1)
                    pe.wait_ge(hid_ready, X + 1)
                    for m, part in enumerate((g_part, u_part)):
                        pe.wait_ge(gu_copied, 2 * X + 2 + m)
                        for f in range(4):
                            last = mm(bank(4)[:, (4 * m + f) * SLOTS:(4 * m + f + 1) * SLOTS],
                                      part[:, f * P:(f + 1) * P], twice, start=True, stop=True)
                    last.then_inc(gu_turned, 1)
                    pe.wait_ge(hid_ready, X + 2)
                    pe.wait_ge(y_copied, 4 * X + 1)
                    for u in range(2):
                        pe.wait_ge(full[4 + u], 16 * X + 16)
                        for f in range(2):
                            for j in range(4):
                                g = j % 2
                                last = mm(bank(5 + j // 2)[64 * g:64 * g + 64, :], hid[:, 2 * u + f, :],
                                          expert_unit(4 + u, 2, D)[:, f, 512 * j:512 * j + 512],
                                          start=(u == 0 and f == 0), stop=(u == 1 and f == 1))
                        last.then_inc(expert_unit_used, 1)
                pe.wait_ge(y_copied, 8 * n + 9)
                for q in range(8):
                    t, j = divmod(q, 4)
                    pe.wait_ge(added, 8 * n + q + 1)
                    mm(bank(0 if q % 2 else 7), ws[:, t * P:(t + 1) * P], y_sb[:, j, :],
                       start=True, stop=True).then_inc(scatter_done, 1)

            pe.sem_inc(gathered, 1)
            pe.sem_inc(scatter_done, 1)
            with pe.Fori(0, NE // 2) as n:
                experts_pair(n)
            pe.wait_ge(route_dve, ROUTE_FLAG)
            with pe.If(pe.value_load(over_i[0:1, 0:1], min_val=0, max_val=1) > 0):
                with pe.Fori(NE // 2, ROUNDS * NE // 2) as n:
                    experts_pair(n)

        @block.scalar
        def _(act):
            act_ = nc.scalar.activation
            line = Line(act, set_act)
            for dst, src in ((gmix_c.rearrange("p (u c) -> p u c", u=2), g_mix[0].rearrange("(u p c) -> p u c", u=2, c=8)),
                             (gffn_c.rearrange("p (u c) -> p u c", u=2), g_ffn[0].rearrange("(u p c) -> p u c", u=2, c=8)),
                             (conv_rows[0:120, :], conv_w[0].rearrange("k (t p) -> (k t) p", p=P)),
                             (dtb, dt_bias[0].rearrange("a b -> (a b)").partition_broadcast(P)),
                             (alog, a_log[0].rearrange("a b -> (a b)").partition_broadcast(P)),
                             (gdn_w, gdn_norm_w[0].partition_broadcast(P)),
                             (diff_w, diff_norm_w[0].partition_broadcast(P)),
                             (lam_in.rearrange("p a b -> p (a b)"), diff_lambda[0].rearrange("a b -> (a b)").partition_broadcast(P)),
                             (bias_r[:, 0:NG], b_group[0].partition_broadcast(P)),
                             (bias_r[:, NG:NG + NE], b_router[0].partition_broadcast(P))):
                act.dma_start(dst, src).then_inc(small_in, 16)
            for u in range(2):
                act.dma_start(w_ab[:, 8 * u:8 * u + 8, :], wi[u, :, :, OFF_AB:OFF_AB + 32]).then_inc(wab_in, 16)
            act.wait_ge(x_in, 32)
            for t in range(TT):
                line(act_(xn[:, t].rearrange("p c q -> p (c q)"), x_sb[:, t, :], ACT.Square, accum_out=ss[:, t:t + 1]))
            act.wait_ge(set_dve, 2)
            line(act_(rstd, ss, ACT.Sqrt, bias=eps_c[:, 0:1], scale=1.0 / D))
            act.wait_ge(set_dve, 3)
            for t in range(TT):
                for u in range(2):
                    line(act_(xn[:, t, 8 * u:8 * u + 8, :], x_sb[:, t, 1024 * u:1024 * u + 1024].rearrange("p (q c) -> p c q", c=8),
                              ACT.Copy, scale=rstd[:, t:t + 1]))
            act.wait_ge(set_dve, AB_X)
            line(act_(ab_u, ab_u, ACT.Exp, scale=-1.0))
            line(act_(alog, alog, ACT.Exp))
            line(act_(lam_s, lam_s, ACT.Exp))
            line(act_(ab_u, ab_u, ACT.Ln, bias=one_c[:, 0:1]))
            act.wait_ge(set_pe, 3)
            line(act_(beta, bank(5)[:, 0:64].rearrange("p (t n) -> p t n", t=2)[:, :, 16:32], ACT.Sigmoid))
            assert line.n == SET_ACT

            def decay_exp():
                act.wait_ge(set_dve, GC_READY)
                line(act_(esfx, esfx, ACT.Exp))
                line(act_(begc, gc, ACT.Exp))

            gdn_line = Line(act, gdn_sem["act"])
            att_line = Line(act, att_sem["act"])
            banks_m = banks[:, MIX:MIX + 4, :]
            m01 = banks[:, MIX:MIX + 2, :]
            m23 = banks[:, MIX + 2:MIX + 4, :]

            def flat(ap):
                return ap.rearrange("p a b c d -> p (a b c d)").rearrange("p (x n) -> p x n", n=512)

            def block_end(b):
                kind, _, i = BLOCKS[b]
                src = banks[:, PROJ + 2 * (b % 2):PROJ + 2 * (b % 2) + 2, :]
                if kind in CONV:
                    act.wait_ge(conv_read, 20 * conv_blocks(b))
                    y = {"q": qT, "k": kT, "v": vT}[kind][:, 4 * i:4 * i + 4, :]
                    ins = act_(y, y, ACT.Silu)
                else:
                    act.wait_ge(unit_used, 2 * b + 2)
                    if kind == "ga" and i == 0:
                        act.wait_ge(gdn_sem["pe"], gdn_count.value("pe", (GDN_BATCHES - 1, "first")))
                        act.wait_ge(gdn_sem["pool"], gdn_count.value("pool", (GDN_BATCHES - 1, "first")))
                    if kind == "gd" and i == 2:
                        act.wait_ge(gdn_sem["pool"], gdn_count.total[2])
                    if kind == "z":
                        ins = act_(zs[:, :, NB * i:NB * i + NB], src, ACT.Silu)
                    elif kind == "av":
                        ins = act_(av[:, :, NB * i:NB * i + NB], src, ACT.Copy)
                    elif kind in ("aq", "ak"):
                        y = (aq if kind == "aq" else ak)[:, 4 * i:4 * i + 4, :].rearrange("p a n -> p (a n)")
                        ins = act_(y.rearrange("p (x n) -> p x n", n=512), src, ACT.Copy)
                    else:
                        y = gates[kind == "gd"][:, 4 * i:4 * i + 4, :].rearrange("p a n -> p (a n)")
                        ins = act_(y.rearrange("p (x n) -> p x n", n=512), src, ACT.Sigmoid)
                ins.then_inc(block_out, 1)

            def gdn_stage(b, s):
                act.wait_ge(gdn_sem["pe"], gdn_count.value("pe", (b, s), 1))
                if s == "norm":
                    gdn_line(act_(rn, bank(MIX + 2)[:, 0:8], ACT.Sqrt, bias=eps_c[:, 0:1]))
                    gdn_line(act_(g_v.rearrange("p a b c -> p (a b c)"), bank(MIX + 1), ACT.Copy))
                elif s == "decay":
                    gdn_line(act_(g_kT.rearrange("p a b -> p (a b)"), bank(MIX), ACT.Copy))
                    act.wait_ge(gdn_sem["dve"], gdn_count.value("dve", (b, s), 1))
                    gdn_line(act_(flat(g_EG), m23, ACT.Exp))
                    act.wait_ge(gdn_sem["dve"], gdn_count.value("dve", (b, s), 2))
                    gdn_line(act_(flat(g_E), flat(g_E), ACT.Exp))
                elif s == "first":
                    gdn_line(act_(flat(g_T), m23, ACT.Copy))
                elif s[:2] == "lt":
                    gdn_line(act_(flat(g_Z), m01, ACT.Copy))
                elif s == "uw":
                    gdn_line(act_(flat(g_WT), m23, ACT.Copy))
                elif s == "out":
                    act.wait_ge(gdn_sem["dve"], gdn_count.value("dve", (b, s), 4))
                    gdn_line(act_(o_r, o_ss, ACT.Sqrt, bias=eps_c[:, 0:1], scale=1.0 / DK))
                elif s == "turn":
                    gdn_line(act_(ya[:, 2 * b:2 * b + 2, :].rearrange("p a b -> p (a b)"), bank(MIX), ACT.Copy))

            def att_stage(a, s):
                act.wait_ge(att_sem["pe"], att_count.value("pe", (a, s), 1))
                if s == "score":
                    act.wait_ge(att_sem["dve"], att_count.value("dve", (a, s), 4))
                    for t in range(TT):
                        for m in range(2):
                            i = 2 * t + m
                            att_line(act_(a_s[:, t, m, :], a_s[:, t, m, :], ACT.Exp, bias=nmx[:, i:i + 1],
                                          scale=DH ** -0.5, accum_out=sums[:, i:i + 1]))
                elif s == "pT":
                    att_line(act_(a_pT.rearrange("p a b c -> p (a b c)"), bank(MIX), ACT.Copy))
                elif s == "norm":
                    act.wait_ge(att_sem["dve"], att_count.value("dve", (a, s), 2))
                    att_line(act_(od_r, od_ss, ACT.Sqrt, bias=eps_c[:, 0:1], scale=1.0 / P))
                elif s == "turn":
                    att_line(act_(yd.rearrange("p a b -> p (a b)").rearrange("p (x n) -> p x n", n=512), banks_m, ACT.Copy))

            for what, i, s in ORDER:
                if what == "end":
                    block_end(i)
                    if i == 0:
                        decay_exp()
                elif what == "gdn":
                    gdn_stage(i, s)
                elif what == "att":
                    att_stage(i, s)

            rline = Line(act, route_act)
            act.wait_ge(out_dve, 8)
            for t in range(TT):
                rline(act_(h2[:, t].rearrange("p c q -> p (c q)"), x_sb[:, t, :], ACT.Square, accum_out=ss[:, t:t + 1]))
            rline(act_(rstd, ss, ACT.Sqrt, bias=eps_c[:, 0:1], scale=1.0 / D))
            act.wait_ge(route_dve, 1)
            for t in range(TT):
                for u in range(2):
                    rline(act_(h2[:, t, 8 * u:8 * u + 8, :], x_sb[:, t, 1024 * u:1024 * u + 1024].rearrange("p (q c) -> p c q", c=8),
                               ACT.Copy, scale=rstd[:, t:t + 1]))
            act.wait_ge(route_dve, GROUP_MAX)
            rline(act_(rt[:, 0, :, 0:NG], rt[:, 0, :, 0:NG], ACT.Exp))
            act.wait_ge(route_dve, TOP_TWO)
            rline(act_(rs1[:, 7, :], rs1[:, 7, :], ACT.Exp))
            assert rline.n == ROUTE_ACT

            def experts_pair(n):
                act.wait_ge(ws_turned, n + 1)
                act.wait_ge(scatter_done, 8 * n + 1)
                act_(ws, bank(4)[:, 0:T], ACT.Copy).then_inc(ws_ready, 1)
                for e in range(2):
                    X = 2 * n + e
                    for m, part in enumerate((g_part, u_part)):
                        act.wait_ge(expert_unit_used, 6 * X + 2 + 2 * m)
                        act_(part, bank(2 + m), ACT.Copy).then_inc(gu_copied, 1)
                    act.wait_ge(gu_turned, X + 1)
                    act_(silu_g.rearrange("p a b -> p (a b)"), bank(4)[:, 0:T], ACT.Silu).then_inc(silu_done, 1)
                    act.wait_ge(expert_unit_used, 6 * X + 6)
                    for j in range(4):
                        g = j % 2
                        act_(y_sb[64 * e:64 * e + 64, j, :], bank(5 + j // 2)[64 * g:64 * g + 64, :],
                             ACT.Copy).then_inc(y_copied, 1)

            act.sem_inc(gu_copied, 1)
            act.sem_inc(y_copied, 1)
            with act.Fori(0, NE // 2) as n:
                experts_pair(n)
            act.wait_ge(route_dve, ROUTE_FLAG)
            with act.If(act.value_load(over_i[0:1, 0:1], min_val=0, max_val=1) > 0):
                with act.Fori(NE // 2, ROUNDS * NE // 2) as n:
                    experts_pair(n)
            act.wait_ge(fin_dve, 2)
            act_(fin_ss, fin_ss, ACT.Sqrt, bias=eps_c[:, 0:1], scale=1.0 / D).then_inc(fin_act, 1)

        @block.gpsimd
        def _(pool):
            tt_ = nc.gpsimd.tensor_tensor
            gdn_line = Line(pool, gdn_sem["pool"])
            att_line = Line(pool, att_sem["pool"])

            def gdn_stage(b, s):
                heads = slice(2 * b, 2 * b + 2)
                if s == "norm":
                    pool.wait_ge(block_out, 3 if b < 2 else 7)
                    for e in ("dve", "act", "pe"):
                        if gdn_count.value(e, (b, s)):
                            pool.wait_ge(gdn_sem[e], gdn_count.value(e, (b, s)))
                    for i, m in enumerate((qT, kT)):
                        gdn_line(tt_(g_sq[:, i], m[:, heads, :], m[:, heads, :], ALU.mult))
                    return
                if not GDN[s][2]:
                    return
                pool.wait_ge(gdn_sem["pe"], gdn_count.value("pe", (b, s), 1))
                if s == "decay":
                    pool.wait_ge(gdn_sem["act"], gdn_count.value("act", (b, s), 3))
                    for h in range(2):
                        gdn_line(tt_(g_E[:, h], g_E[:, h], tri[:, 0:2].unsqueeze(2).broadcast_to([P, 2, 2, P]), ALU.mult))
                elif s == "gram":
                    for h in range(2):
                        qh = qT[:, 2 * b + h, :].rearrange("p (t n) -> p t n", t=2)
                        gdn_line(tt_(g_EG[:, h], g_EG[:, h], qh.unsqueeze(1).broadcast_to([P, 2, 2, P]), ALU.mult))
                    pool.wait_ge(gdn_sem["dve"], gdn_count.value("dve", (b, s), 5))
                    mask_level(b, 0)
                    flat8 = g_UT.rearrange("p a b c d -> p (a b c) d")
                    gdn_line(tt_(g_TT.rearrange("p a b c d -> p (a b c) d"),
                                 ident.unsqueeze(1).broadcast_to([P, 8, P]), flat8, ALU.subtract))
                elif s == "first":
                    mask_level(b, 1)
                elif s[:3] == "sub":
                    mask_level(b, int(s[3:]) + 1)
                elif s == "uw":
                    for h in range(2):
                        es = esfx[:, 2 * b + h].unsqueeze(3).broadcast_to([P, 2, 2, P])
                        gdn_line(tt_(g_KS[:, h], g_k[:, h].unsqueeze(1).broadcast_to([P, 2, 2, P]), es, ALU.mult))
                elif s == "out":
                    pool.wait_ge(gdn_sem["dve"], gdn_count.value("dve", (b, s), 6))
                    o4 = g_o.rearrange("p t h n -> p (t h) n")
                    gdn_line(tt_(o4, o4, gdn_w.unsqueeze(1).broadcast_to([P, 4, P]), ALU.mult))
                    pool.wait_ge(block_out, 4 if b < 2 else 8)
                    o2 = g_o.rearrange("p t h n -> p t (h n)")
                    gdn_line(tt_(o2, o2, zs[:, :, 2 * b * P:(2 * b + 2) * P], ALU.mult))

            def mask_level(b, lv):
                for h in range(2):
                    m = level[:, lv].unsqueeze(2).broadcast_to([P, 2, 2, P])
                    gdn_line(tt_(g_UT[:, h], g_LT[:, h], m, ALU.mult))

            def att_stage(a, s):
                if a == HEADS and s == "norm":
                    pool.wait_ge(att_sem["dve"], att_count.value("dve", (a, s), 4))
                    o = a_od.rearrange("p t h n -> p (t h) n")
                    att_line(tt_(o, o, diff_w.unsqueeze(1).broadcast_to([P, TT * HEADS, P]), ALU.mult))

            pool.wait_ge(set_dve, COLS_READY)
            for what, i, s in ORDER:
                if what == "gdn":
                    gdn_stage(i, s)
                elif what == "att":
                    att_stage(i, s)
            for k in range(4):
                pool.wait_ge(merge_dve, 4 * k + 4)
                j = slice(4 * k, 4 * k + 4)
                if k == 0:
                    pool.wait_ge(unit_used, UNITS_A)
                tt_(merged[:, j, :], gates[0][:, j, :], gates[1][:, j, :], ALU.add).then_inc(merge_pool, 1)

        @block.vector
        def _(dve):
            V = nc.vector
            tt_, ts_, stt_ = V.tensor_tensor, V.tensor_scalar, V.scalar_tensor_tensor
            line = Line(dve, set_dve)
            line(V.memset(one_c, 1.0))
            line(V.memset(eps_c, EPS))
            dve.wait_ge(set_act, 3)
            line(V.reciprocal(rstd, rstd))
            dve.wait_ge(set_pe, 1)
            dve.wait_ge(small_in, SMALL_ALL)
            for k in range(8):
                line(tt_(hT[:, 2 * k:2 * k + 2, :], bank(k).rearrange("p (c n) -> p c n", c=2),
                         spread(gmix_c[:, 2 * k:2 * k + 2], 2, T), ALU.mult))
            assert line.n == HT_READY
            dve.wait_ge(set_pe, 2)
            line(V.tensor_copy(conv_c, bank(4)[:, 0:120]))
            line(tt_(lam_p, lam_in[:, 0:4:2, :], lam_in[:, 1:4:2, :], ALU.mult))
            line(V.tensor_reduce(lam_s, lam_p, AX.X, ALU.add))
            line(ts_(diff_w, diff_w, 1.0 - LAM_INIT, None, ALU.mult))
            dve.wait_ge(set_pe, 3)
            ab_ps = bank(5)[:, 0:64].rearrange("p (t n) -> p t n", t=2)
            line(tt_(ab_x, ab_ps[:, :, 0:16], dtb.unsqueeze(1).broadcast_to([P, TT, 16]), ALU.add))
            line(stt_(ab_u, ab_x, -1.0, ab_x, ALU.mult, ALU.max))
            line(ts_(ab_x, ab_x, 0.0, None, ALU.max))
            assert line.n == AB_X
            dve.wait_ge(set_act, SET_ACT - 1)
            line(tt_(ab_x, ab_x, ab_u, ALU.add))
            line(stt_(g_log, ab_x, -1.0, alog.unsqueeze(1).broadcast_to([P, TT, 16]), ALU.mult, ALU.mult))
            assert line.n == G_READY
            line(tt_(nlam, lam_s[:, 1:2], lam_s[:, 0:1], ALU.subtract))
            line(ts_(nlam, nlam, LAM_INIT, None, ALU.subtract))
            dve.wait_ge(set_act, SET_ACT)

            def by_head(v):
                return v.rearrange("p h d t -> p t d h")

            line(V.tensor_copy(by_head(bcol), beta.rearrange("p t (d h) -> p t d h", d=2)))

            def decay_columns():
                dve.wait_ge(set_pe, 4)
                for v, k in ((gc, 0), (esfx, 2)):
                    for d in range(2):
                        src = bank(6)[:, (k + d) * 16:(k + d) * 16 + 16].rearrange("p (t h) -> p t h", t=2)
                        line(V.tensor_copy(v[:, :, d, :].rearrange("p h t -> p t h"), src))
                assert line.n == GC_READY
                dve.wait_ge(set_act, SET_ACT + 2)
                line(tt_(begc, begc, bcol, ALU.mult))
                assert line.n == COLS_READY

            convs = [0]

            def conv(b):
                kind, col, _ = BLOCKS[b]
                i = BLOCKS[b][2]
                y = {"q": qT, "k": kT, "v": vT}[kind][:, 4 * i:4 * i + 4, :]
                dve.wait_ge(unit_used, 2 * b + 2)
                for k, tap in enumerate((2, 0, 1, 3, 4)):
                    for j in range(4):
                        src = bank(PROJ + 2 * (b % 2) + j // 2)[:, (j % 2) * T:(j % 2 + 1) * T]
                        ct = (col // P) + j
                        w = conv_c[:, tap * 24 + ct:tap * 24 + ct + 1]
                        o = tap - 2
                        lo, hi = max(0, -o), T - max(0, o)
                        if k == 0:
                            ins = ts_(y[:, j, :], src, w, None, ALU.mult)
                        else:
                            dve.wait_ge(conv_read, convs[0] - 3)
                            ins = stt_(y[:, j, lo:hi], src[:, lo + o:hi + o], w, y[:, j, lo:hi], ALU.mult, ALU.add)
                        ins.then_inc(conv_read, 1)
                        convs[0] += 1

            gdn_line = Line(dve, gdn_sem["dve"])
            att_line = Line(dve, att_sem["dve"])
            m01 = banks[:, MIX:MIX + 2, :]
            m23 = banks[:, MIX + 2:MIX + 4, :]

            def eight(ap):
                return ap.rearrange("p a b c d -> p (a b c) d")

            def mats(ap):
                return ap.rearrange("p b (t n) -> p (b t) n", n=P)

            def gdn_stage(b, s):
                if not GDN[s][0]:
                    return
                heads = (2 * b, 2 * b + 1)
                hs = slice(2 * b, 2 * b + 2)
                dve.wait_ge(gdn_sem["pe"], gdn_count.value("pe", (b, s), 1))
                if s == "norm":
                    dve.wait_ge(gdn_sem["act"], gdn_count.value("act", (b, s), 1))
                    gdn_line(V.reciprocal(rr, rn))
                    gdn_line(tt_(g_k.rearrange("p h t n -> p (h t) n"), bank(MIX).rearrange("p (a n) -> p a n", n=P),
                                 spread(rr[:, 4:8], 4, P), ALU.mult))
                    gdn_line(ts_(rr[:, 0:4], rr[:, 0:4], DK ** -0.5, None, ALU.mult))
                elif s == "decay":
                    gcol = gc[:, hs].rearrange("p h d t -> p (h d t)")
                    gdn_line(tt_(eight(g_E), mats(m23), spread(gcol, 8, P), ALU.subtract))
                    gdn_line(ts_(eight(g_E), eight(g_E), 0.0, None, ALU.min))
                    dve.wait_ge(gdn_sem["act"], gdn_count.value("act", (b, s), 2))
                    for d in range(2):
                        off = CH - 1 if d == 0 else 0
                        gdn_line(V.tensor_copy(glast[:, :, d], g_EG[:, :, d, :, off:P:CH]))
                elif s == "gram":
                    dve.wait_ge(gdn_sem["pool"], gdn_count.value("pool", (b, s)))
                    for h in range(2):
                        kq = bank(MIX + 1)[:, 256 * h:256 * h + 256].rearrange("p (t n) -> p t n", t=2)
                        gdn_line(tt_(g_AT[:, h], kq.unsqueeze(1).broadcast_to([P, 2, 2, P]), g_E[:, h], ALU.mult))
                    gdn_line(tt_(eight(g_E), mats(m23), eight(g_E), ALU.mult))
                    for h in range(2):
                        kk = bank(MIX)[:, 256 * h:256 * h + 256].rearrange("p (t n) -> p t n", t=2)
                        gdn_line(tt_(g_LT[:, h], kk.unsqueeze(1).broadcast_to([P, 2, 2, P]), g_E[:, h], ALU.mult))
                elif s == "first":
                    for dst, src, cols in ((g_XV, g_v, bcol), (g_XK, g_k, begc)):
                        for h in range(2):
                            c = cols[:, heads[h]].unsqueeze(3).broadcast_to([P, 2, 2, P])
                            gdn_line(tt_(dst[:, h], src[:, h].unsqueeze(1).broadcast_to([P, 2, 2, P]), c, ALU.mult))
                elif s[:3] == "sub":
                    gdn_line(tt_(eight(g_TT), eight(g_TT), mats(m23), ALU.subtract))
                    if s != f"sub{LEVELS - 1}":
                        gdn_line(tt_(eight(g_T), eight(g_T), mats(m01), ALU.subtract))
                elif s == "uw":
                    gdn_line(V.tensor_copy(eight(g_U), mats(m01)))
                elif s[0] == "s":
                    step = int(s[1])
                    for d in range(2):
                        tile, r = chunk_of(d, step)
                        new = bank(MIX + 2 * d)[:, 0:256].rearrange("p (h n) -> p h n", h=2)
                        if step == 0:
                            gdn_line(V.tensor_copy(g_S[:, :, d, 0, :], new))
                        else:
                            for h in range(2):
                                gdn_line(stt_(g_S[:, h, d, step, :], g_S[:, h, d, step - 1, :],
                                              glast[:, h, d, tile, r:r + 1], new[:, h, :], ALU.mult, ALU.add))
                elif s[0] == "v":
                    for d in range(2):
                        tile, r = chunk_of(d, int(s[1]))
                        rows = slice(64 * r, 64 * r + 64)
                        u = g_U[rows, :, d, tile, :]
                        gdn_line(tt_(u, u, bank(MIX + 1)[rows, 0:256].rearrange("p (h n) -> p h n", h=2), ALU.subtract))
                elif s == "out":
                    for t in range(2):
                        src = bank(MIX + 2 * t)[:, 0:256].rearrange("p (h n) -> p h n", h=2)
                        q = rr[:, 0:4].rearrange("p (h t) -> p t h", h=2)[:, t]
                        gdn_line(tt_(g_o[:, t], src, spread(q, 2, P), ALU.mult))
                    o4 = g_o.rearrange("p t h n -> p (t h) n")
                    gdn_line(tt_(g_osq.rearrange("p t h n -> p (t h) n"), o4, o4, ALU.mult))
                    gdn_line(V.tensor_reduce(o_ss, g_osq.rearrange("p t h n -> p (t h) n"), AX.X, ALU.add))
                    dve.wait_ge(gdn_sem["act"], gdn_count.value("act", (b, s), 1))
                    gdn_line(V.reciprocal(o_r, o_r))
                    gdn_line(tt_(o4, o4, spread(o_r, 4, P), ALU.mult))

            def att_stage(a, s):
                if a < HEADS and not ATT[s][0] or a == HEADS and not ATT_END[s][0]:
                    return
                dve.wait_ge(att_sem["pe"], att_count.value("pe", (a, s), 1))
                if s == "score":
                    slope = 2.0 ** (-8.0 * (a + 1) / HEADS)
                    for t in range(TT):
                        ps = banks[:, MIX + 2 * t:MIX + 2 * t + 2, 0:T]
                        dd = dist[:, t].unsqueeze(1).broadcast_to([P, 2, T])
                        att_line(stt_(a_s[:, t], dd, -slope * DH ** 0.5, ps, ALU.mult, ALU.add))
                    att_line(V.tensor_reduce(mx, a_s.rearrange("p t m n -> p (t m) n"), AX.X, ALU.max))
                    att_line(ts_(nmx, mx, -DH ** -0.5, None, ALU.mult))
                    dve.wait_ge(att_sem["act"], att_count.value("act", (a, s), 4))
                    att_line(V.reciprocal(rs, sums))
                    att_line(ts_(rl, rs[:, 1:4:2], nlam[:, 0:1], None, ALU.mult))
                    for t in range(TT):
                        att_line(ts_(a_p[:, t, :], a_s[:, t, 0, :], rs[:, 2 * t:2 * t + 1], None, ALU.mult))
                        att_line(stt_(a_p[:, t, :], a_s[:, t, 1, :], rl[:, t:t + 1], a_p[:, t, :], ALU.mult, ALU.add))
                elif s == "pv":
                    att_line(V.tensor_copy(a_od[:, :, a, :], bank(MIX + 1)[:, 0:256].rearrange("p (t n) -> p t n", t=2)))
                elif s == "norm":
                    o = a_od.rearrange("p t h n -> p (t h) n")
                    att_line(tt_(a_sq, o, o, ALU.mult))
                    att_line(V.tensor_reduce(od_ss, a_sq, AX.X, ALU.add))
                    dve.wait_ge(att_sem["act"], att_count.value("act", (a, s), 1))
                    att_line(V.reciprocal(od_r, od_r))
                    att_line(tt_(o, o, spread(od_r, 16, P), ALU.mult))

            for what, i, s in ORDER:
                if what == "end":
                    if BLOCKS[i][0] in CONV:
                        conv(i)
                    if i == 0:
                        decay_columns()
                elif what == "gdn":
                    gdn_stage(i, s)
                elif what == "att":
                    att_stage(i, s)

            for k in range(4):
                for br in range(2):
                    dve.wait_ge(unit_used, UNITS_A + 2 * k + br + 1)
                    if k == 0:
                        dve.wait_ge(block_out, len(BLOCKS))
                    for i in range(2):
                        g = gates[br][:, 4 * k + 2 * i:4 * k + 2 * i + 2, :].rearrange("p a n -> p (a n)")
                        tt_(g, bank(4 * (k % 2) + 2 * br + i), g, ALU.mult).then_inc(merge_dve, 1)
            dve.wait_ge(x_again, 16)
            for k in range(4):
                dve.wait_ge(unit_used, UNITS_A + 8 + 2 * k + 2)
                for t in range(TT):
                    y = x_sb[:, t, NB * k:NB * k + NB]
                    tt_(y, y, bank(2 * (k % 2) + t), ALU.add).then_inc(out_dve, 1)

            rline = Line(dve, route_dve)
            dve.wait_ge(route_act, 3)
            rline(V.reciprocal(rstd, rstd))
            dve.wait_ge(route_pe, 1)
            for k in range(8):
                rline(tt_(h2T[:, 2 * k:2 * k + 2, :], bank(k).rearrange("p (c n) -> p c n", c=2),
                          spread(gffn_c[:, 2 * k:2 * k + 2], 2, T), ALU.mult))
            assert rline.n == H2T_READY
            dve.wait_ge(route_pe, 2)
            rline(tt_(logits, bank(0)[:, 0:2 * (NG + NE)].rearrange("p (t n) -> p t n", t=2),
                      bias_r.unsqueeze(1).broadcast_to([P, TT, NG + NE]), ALU.add))
            glog = logits[:, :, 0:NG]
            BIG = 1024.0

            def per_tile(v, n):
                return v.unsqueeze(2).broadcast_to([P, TT, n])

            def first_max(vals, n, top, hot, tmp):
                iot = iota[:, 0:n].unsqueeze(1).broadcast_to([P, TT, n])
                rline(V.tensor_reduce(top, vals, AX.X, ALU.max))
                rline(tt_(tmp, vals, per_tile(top, n), ALU.is_equal))
                rline(stt_(tmp, tmp, -BIG, iot, ALU.mult, ALU.add))
                rline(V.tensor_reduce(rs1[:, 15, :], tmp, AX.X, ALU.min))
                rline(tt_(hot, tmp, per_tile(rs1[:, 15, :], n), ALU.is_equal))

            ghot = rt[:, 1, :, 0:NG]
            first_max(glog, NG, rs1[:, 0, :], ghot, rt[:, 2, :, 0:NG])
            rline(tt_(rt[:, 0, :, 0:NG], glog, per_tile(rs1[:, 0, :], NG), ALU.subtract))
            assert rline.n == GROUP_MAX
            ehot = rt[:, 3].rearrange("p t (g e) -> p t g e", g=NG)
            el = logits[:, :, NG:NG + NE].rearrange("p t (g e) -> p t g e", g=NG)
            for t in range(TT):
                rline(tt_(ehot[:, t], el[:, t], ghot[:, t, :].unsqueeze(2).broadcast_to([P, NG, EPG]), ALU.mult))
            esel = rt[:, 4, :, 0:EPG]
            for t in range(TT):
                rline(V.tensor_reduce(esel[:, t], ehot[:, t].rearrange("p g e -> p e g"), AX.X, ALU.add))
            hot1, hot2, tmp8 = (rt[:, i, :, 0:EPG] for i in (5, 6, 2))
            first_max(esel, EPG, rs1[:, 1, :], hot1, tmp8)
            rline(stt_(esel, hot1, -1e30, esel, ALU.mult, ALU.add))
            first_max(esel, EPG, rs1[:, 2, :], hot2, tmp8)
            rline(tt_(rs1[:, 7, :], rs1[:, 2, :], rs1[:, 1, :], ALU.subtract))
            assert rline.n == TOP_TWO
            dve.wait_ge(route_act, ROUTE_ACT)
            rline(V.tensor_reduce(rs1[:, 3, :], rt[:, 0, :, 0:NG], AX.X, ALU.add))
            rline(ts_(rs1[:, 4, :], rs1[:, 7, :], 1.0, None, ALU.add))
            rline(tt_(rs1[:, 5, :], rs1[:, 3, :], rs1[:, 4, :], ALU.mult))
            rline(V.reciprocal(rs1[:, 5, :], rs1[:, 5, :]))
            rline(tt_(rs1[:, 6, :], rs1[:, 5, :], rs1[:, 7, :], ALU.mult))
            rline(tt_(rt[:, 7, :, 0:EPG], hot1, per_tile(rs1[:, 5, :], EPG), ALU.mult))
            rline(tt_(rt[:, 7, :, 8:8 + EPG], hot2, per_tile(rs1[:, 6, :], EPG), ALU.mult))
            rline(tt_(rt[:, 7, :, 0:EPG], rt[:, 7, :, 0:EPG], rt[:, 7, :, 8:8 + EPG], ALU.add))
            rline(tt_(hot1, hot1, hot2, ALU.add))
            for dst, src in ((m_weight, rt[:, 7, :, 0:EPG]), (m_mask, hot1)):
                for t in range(TT):
                    rline(tt_(dst[:, t].rearrange("p (g e) -> p g e", g=NG), src[:, t].unsqueeze(1).broadcast_to([P, NG, EPG]),
                              ghot[:, t, :].unsqueeze(2).broadcast_to([P, NG, EPG]), ALU.mult))
            assert rline.n == MASK_READY
            dve.wait_ge(route_pe, 3)
            rline(stt_(m_rank, bank(1)[:, 0:2 * NE].rearrange("p (t n) -> p t n", t=2), 1.0, m_mask, ALU.add, ALU.mult))
            rline(ts_(m_rank, m_rank, 1.0, None, ALU.subtract))
            rline(V.tensor_reduce(over_f, bank(1)[:, 2 * NE:3 * NE], AX.X, ALU.max))
            rline(ts_(over_f, over_f, float(SLOTS), None, ALU.is_gt))
            rline(V.tensor_copy(over_i, over_f))
            assert rline.n == ROUTE_FLAG

            def experts_pair(n, i):
                dve.wait_ge(gathered, 4 * n + 1)
                for t in range(TT):
                    r = m_rank[:, t, bass.ds(2 * i, 2)].unsqueeze(2).broadcast_to([P, 2, SLOTS])
                    tt_(pick[:, t], iota.unsqueeze(1).broadcast_to([P, 2, SLOTS]), r, ALU.is_equal).then_inc(pick_ready, 1)
                dve.wait_ge(pick_ready, 4 * n + 2)
                for t in range(TT):
                    w = m_weight[:, t, bass.ds(2 * i, 2)].unsqueeze(2).broadcast_to([P, 2, SLOTS])
                    tt_(pick_w[:, t], pick[:, t], w, ALU.mult).then_inc(pick_ready, 1)
                for k in range(4):
                    dve.wait_ge(gathered, 4 * n + k + 2)
                    tt_(xe[:, 4 * k:4 * k + 4, :], bank(k % 2).rearrange("p (c n) -> p c n", c=4),
                        spread(gffn_c[:, 4 * k:4 * k + 4], 4, P), ALU.mult).then_inc(gather_read, 1)
                for e in range(2):
                    X = 2 * n + e
                    dve.wait_ge(silu_done, X + 1)
                    tt_(hid.rearrange("p a b -> p (a b)"), silu_g.rearrange("p a b -> p (a b)"), bank(4)[:, T:2 * T],
                        ALU.mult).then_inc(hid_ready, 1)
                for q in range(8):
                    t, j = divmod(q, 4)
                    dve.wait_ge(scatter_done, 8 * n + q + 2)
                    y = x_sb[:, t, NB * j:NB * j + NB]
                    dve.wait_ge(added, 8 * n + 2)
                    tt_(y, y, bank(0 if q % 2 else 7), ALU.add).then_inc(added, 1)

            dve.sem_inc(gather_read, 2)
            dve.sem_inc(added, 2)
            dve.sem_inc(hid_ready, 1)
            with dve.Fori(0, NE // 2) as n:
                experts_pair(n, n)
            with dve.If(dve.value_load(over_i[0:1, 0:1], min_val=0, max_val=1) > 0):
                for r in range(1, ROUNDS):
                    dve.wait_ge(gathered, 4 * (NE // 2) * r + 1)
                    ts_(m_rank, m_rank, float(SLOTS), None, ALU.subtract).then_inc(next_round, 1)
                    dve.wait_ge(next_round, r)
                    with dve.Fori(0, NE // 2) as i:
                        experts_pair(i + r * (NE // 2), i)
            fline = Line(dve, fin_dve)
            for t in range(TT):
                fline(V.tensor_tensor_reduce(out=h2[:, t].rearrange("p c q -> p (c q)"), in0=x_sb[:, t, :], in1=x_sb[:, t, :],
                                             scale=1.0, scalar=0.0, op0=ALU.mult, op1=ALU.add, accum_out=fin_ss[:, t:t + 1]))
            dve.wait_ge(fin_act, 1)
            fline(V.reciprocal(fin_ss, fin_ss))
            dve.wait_ge(final_in, 16)
            for t in range(TT):
                fline(stt_(x_sb[:, t, :], x_sb[:, t, :], fin_ss[:, t:t + 1], g_last, ALU.mult, ALU.mult))
            assert fline.n == FINAL_ROWS


_INS = ["x", "g_mix", "w_in", "conv_w", "a_log", "dt_bias", "gdn_norm_w", "diff_lambda", "diff_norm_w",
        "w_branch_a", "w_branch_d", "w_out", "g_ffn", "w_group", "b_group", "w_router", "b_router",
        "w_exp_gate", "w_exp_up", "w_exp_down", "g_final"]


def kernel(**inputs):
    import numpy as _np
    import concourse.bacc as _bacc
    from concourse import mybir as _mybir
    from concourse.bass_utils import run_bass_kernel_spmd as _run

    nc = _bacc.Bacc("TRN2", target_bir_lowering=False, num_devices=1)
    arrays = {f"in_{name}_dram": _np.ascontiguousarray(inputs[name]) for name in _INS}
    arrays["in_tables_dram"] = constants()
    args = [nc.dram_tensor(name, a.shape, _mybir.dt.from_np(a.dtype), kind="ExternalInput").ap()
            for name, a in arrays.items()]
    args.append(nc.dram_tensor("out_dram", (1, T, D), F32, kind="ExternalOutput").ap())
    encoder(nc, *args)
    r = _run(nc, [arrays], core_ids=[0])
    return r.results[0]["out_dram"]
```

```python
import math
from contextlib import ExitStack

import concourse.bass as bass
from concourse import mybir

F32 = mybir.dt.float32
F32R = mybir.dt.float32r
I32 = mybir.dt.int32
ALU = mybir.AluOpType
ACT = mybir.ActivationFunctionType
AX = mybir.AxisListType

P = 128
D = 2048
T = 256
TT = T // P
KC = D // P
HEADS = 8
DK = 128
CH = 64
DH = 64
NG, EPG = 4, 8
NE = NG * EPG
FE = 512
SLOTS = 64
ROUNDS = T // SLOTS
EPS = 1e-6
LAM_INIT = 0.8 - 0.6 * math.exp(-0.3 * 0)

QK = HEADS * DK
OFF_Q, OFF_K, OFF_V, OFF_Z = 0, QK, 2 * QK, 3 * QK
OFF_AB = 4 * QK
OFF_AQ = OFF_AB + 4 * HEADS
OFF_AK, OFF_AV = OFF_AQ + QK, OFF_AQ + 2 * QK
OFF_GA = OFF_AQ + 3 * QK
OFF_GD = OFF_GA + D
NB = 512

BLOCKS = [("q", OFF_Q, 0), ("k", OFF_K, 0), ("v", OFF_V, 0), ("z", OFF_Z, 0), ("z", OFF_Z + NB, 1),
          ("aq", OFF_AQ, 0), ("aq", OFF_AQ + NB, 1),
          ("q", OFF_Q + NB, 1), ("k", OFF_K + NB, 1), ("v", OFF_V + NB, 1),
          ("ak", OFF_AK, 0), ("ak", OFF_AK + NB, 1), ("av", OFF_AV, 0), ("av", OFF_AV + NB, 1)]
BLOCKS += [("ga", OFF_GA + NB * i, i) for i in range(4)] + [("gd", OFF_GD + NB * i, i) for i in range(4)]
QKV_THERE = (3, 10)
Z_THERE = (4, 5)
MIX_FROM, GDN_AGAIN, ATT_FROM = 3, 10, 16
CONV = ("q", "k", "v")
TAPS = 5
TOKEN_MAJOR = ("z", "av")

LEVELS = 6
GDN = {"norm": (3, 2, 2), "decay": (4, 3, 1), "gram": (3, 0, 2), "first": (0, 1, 1)}
for _l in range(1, LEVELS):
    GDN[f"lt{_l}"] = (1, 1, 1) if _l <= 2 else (0, 1, 0)
    GDN[f"sub{_l}"] = (2, 0, 1) if _l < LEVELS - 1 else (1, 0, 0)
GDN |= {"uw": (1, 1, 0), "s0": (2, 0, 0), "v1": (2, 0, 0), "s1": (4, 0, 0), "v2": (2, 0, 0),
        "s2": (4, 0, 0), "v3": (2, 0, 0), "out": (6, 1, 2), "turn": (0, 1, 0)}
ATT = {"score": (10, 4, 0), "pT": (0, 1, 0), "pv": (1, 0, 0)}
ATT_END = {"norm": (4, 1, 1), "turn": (0, 1, 0)}
GDN_BATCHES = HEADS // 2

PARTS_ACT, SET_ACT, XN_READY = 16, 21, (5, 7)
CONV_BANK, HT_READY, AB_PARTS, AB_X, G_READY, GC_READY, COLS_READY = 8, 11, 20, 27, 29, 36, 37
SMALL_ALL = 16 * 10
H2_READY, ROUTE_ACT = (4, 6), 9
H2T_READY, GROUP_MAX, TOP_TWO, MASK_READY, ROUTE_FLAG = 14, 21, 37, 50, 61
FINAL_ROWS = 5


def conv_blocks(b):
    return sum(kind in CONV for kind, _, _ in BLOCKS[:b + 1])


def chunk_of(direction, step):
    return divmod(step if direction == 0 else T // CH - 1 - step, 2)


class StageCounts:

    def __init__(self, stages):
        self.before = {}
        at = [0, 0, 0, 0]
        for key, ops in stages:
            self.before[key] = tuple(at)
            at = [a + b for a, b in zip(at, (*ops, 1))]
        self.total = tuple(at)

    def value(self, engine, key, k=0):
        return self.before[key][("dve", "act", "pool", "pe").index(engine)] + k


GDN_STAGES = [((b, s), ops) for b in range(GDN_BATCHES) for s, ops in GDN.items()]
ATT_STAGES = [((0, "score"), ATT["score"])]
for _a in range(HEADS):
    if _a < HEADS - 1:
        ATT_STAGES.append(((_a + 1, "score"), ATT["score"]))
    ATT_STAGES += [((_a, s), ATT[s]) for s in ("pT", "pv")]
ATT_STAGES += [((HEADS, s), ops) for s, ops in ATT_END.items()]


def stage_order():
    gdn = [("gdn", *key) for key, _ in GDN_STAGES]
    att = [("att", *key) for key, _ in ATT_STAGES]
    order = []
    conv = []
    rest = 0
    for b in range(len(BLOCKS)):
        for s in range(KC // 2):
            order.append(("pair", b, s))
            if conv:
                order.append(conv.pop(0))
            if gdn and (gdn[0][1] < 2 or b >= GDN_AGAIN) and (b, s) >= (MIX_FROM, TAPS):
                if b > GDN_AGAIN or b < GDN_AGAIN and gdn[0][1] < 2 or s >= TAPS:
                    order.append(gdn.pop(0))
            elif b >= ATT_FROM and not gdn and att:
                if rest:
                    rest -= 1
                    continue
                order.append(att.pop(0))
                rest = order[-1][1:] == (0, "score")
        order.append(("end", b, 0))
        if BLOCKS[b][0] in CONV:
            conv = [("conv", b, k) for k in range(TAPS + 1)]
    assert not gdn and not att
    return order


ORDER = stage_order()

SLOT = 4096
RING = 0
G_E, G_LT, G_EG, G_AT, G_UT, G_T, G_TT, G_Z = 0, 512, 1024, 2048, 2560, 3072, 3584, 4096
G_XV, G_XK, G_KS, G_U, G_WT = (4608 + 1024 * i for i in range(5))
G_S = G_WT + 1024
G_KTM = G_S + 1536
G_VTM = G_KTM + 512
A_OD = 8192
A_TMP = A_OD + 2048
UNIT = 2048
UNIT_RING = 12288
QKV = UNIT_RING + 3 * UNIT
ZS = QKV + 3072
AQK = ZS + 2048
X2 = AQK + 2048
YA = AQK + 6144
YD = YA + 2048
CONST = YD + 2048
W_ROUTE = 6 * SLOT
MOE = YA
LATE = CONST + 512
SMALL = LATE + 2560
WORDS = 38864
PARTS = 2 * 4096
STAGE = 1024
STAGES = 5
R_STAGE = PARTS
R_AB = R_STAGE + STAGES * STAGE
R_WORDS = R_AB + 1024
LEAD = 4

C_IDENT, C_BEFORE, C_ONES, C_IOTA = 0, 128, 256, 384
C_TWICE = C_IOTA + 64
C_TRI = C_TWICE + 64
C_TRI64 = C_TRI + 512
C_LEVEL = C_TRI64 + 128
C_DIST = C_LEVEL + 2 * LEVELS * CH
N_CONST = C_DIST + 512
assert CONST + C_TRI == LATE and CONST + N_CONST <= SMALL


def constants():
    import numpy as np
    c = np.zeros((P, N_CONST), np.float32)
    i = np.arange(P)
    r, n = i[:, None], i[None, :]
    same = (r // CH) == (n // CH)
    c[:, C_IDENT:C_IDENT + 128] = r == n
    for k, m in enumerate([r <= n, r >= n, r > n, r < n]):
        c[:, C_TRI + 128 * k:C_TRI + 128 * (k + 1)] = same & m
    r, n = (i % CH)[:, None], np.arange(CH)[None, :]
    for k, m in enumerate([r <= n, r >= n]):
        c[:, C_TRI64 + CH * k:C_TRI64 + CH * (k + 1)] = m
    for lv in range(LEVELS):
        m = 1 << lv
        block = (r // (2 * m)) == (n // (2 * m))
        low_r, low_n = (r // m) % 2 == 0, (n // m) % 2 == 0
        for d, mask in enumerate([low_r & ~low_n, ~low_r & low_n]):
            at = C_LEVEL + (lv * 2 + d) * CH
            c[:, at:at + CH] = block & mask
    r, n = i[:, None], i[None, :]
    for t in range(TT):
        c[:, C_DIST + 256 * t:C_DIST + 256 * (t + 1)] = np.abs(i[:, None] + 128 * t - np.arange(T)[None, :])
    c[:, C_BEFORE:C_BEFORE + 128] = r < n
    c[:, C_ONES:C_ONES + 128] = 1.0
    c[:, C_IOTA:C_IOTA + 64] = np.arange(64)[None, :]
    c[:, C_TWICE:C_TWICE + 64] = (i % 64)[:, None] == np.arange(64)[None, :]
    return c


def encoder(nc, x, g_mix, w_in, conv_w, a_log, dt_bias, gdn_norm_w, diff_lambda, diff_norm_w,
            w_branch_a, w_branch_d, w_out, g_ffn, w_group, b_group, w_router, b_router,
            w_exp_gate, w_exp_up, w_exp_down, g_final, const_tables, out):
    ctx = ExitStack()
    with ctx:
        def sem(name):
            return ctx.enter_context(nc.semaphore(name))

        arena = ctx.enter_context(nc.sbuf_tensor("arena", [P, WORDS], F32))
        rounded = ctx.enter_context(nc.sbuf_tensor("rounded", [P, R_WORDS], F32R))
        banks = ctx.enter_context(nc.psum_tensor("banks", [P, 8, 512], F32))
        PROJ, MIX = 0, 4

        def at(off, *shape, tensor=None):
            n = math.prod(shape)
            v = (arena if tensor is None else tensor)[:, off:off + n]
            names = "abcde"[:len(shape)]
            if len(shape) > 1:
                v = v.rearrange(f"p ({' '.join(names)}) -> p {' '.join(names)}",
                                **dict(zip(names[:-1], shape[:-1])))
            return v

        def bank(i):
            return banks[:, i, :]

        def spread(ap, *shape):
            return ap.unsqueeze(len(shape)).broadcast_to([P, *shape])

        ident = at(CONST + C_IDENT, 128)
        tri = at(CONST + C_TRI, 4, 128)
        tri64 = at(CONST + C_TRI64, 2, CH)
        level = at(CONST + C_LEVEL, LEVELS, 2, CH)
        dist = at(CONST + C_DIST, TT, T)
        before = at(CONST + C_BEFORE, 128)
        ones = at(CONST + C_ONES, 128)
        iota = at(CONST + C_IOTA, 64)
        twice = at(CONST + C_TWICE, 64)
        small = [SMALL]

        def take(*shape):
            v = at(small[0], *shape)
            small[0] += math.prod(shape)
            assert small[0] <= WORDS
            return v

        gmix_c, gffn_c = take(KC), take(KC)
        conv_rows, conv_c = take(P), take(5 * 24)
        dtb, alog = take(16), take(16)
        gdn_w, diff_w = take(DK), take(DK)
        lam_in = take(4, 64)
        w_ab = take(KC, 32)
        bias_r = take(NG + NE)
        eps_c, one_c, nlam = take(1), take(1), take(1)
        ss, rstd = take(2), take(2)
        ab_x, ab_t, ab_u = take(TT, 16), take(TT, 16), take(TT, 16)
        g_log, beta = take(TT, 16), take(TT, 16)
        gc, begc, esfx, bcol = (take(2, HEADS, 2) for _ in range(4))
        lam_p, lam_s = take(2, 64), take(2)
        rn, rr = take(8), take(8)
        glast = take(2, 2, 2, 2)
        o_ss, o_r = take(4), take(4)
        mx, nmx, sums, rs, rl = take(4), take(4), take(4), take(4), take(2)
        od_ss, od_r = take(16), take(16)
        w_route = at(W_ROUTE, KC, NG + NE)

        x_sb = at(X2, TT, D)
        xn = at(RING, TT, KC, P)
        hT = at(YA, KC, T)
        h_part = [at(4096 * i, KC, T, tensor=rounded) for i in range(2)]
        y_part = [[at(4096 * i + 2048 * br, HEADS, T, tensor=rounded) for i in range(2)] for br in range(2)]
        w_part = [[at(R_STAGE + STAGE * i + 512 * k, NB, tensor=rounded) for k in range(2)] for i in range(STAGES)]
        ab_part = [at(R_AB + 512 * i, KC, 32, tensor=rounded) for i in range(2)]
        qT, kT, vT = (at(QKV + 1024 * i, HEADS // 2, T) for i in range(3))
        zs = at(ZS, TT, QK)
        aq, ak = at(AQK, HEADS, T), at(AQK + 2048, HEADS, T)
        av = at(AQK + 4096, TT, QK)

        def gate(br, k):
            n = 4 * br + k
            return at(QKV + 1024 * n if n < 2 else 1024 * (n - 2), 4 * T)

        ya, yd = at(YA, HEADS, T), at(YD, HEADS, T)

        g_sq = at(G_KS, 2, 2, T)
        g_E, g_LT, g_AT, g_UT, g_T, g_TT, g_Z = (
            at(o, 2, 2, 2, CH) for o in (G_E, G_LT, G_AT, G_UT, G_T, G_TT, G_Z))
        g_EG, g_XV, g_XK, g_KS, g_U = (at(o, 2, 2, 2, P) for o in (G_EG, G_XV, G_XK, G_KS, G_U))
        g_WT = at(G_WT, 2, 2, 2, 2, CH)
        g_S = at(G_S, 2, 2, 3, P)
        g_k, g_v = at(G_KTM, 2, 2, P), at(G_VTM, 2, 2, P)
        g_kT = at(G_U, 2, T)
        g_o, g_osq = at(G_XV, 2, 2, P), at(G_XV + 512, 2, 2, P)

        a_od = at(A_OD, TT, HEADS, P)
        a_s = at(A_TMP, TT, 2, T)
        a_p, a_pT = at(A_TMP + 1024, TT, T), at(A_TMP + 1536, 2, TT, P)
        a_sq = at(A_TMP, TT * HEADS, P)

        h2_part = [at(4096 * i, TT, KC, P, tensor=rounded) for i in range(2)]
        h2T = at(YA, KC, T)
        ident_r = at(R_AB + 512, P, tensor=rounded)
        pick = at(R_AB, TT, 2, SLOTS, tensor=rounded)
        y_sb = at(LATE, 4, 512)
        g_last = at(RING, D)
        junk = [at(RING + SLOT * (1 + t), D) for t in range(TT)]
        moe_at = [MOE]

        def moe(*shape):
            v = at(moe_at[0], *shape)
            moe_at[0] += math.prod(shape)
            assert moe_at[0] <= CONST
            return v

        xe = moe(KC, 2 * SLOTS)
        g_part, u_part = moe(FE), moe(FE)
        silu_g, hid = moe(4, SLOTS), moe(4, SLOTS)
        pick_w, ws = moe(TT, 2, SLOTS), moe(T)
        rt = at(LATE + 2048, 8, TT, NE)
        logits = take(TT, NG + NE)
        rs1 = take(16, TT)
        m_mask, m_weight = at(W_ROUTE + KC * (NG + NE), TT, NE), at(W_ROUTE + KC * (NG + NE) + TT * NE, TT, ROUNDS * NE)
        m_rank = w_ab.rearrange("p a b -> p (a b)")[:, :TT * ROUNDS * NE].rearrange("p (a b) -> p a b", a=TT)
        fit = W_ROUTE + KC * (NG + NE) + TT * NE * (1 + ROUNDS)
        assert fit <= X2
        fin_ss = take(TT)
        over_f, over_i = take(1), take(1).bitcast(I32)

        x_in, table_in, small_in, wab_in = sem("x_in"), sem("table_in"), sem("small_in"), sem("wab_in")
        set_act, set_dve, set_pe = sem("set_act"), sem("set_dve"), sem("set_pe")
        unit_in = [sem(f"unit_in{i}") for i in range(3)]
        split_h, split_l = sem("split_h"), sem("split_l")
        chunk_used = sem("chunk_used")
        y_split_h, y_split_l = sem("y_split_h"), sem("y_split_l")
        m_split_h, m_split_l = sem("m_split_h"), sem("m_split_l")
        conv_read = sem("conv_read")
        block_out = sem("block_out")
        gdn_sem = {e: sem(f"gdn_{e}") for e in ("dve", "act", "pool", "pe")}
        att_sem = {e: sem(f"att_{e}") for e in ("dve", "act", "pool", "pe")}
        merge_dve, merge_pool = sem("merge_dve"), sem("merge_pool")
        x_again, out_dve = sem("x_again"), sem("out_dve")
        route_in = sem("route_in")
        route_pe, route_dve, route_act = sem("route_pe"), sem("route_dve"), sem("route_act")
        full = [sem(f"expert_unit_in{i}") for i in range(6)]
        unit_free = [sem(f"{w}_used") for w in ("gate", "up", "down")]
        pick_ready, ws_turned, ws_ready = sem("pick_ready"), sem("ws_turned"), sem("ws_ready")
        gathered, gather_read = sem("gathered"), sem("gather_read")
        gu_copied, gu_turned = sem("gu_copied"), sem("gu_turned")
        silu_done, hid_ready, y_copied = sem("silu_done"), sem("hid_ready"), sem("y_copied")
        scatter_done, added = sem("scatter_done"), sem("added")
        final_in, fin_act, fin_dve, stored = sem("final_in"), sem("fin_act"), sem("fin_dve"), sem("stored")

        gdn_count = StageCounts(GDN_STAGES)
        att_count = StageCounts(ATT_STAGES)

        def wait_part(eng, sems, counts, me, key, offsets=()):
            off = dict(offsets)
            for e in ("dve", "act", "pool", "pe"):
                n = counts.value(e, key, off.get(e, 0))
                if n > 0:
                    eng.wait_ge(sems[e], n)

        class Line:

            def __init__(self, eng, s):
                self.eng, self.sem, self.n = eng, s, 0

            def __call__(self, ins):
                self.n += 1
                ins.then_inc(self.sem, 1)
                self.eng.wait_ge(self.sem, self.n)

        block = ctx.enter_context(nc.Block())

        wi = w_in[0].rearrange("(u p c) n -> u p c n", u=2, c=8)
        wa, wd = (w[0].rearrange("(c p) n -> p c n", p=P) for w in (w_branch_a, w_branch_d))
        wo = w_out[0].rearrange("(c p) n -> p c n", p=P)
        xt = x[0].rearrange("(t p) d -> p t d", p=P)
        M0 = KC * len(BLOCKS)
        O0 = M0 + 4 * 2 * HEADS
        CHUNKS = O0 + 4 * KC
        UNITS = CHUNKS // 4

        def unit_source(n):
            c = 4 * n
            if c < M0:
                col = BLOCKS[c // KC][1]
                return wi[c % KC // 8, :, c % 8:c % 8 + 4, col:col + NB]
            if c < O0:
                k, br = divmod((c - M0) // HEADS, 2)
                return (wa, wd)[br][:, c % HEADS:c % HEADS + 4, NB * k:NB * k + NB]
            k = (c - O0) // KC
            return wo[:, c % KC:c % KC + 4, NB * k:NB * k + NB]

        def unit(n):
            return at(UNIT_RING + UNIT * (n % 3), 4, NB)

        eg = w_exp_gate[0].rearrange("e (u p c) f -> e u p c f", u=2, c=8)
        eu = w_exp_up[0].rearrange("e (u p c) f -> e u p c f", u=2, c=8)
        ed = w_exp_down[0].rearrange("e (u k p) d -> e u p k d", u=2, p=P)

        def expert_unit(s, *shape):
            return at(RING + SLOT * s, *shape)

        def expert_source(e, s):
            return (eg, eu, ed)[s // 2][e, s % 2]

        def expert_target(s):
            return expert_unit(s, 8, FE) if s < 4 else expert_unit(s, 2, D)

        @block.sync
        def _(sp):
            sp.dma_start(x_sb[:, 0], xt[:, 0]).then_inc(x_in, 16)
            sp.dma_start(x_sb[:, 1], xt[:, 1]).then_inc(x_in, 16)
            sp.dma_start(at(CONST, N_CONST), const_tables).then_inc(table_in, 16)
            for n in range(UNITS):
                if n >= 3:
                    sp.wait_ge(split_l, 4 * (n - 2))
                sp.dma_start(unit(n), unit_source(n)).then_inc(unit_in[n % 3], 16)
                if n == M0 // 4 + 2:
                    sp.wait_ge(att_sem["pe"], att_count.total[3])
                    sp.wait_ge(att_sem["act"], att_count.total[1])
                    sp.dma_start(x_sb, xt).then_inc(x_again, 16)
                    for w, a, b in ((w_group, 0, NG), (w_router, NG, NG + NE)):
                        for u in range(2):
                            sp.dma_start(w_route[:, 8 * u:8 * u + 8, a:b],
                                         w[0].rearrange("(u p c) n -> u p c n", u=2, c=8)[u]).then_inc(route_in, 16)
                    for s in (2, 5):
                        sp.dma_start(expert_target(s), expert_source(0, s)).then_inc(full[s], 16)
                if n == O0 // 4 + 4:
                    sp.wait_ge(m_split_l, 4)
                    for s in (0, 1):
                        sp.dma_start(expert_target(s), expert_source(0, s)).then_inc(full[s], 16)
            sp.wait_ge(split_l, CHUNKS)
            for s in (3, 4):
                sp.dma_start(expert_target(s), expert_source(0, s)).then_inc(full[s], 16)

            def load_expert(n, e):
                for s in range(6):
                    sp.wait_ge(unit_free[s // 2], 2 * n + (s % 2 - 1))
                    sp.dma_start(expert_target(s), expert_source(e, s)).then_inc(full[s], 16)

            with sp.Fori(1, NE) as e:
                load_expert(e, e)
            sp.wait_ge(route_dve, ROUTE_FLAG)
            sp_over = sp.value_load(over_i[0:1, 0:1], min_val=0, max_val=1)
            with sp.If(sp_over > 0):
                with sp.Fori(1, ROUNDS) as r:
                    with sp.Fori(0, NE) as e:
                        load_expert(r * NE + e, e)
            sp.wait_ge(added, 8 * (NE // 2) + 2)
            sp.wait_ge(fin_dve, 1)
            sp.dma_start(g_last, g_final.partition_broadcast(P)).then_inc(final_in, 16)
            for t in range(TT):
                sp.wait_ge(fin_dve, FINAL_ROWS - 1 + t)
                sp.dma_start(out[0].rearrange("(t p) d -> p t d", p=P)[:, t], x_sb[:, t]).then_inc(stored, 16)
            sp.wait_ge(stored, 32)

        @block.tensor
        def _(pe):
            mm = nc.tensor.matmul
            turn = nc.tensor.transpose

            pe.wait_ge(table_in, 16)
            for t in range(TT):
                pe.wait_ge(set_act, XN_READY[t])
                for c in range(KC):
                    last = turn(bank(c // 2)[:, (c % 2) * T + t * P:(c % 2) * T + t * P + P], xn[:, t, c, :], ident)
            last.then_inc(set_pe, 1)
            pe.wait_ge(small_in, SMALL_ALL)
            pe.wait_ge(set_dve, CONV_BANK)
            turn(bank(4)[:, 0:120], conv_rows[0:120, :], ident[0:120, 0:120]).then_inc(set_pe, 1)

            def thrice(out, lefts, rights, first, final, **more):
                lh, ll = lefts
                rh, rl = rights
                mm(out, lh, rh, start=first, stop=False, skip_group_check=True)
                mm(out, lh, rl, start=False, stop=False, skip_group_check=True)
                return mm(out, ll, rh, start=False, stop=final, skip_group_check=True)

            def decay_and_beta():
                pe.wait_ge(set_dve, AB_PARTS)
                for t in range(TT):
                    for c in range(KC):
                        last = thrice(bank(5)[:, 32 * t:32 * t + 32], [h[:, c, t * P:(t + 1) * P] for h in h_part],
                                      [w[:, c, :] for w in ab_part], c == 0, c == KC - 1)
                last.then_inc(set_pe, 1)

            def decay_sums():
                pe.wait_ge(set_dve, G_READY)
                for k in range(4):
                    for t in range(TT):
                        last = mm(bank(6)[:, (k * 2 + t) * 8:(k * 2 + t) * 8 + 8], tri[:, k, :],
                                  g_log[:, t, (k % 2) * 8:(k % 2) * 8 + 8], start=True, stop=True)
                last.then_inc(set_pe, 1)

            def by_channel(m, b0, moving, first, final):
                pe.wait_ge(split_l, m + 1)
                w = w_part[m % STAGES]
                for j in range(4):
                    last = thrice(bank(b0 + j // 2)[:, (j % 2) * T:(j % 2 + 1) * T], [p[:, j * P:(j + 1) * P] for p in w],
                                  moving, first and j % 2 == 0, final)
                last.then_inc(chunk_used, 1)

            def by_token(m, b0, stationary, first, final):
                pe.wait_ge(split_l, m + 1)
                for t in range(TT):
                    last = thrice(bank(b0 + t), [p[:, t * P:(t + 1) * P] for p in stationary], w_part[m % STAGES],
                                  first, final)
                last.then_inc(chunk_used, 1)

            def pair(b, s):
                kind = BLOCKS[b][0]
                b0 = PROJ + 2 * (b % 2)
                if s == 0 and b >= 2:
                    if BLOCKS[b - 2][0] in CONV:
                        pe.wait_ge(conv_read, 20 * conv_blocks(b - 2))
                    else:
                        pe.wait_ge(block_out, b - 1)
                if b == 0:
                    pe.wait_ge(set_dve, HT_READY + s + 1)
                for c in (2 * s, 2 * s + 1):
                    (by_token if kind in TOKEN_MAJOR else by_channel)(
                        KC * b + c, b0, [h[:, c, :] for h in h_part], c == 0, c == KC - 1)

            DHT = [(d, h, t) for d in range(2) for h in range(2) for t in range(2)]

            def mix(i, j=0, n=P):
                return bank(MIX + i)[:, P * j:P * j + n]

            def chunkwise(i, left, right):
                for n, (d, h, t) in enumerate(DHT):
                    for r in range(2):
                        rows = slice(CH * r, CH * r + CH)
                        last = mm(bank(MIX + i)[rows, CH * n:CH * n + CH], left(d, h, t)[rows], right(d, h, t)[rows],
                                  start=True, stop=True)
                return last

            def gdn_stage(b, s):
                if s == "gram":
                    pe.wait_ge(gdn_sem["act"], gdn_count.value("act", (b, "decay"), 2))
                    pe.wait_ge(gdn_sem["dve"], gdn_count.value("dve", (b, "decay"), 1))
                else:
                    wait_part(pe, gdn_sem, gdn_count, "pe", (b, s), {"pool": 2} if s == "norm" else {})
                heads = (2 * b, 2 * b + 1)
                single = dict(start=True, stop=True)
                if s == "norm":
                    pe.wait_ge(block_out, QKV_THERE[b // 2])
                    for k, src in enumerate((kT, vT)):
                        for h in range(2):
                            for t in range(2):
                                turn(mix(k, 2 * h + t), src[:, heads[h] % 4, t * P:(t + 1) * P], ident)
                    for qk in range(2):
                        for h in range(2):
                            for t in range(2):
                                n = qk * 4 + h * 2 + t
                                last = mm(mix(2)[:, n:n + 1], g_sq[:, qk, h, t * P:(t + 1) * P], ones[:, 0:1], **single)
                elif s == "decay":
                    if b == 0:
                        pe.wait_ge(set_dve, COLS_READY)
                    for h in range(2):
                        for t in range(2):
                            turn(mix(0, 2 * h + t), g_k[:, h, t, :], ident)
                    def log_col(d, h, t):
                        return g_log[:, t, d * 8 + heads[h]:d * 8 + heads[h] + 1]

                    chunkwise(1, lambda d, h, t: log_col(d, h, t).broadcast_to([P, CH]), lambda d, h, t: tri64[:, d, :])
                    for d, h, t in DHT:
                        last = mm(mix(2 + d, 2 * h + t), log_col(d, h, t).broadcast_to([P, P]), tri[:, d, :], **single)
                elif s == "gram":
                    for h in range(2):
                        for t in range(2):
                            for r in range(2):
                                cols = slice(P * t + CH * r, P * t + CH * r + CH)
                                o = bank(MIX)[CH * r:CH * r + CH]
                                n = CH * (2 * h + t)
                                mm(o[:, n:n + CH], g_kT[:, h, cols], g_kT[:, h, cols], **single)
                                mm(bank(MIX + 1)[CH * r:CH * r + CH, n:n + CH], g_kT[:, h, cols], qT[:, heads[h] % 4, cols], **single)
                    last = chunkwise(2, lambda d, h, t: bcol[:, d, heads[h], t:t + 1].broadcast_to([P, CH]),
                                     lambda d, h, t: twice)
                elif s == "first":
                    last = chunkwise(2, lambda *m: g_TT[:, *m, :], lambda *m: twice)
                elif s[:2] == "lt":
                    last = chunkwise(0, lambda *m: g_UT[:, *m, :], lambda *m: g_T[:, *m, :])
                elif s[:3] == "sub":
                    if s != f"sub{LEVELS - 1}":
                        chunkwise(1, lambda *m: g_TT[:, *m, :], lambda *m: g_Z[:, *m, :])
                    last = chunkwise(2, lambda *m: g_Z[:, *m, :], lambda *m: g_TT[:, *m, :])
                elif s == "uw":
                    for n, (d, h, t) in enumerate(DHT):
                        for r in range(2):
                            rows = slice(CH * r, CH * r + CH)
                            mm(mix(d, 2 * h + t)[rows], g_TT[rows, d, h, t, :], g_XV[rows, d, h, t, :], **single)
                    for n, (d, h, t) in enumerate(DHT):
                        for r in range(2):
                            rows = slice(CH * r, CH * r + CH)
                            last = mm(bank(MIX + 2 + r)[:, CH * n:CH * n + CH], g_XK[rows, d, h, t, :],
                                      g_TT[rows, d, h, t, :], **single)
                elif s[0] == "s":
                    for d in range(2):
                        tile, r = chunk_of(d, int(s[1]))
                        for h in range(2):
                            last = mm(mix(2 * d, h), g_KS[64 * r:64 * r + 64, d, h, tile, :],
                                      g_U[64 * r:64 * r + 64, d, h, tile, :], **single)
                elif s[0] == "v":
                    step = int(s[1])
                    for d in range(2):
                        tile, r = chunk_of(d, step)
                        for h in range(2):
                            last = mm(mix(1, h)[64 * r:64 * r + 64, :], g_WT[:, r, d, h, tile, :],
                                      g_S[:, h, d, step - 1, :], **single)
                elif s == "out":
                    for t in range(2):
                        for h in range(2):
                            o = mix(2 * t, h)
                            for d in range(2):
                                for r in range(2):
                                    rows = slice(CH * r, CH * r + CH)
                                    mm(o[rows], g_AT[rows, d, h, t, :], g_U[rows, d, h, t, :], start=(d == 0), stop=False,
                                       skip_group_check=True)
                            for d in range(2):
                                for r in range(2):
                                    step = 2 * t + r if d == 0 else 3 - 2 * t - r
                                    if step:
                                        last = mm(o[64 * r:64 * r + 64, :], g_EG[:, d, h, t, 64 * r:64 * r + 64],
                                                  g_S[:, h, d, step - 1, :], start=False, stop=True, skip_group_check=True)
                elif s == "turn":
                    for t in range(2):
                        for h in range(2):
                            last = turn(mix(0, 2 * h + t), g_o[:, t, h, :], ident)
                last.then_inc(gdn_sem["pe"], 1)

            def att_stage(a, s):
                if (a, s) == (0, "score"):
                    for e in ("dve", "act", "pool"):
                        pe.wait_ge(gdn_sem[e], gdn_count.total[("dve", "act", "pool").index(e)])
                    pe.wait_ge(block_out, 14)
                if s == "score" and a:
                    pe.wait_ge(att_sem["dve"], att_count.value("dve", (a - 1, s), 2))
                elif s == "pT":
                    pe.wait_ge(att_sem["dve"], att_count.value("dve", (a, "score"), 10))
                    if a:
                        pe.wait_ge(att_sem["act"], att_count.value("act", (a - 1, s), 1))
                elif s == "pv":
                    pe.wait_ge(att_sem["act"], att_count.value("act", (a, "pT"), 1))
                    if a:
                        pe.wait_ge(att_sem["dve"], att_count.value("dve", (a - 1, s), 1))
                elif a == HEADS:
                    wait_part(pe, att_sem, att_count, "pe", (a, s))
                if s == "score":
                    for t in range(TT):
                        for m in range(2):
                            rows = slice(DH * m, DH * m + DH)
                            last = mm(bank(MIX + 2 + m)[:, T * t:T * t + T], aq[rows, a, t * P:(t + 1) * P], ak[rows, a, :],
                                      start=True, stop=True)
                elif s == "pT":
                    for k in range(2):
                        for t in range(TT):
                            last = turn(mix(0, 2 * k + t), a_p[:, t, k * P:(k + 1) * P], ident)
                elif s == "pv":
                    for t in range(TT):
                        for k in range(2):
                            last = mm(mix(1, t), a_pT[:, k, t, :], av[:, k, a * P:(a + 1) * P], start=(k == 0), stop=(k == 1))
                elif s == "norm":
                    last = turn(mix(0), ident, ident)
                elif s == "turn":
                    for h in range(HEADS):
                        for t in range(TT):
                            last = turn(bank(MIX + h // 2)[:, (h % 2) * T + t * P:(h % 2) * T + t * P + P],
                                        a_od[:, t, h, :], ident)
                last.then_inc(att_sem["pe"], 1)

            for what, i, s in ORDER:
                if what == "pair":
                    pair(i, s)
                    if (i, s) == (0, KC // 2 - 1):
                        decay_and_beta()
                    if (i, s) == (1, KC // 2 - 1):
                        decay_sums()
                elif what == "gdn":
                    gdn_stage(i, s)
                elif what == "att":
                    att_stage(i, s)

            for k in range(4):
                b0 = 4 * (k % 2)
                if k == 0:
                    pe.wait_ge(block_out, len(BLOCKS))
                    pe.wait_ge(att_sem["act"], att_count.total[1])
                if k >= 2:
                    pe.wait_ge(merge_dve, 4 * (k - 1))
                for br in range(2):
                    for c in range(HEADS):
                        if k == 0:
                            pe.wait_ge(y_split_l, 2 * br + c // 4 + 1)
                        by_channel(M0 + (2 * k + br) * HEADS + c, b0 + 2 * br, [y[:, c, :] for y in y_part[br]],
                                   c == 0, c == HEADS - 1)
            pe.wait_ge(merge_dve, 16)
            for k in range(4):
                if k >= 2:
                    pe.wait_ge(out_dve, 2 * (k - 1))
                for c in range(KC):
                    if k == 0:
                        pe.wait_ge(m_split_l, c // 4 + 1)
                    by_token(O0 + KC * k + c, 2 * (k % 2), [h[:, c, :] for h in h_part], c == 0, c == KC - 1)
            pe.wait_ge(out_dve, 8)
            for t in range(TT):
                pe.wait_ge(route_dve, H2_READY[t])
                for c in range(KC):
                    o = bank(c // 2)[:, (c % 2) * T + t * P:(c % 2) * T + t * P + P]
                    mm(o, h2_part[0][:, t, c, :], ident_r, start=True, stop=False)
                    last = mm(o, h2_part[1][:, t, c, :], ident_r, start=False, stop=True)
            last.then_inc(route_pe, 1)
            pe.wait_ge(route_in, 64)
            pe.wait_ge(route_dve, H2T_READY)
            for t in range(TT):
                for c in range(KC):
                    last = mm(bank(0)[:, 36 * t:36 * t + 36], h2T[:, c, t * P:(t + 1) * P], w_route[:, c, :],
                              start=(c == 0), stop=(c == KC - 1))
            last.then_inc(route_pe, 1)
            pe.wait_ge(route_dve, MASK_READY)
            mm(bank(1)[:, 0:NE], before, m_mask[:, 0, :], start=True, stop=True)
            mm(bank(1)[:, NE:2 * NE], before, m_mask[:, 1, :], start=True, stop=False)
            mm(bank(1)[:, NE:2 * NE], ones, m_mask[:, 0, :], start=False, stop=True)
            mm(bank(1)[:, 2 * NE:3 * NE], ones, m_mask[:, 0, :], start=True, stop=False)
            mm(bank(1)[:, 2 * NE:3 * NE], ones, m_mask[:, 1, :], start=False, stop=True).then_inc(route_pe, 1)

            def turn_weights(n):
                pe.wait_ge(pick_ready, 4 * n + 4)
                pe.wait_ge(hid_ready, 2 * n + 3)
                for t in range(TT):
                    last = turn(bank(4)[:, t * P:(t + 1) * P], pick_w[:, t].rearrange("p a b -> p (a b)"), ident)
                last.then_inc(ws_turned, 1)

            def gather(n, groups, sums=None):
                pe.wait_ge(pick_ready, 4 * n + 2)
                for k in groups:
                    pe.wait_ge(gather_read, 4 * n + k + 1)
                    if k == 0 and sums is not None:
                        pe.wait_ge(added, sums + 2)
                    for c in range(4 * k, 4 * k + 4):
                        for i, (t, h2) in enumerate((t, h2) for t in range(TT) for h2 in h2_part):
                            last = mm(bank(k % 2)[:, (c % 4) * P:(c % 4 + 1) * P], h2[:, t, c, :],
                                      pick[:, t].rearrange("p a b -> p (a b)"), start=(i == 0), stop=(i == 2 * TT - 1))
                    last.then_inc(gathered, 1)

            def gate_or_up(X, e, m):
                pe.wait_ge(gu_copied, 2 * X + 1)
                for u in range(2):
                    pe.wait_ge(full[2 * m + u], 16 * X + 16)
                    for c in range(8):
                        g = c % 2
                        last = mm(bank(2 + m)[64 * g:64 * g + 64, :],
                                  xe[:, 8 * u + c, SLOTS * e:SLOTS * e + SLOTS],
                                  expert_unit(2 * m + u, 8, FE)[:, c, :],
                                  start=(u == 0 and c < 2), stop=(u == 1 and c >= 6))
                    last.then_inc(unit_free[m], 1)

            def turn_part(X, m):
                pe.wait_ge(gu_copied, 2 * X + 2 + m)
                for f in range(4):
                    last = mm(bank(4)[:, (4 * m + f) * SLOTS:(4 * m + f + 1) * SLOTS],
                              (g_part, u_part)[m][:, f * P:(f + 1) * P], twice, start=True, stop=True)
                if m:
                    last.then_inc(gu_turned, 1)

            def down(X):
                pe.wait_ge(hid_ready, X + 2)
                pe.wait_ge(y_copied, 4 * X + 1)
                for u in range(2):
                    pe.wait_ge(full[4 + u], 16 * X + 16)
                    for f in range(2):
                        for j in range(4):
                            g = j % 2
                            last = mm(bank(5 + j // 2)[64 * g:64 * g + 64, :], hid[:, 2 * u + f, :],
                                      expert_unit(4 + u, 2, D)[:, f, 512 * j:512 * j + 512],
                                      start=(u == 0 and f == 0), stop=(u == 1 and f == 1))
                    last.then_inc(unit_free[2], 1)

            def scatter(n, t):
                pe.wait_ge(y_copied, 8 * n + 9)
                pe.wait_ge(ws_ready, n + 1)
                for j in range(4):
                    q = 4 * t + j
                    pe.wait_ge(added, 8 * n + q + 1)
                    mm(bank(0 if q % 2 else 7), ws[:, t * P:(t + 1) * P], y_sb[:, j, :],
                       start=True, stop=True).then_inc(scatter_done, 1)

            def pair_in_pipeline(n, first=False, last=False):
                a, b = 2 * n, 2 * n + 1
                pe.wait_ge(gather_read, 4 * n + 6)
                gate_or_up(a, 0, 0)
                if not first:
                    scatter(n - 1, 0)
                gate_or_up(a, 0, 1)
                pe.wait_ge(hid_ready, a + 1)
                turn_part(a, 0)
                if not first:
                    scatter(n - 1, 1)
                turn_part(a, 1)
                gate_or_up(b, 1, 0)
                down(a)
                gate_or_up(b, 1, 1)
                turn_part(b, 0)
                if not last:
                    gather(n + 1, (0, 1), sums=8 * n)
                turn_part(b, 1)
                if not last:
                    gather(n + 1, (2, 3))
                down(b)
                turn_weights(n)

            def pair_alone(n):
                gather(n, range(4), sums=8 * n)
                pe.wait_ge(gather_read, 4 * n + 6)
                for e in range(2):
                    gate_or_up(2 * n + e, e, 0)
                    gate_or_up(2 * n + e, e, 1)
                    pe.wait_ge(hid_ready, 2 * n + e + 1)
                    turn_part(2 * n + e, 0)
                    turn_part(2 * n + e, 1)
                    down(2 * n + e)
                turn_weights(n)
                scatter(n, 0)
                scatter(n, 1)

            pe.sem_inc(gathered, 1)
            pe.sem_inc(scatter_done, 1)
            PAIRS = NE // 2
            gather(0, range(4))
            pair_in_pipeline(0, first=True)
            with pe.Fori(1, PAIRS - 1) as n:
                pair_in_pipeline(n)
            pair_in_pipeline(PAIRS - 1, last=True)
            scatter(PAIRS - 1, 0)
            scatter(PAIRS - 1, 1)
            pe.wait_ge(route_dve, ROUTE_FLAG)
            with pe.If(pe.value_load(over_i[0:1, 0:1], min_val=0, max_val=1) > 0):
                with pe.Fori(PAIRS, ROUNDS * PAIRS) as n:
                    pair_alone(n)

        @block.scalar
        def _(act):
            act_ = nc.scalar.activation
            line = Line(act, set_act)
            for dst, src in ((gmix_c.rearrange("p (u c) -> p u c", u=2), g_mix[0].rearrange("(u p c) -> p u c", u=2, c=8)),
                             (gffn_c.rearrange("p (u c) -> p u c", u=2), g_ffn[0].rearrange("(u p c) -> p u c", u=2, c=8)),
                             (conv_rows[0:120, :], conv_w[0].rearrange("k (t p) -> (k t) p", p=P)),
                             (dtb, dt_bias[0].rearrange("a b -> (a b)").partition_broadcast(P)),
                             (alog, a_log[0].rearrange("a b -> (a b)").partition_broadcast(P)),
                             (gdn_w, gdn_norm_w[0].partition_broadcast(P)),
                             (diff_w, diff_norm_w[0].partition_broadcast(P)),
                             (lam_in.rearrange("p a b -> p (a b)"), diff_lambda[0].rearrange("a b -> (a b)").partition_broadcast(P)),
                             (bias_r[:, 0:NG], b_group[0].partition_broadcast(P)),
                             (bias_r[:, NG:NG + NE], b_router[0].partition_broadcast(P))):
                act.dma_start(dst, src).then_inc(small_in, 16)
            for u in range(2):
                act.dma_start(w_ab[:, 8 * u:8 * u + 8, :], wi[u, :, :, OFF_AB:OFF_AB + 32]).then_inc(wab_in, 16)
            act.wait_ge(x_in, 32)
            for t in range(TT):
                line(act_(xn[:, t].rearrange("p c q -> p (c q)"), x_sb[:, t, :], ACT.Square, accum_out=ss[:, t:t + 1]))
            act.wait_ge(set_dve, 2)
            line(act_(rstd, ss, ACT.Sqrt, bias=eps_c[:, 0:1], scale=1.0 / D))
            act.wait_ge(set_dve, 3)
            for t in range(TT):
                for u in range(2):
                    line(act_(xn[:, t, 8 * u:8 * u + 8, :], x_sb[:, t, 1024 * u:1024 * u + 1024].rearrange("p (q c) -> p c q", c=8),
                              ACT.Copy, scale=rstd[:, t:t + 1]))
            for k in range(8):
                act.wait_ge(set_dve, 4 + k)
                line(act_(h_part[0][:, 2 * k:2 * k + 2, :], hT[:, 2 * k:2 * k + 2, :], ACT.Copy))
            act.wait_ge(wab_in, 32)
            line(act_(ab_part[0], w_ab, ACT.Copy))
            assert line.n == PARTS_ACT

            def softplus():
                act.wait_ge(set_dve, AB_X)
                line(act_(ab_u, ab_u, ACT.Exp, scale=-1.0))
                line(act_(alog, alog, ACT.Exp))
                line(act_(lam_s, lam_s, ACT.Exp))
                line(act_(ab_u, ab_u, ACT.Ln, bias=one_c[:, 0:1]))
                line(act_(beta, bank(5)[:, 0:64].rearrange("p (t n) -> p t n", t=2)[:, :, 16:32], ACT.Sigmoid))
                assert line.n == SET_ACT

            def decay_exp():
                act.wait_ge(set_dve, GC_READY)
                line(act_(esfx, esfx, ACT.Exp))
                line(act_(begc, gc, ACT.Exp))

            fed = [0]

            def feed(upto):
                while fed[0] < min(upto, CHUNKS):
                    m = fed[0]
                    if m % 4 == 0:
                        act.wait_ge(unit_in[m // 4 % 3], 16 * (m // 12 + 1))
                    if m >= STAGES:
                        act.wait_ge(chunk_used, m - STAGES + 1)
                    act_(w_part[m % STAGES][0], unit(m // 4)[:, m % 4, :], ACT.Copy).then_inc(split_h, 1)
                    fed[0] += 1

            gdn_line = Line(act, gdn_sem["act"])
            att_line = Line(act, att_sem["act"])
            banks_m = banks[:, MIX:MIX + 4, :]
            m01 = banks[:, MIX:MIX + 2, :]
            m23 = banks[:, MIX + 2:MIX + 4, :]

            def flat(ap):
                return ap.rearrange("p a b c d -> p (a b c d)").rearrange("p (x n) -> p x n", n=512)

            def block_end(b):
                kind, _, i = BLOCKS[b]
                src = banks[:, PROJ + 2 * (b % 2):PROJ + 2 * (b % 2) + 2, :]
                if kind in CONV:
                    act.wait_ge(conv_read, 20 * conv_blocks(b))
                    y = {"q": qT, "k": kT, "v": vT}[kind]
                    ins = act_(y, y, ACT.Silu)
                else:
                    act.wait_ge(chunk_used, KC * (b + 1))
                    if kind == "ga" and i == 0:
                        act.wait_ge(gdn_sem["pe"], gdn_count.value("pe", (GDN_BATCHES - 1, "first")))
                        act.wait_ge(gdn_sem["pool"], gdn_count.value("pool", (GDN_BATCHES - 1, "lt3")))
                    if kind == "ga" and i == 2:
                        for e in ("dve", "pool", "pe"):
                            act.wait_ge(gdn_sem[e], gdn_count.total[("dve", "act", "pool", "pe").index(e)])
                    if kind == "z":
                        ins = act_(zs[:, :, NB * i:NB * i + NB], src, ACT.Silu)
                    elif kind == "av":
                        ins = act_(av[:, :, NB * i:NB * i + NB], src, ACT.Copy)
                    elif kind in ("aq", "ak"):
                        y = (aq if kind == "aq" else ak)[:, 4 * i:4 * i + 4, :].rearrange("p a n -> p (a n)")
                        ins = act_(y.rearrange("p (x n) -> p x n", n=512), src, ACT.Copy)
                    else:
                        y = gate(kind == "gd", i)
                        ins = act_(y.rearrange("p (x n) -> p x n", n=512), src, ACT.Sigmoid)
                ins.then_inc(block_out, 1)

            def gdn_stage(b, s):
                act.wait_ge(gdn_sem["pe"], gdn_count.value("pe", (b, s), 1))
                if s == "norm":
                    gdn_line(act_(rn, bank(MIX + 2)[:, 0:8], ACT.Sqrt, bias=eps_c[:, 0:1]))
                    gdn_line(act_(g_v.rearrange("p a b c -> p (a b c)"), bank(MIX + 1), ACT.Copy))
                elif s == "decay":
                    gdn_line(act_(g_kT.rearrange("p a b -> p (a b)"), bank(MIX), ACT.Copy))
                    gdn_line(act_(flat(g_EG), m23, ACT.Exp))
                    act.wait_ge(gdn_sem["dve"], gdn_count.value("dve", (b, s), 2))
                    gdn_line(act_(g_E.rearrange("p a b c d -> p (a b c d)"), g_E.rearrange("p a b c d -> p (a b c d)"), ACT.Exp))
                elif s == "first":
                    gdn_line(act_(g_T.rearrange("p a b c d -> p (a b c d)"), bank(MIX + 2), ACT.Copy))
                elif s[:2] == "lt":
                    gdn_line(act_(g_Z.rearrange("p a b c d -> p (a b c d)"), bank(MIX), ACT.Copy))
                elif s == "uw":
                    gdn_line(act_(g_WT.rearrange("p r a b c d -> p r (a b c d)"), m23, ACT.Copy))
                elif s == "out":
                    act.wait_ge(gdn_sem["dve"], gdn_count.value("dve", (b, s), 4))
                    gdn_line(act_(o_r, o_ss, ACT.Sqrt, bias=eps_c[:, 0:1], scale=1.0 / DK))
                elif s == "turn":
                    gdn_line(act_(ya[:, 2 * b:2 * b + 2, :].rearrange("p a b -> p (a b)"), bank(MIX), ACT.Copy))

            def att_stage(a, s):
                act.wait_ge(att_sem["pe"], att_count.value("pe", (a, s), 1))
                if s == "score":
                    act.wait_ge(att_sem["dve"], att_count.value("dve", (a, s), 4))
                    for t in range(TT):
                        for m in range(2):
                            i = 2 * t + m
                            att_line(act_(a_s[:, t, m, :], a_s[:, t, m, :], ACT.Exp, bias=nmx[:, i:i + 1],
                                          scale=DH ** -0.5, accum_out=sums[:, i:i + 1]))
                elif s == "pT":
                    att_line(act_(a_pT.rearrange("p a b c -> p (a b c)"), bank(MIX), ACT.Copy))
                elif s == "norm":
                    act.wait_ge(att_sem["dve"], att_count.value("dve", (a, s), 2))
                    att_line(act_(od_r, od_ss, ACT.Sqrt, bias=eps_c[:, 0:1], scale=1.0 / P))
                elif s == "turn":
                    att_line(act_(yd.rearrange("p a b -> p (a b)").rearrange("p (x n) -> p x n", n=512), banks_m, ACT.Copy))

            feed(LEAD)
            for what, i, s in ORDER:
                if what == "pair":
                    feed(KC * i + 2 * s + 2 + LEAD)
                elif what == "conv" and s == TAPS or what == "end" and BLOCKS[i][0] not in CONV:
                    block_end(i)
                elif what == "end" and i < 2:
                    (softplus, decay_exp)[i]()
                elif what == "gdn":
                    gdn_stage(i, s)
                elif what == "att":
                    att_stage(i, s)

            act.wait_ge(chunk_used, M0)
            for br, y in enumerate((ya, yd)):
                for i in range(2):
                    act_(y_part[br][0][:, 4 * i:4 * i + 4, :], y[:, 4 * i:4 * i + 4, :], ACT.Copy).then_inc(y_split_h, 1)
            feed(O0 + LEAD)
            act.wait_ge(chunk_used, O0)
            for k in range(4):
                act.wait_ge(merge_pool, k + 1)
                act_(h_part[0][:, 4 * k:4 * k + 4, :], gate(0, k).rearrange("p (a n) -> p a n", n=T), ACT.Copy).then_inc(m_split_h, 1)
            feed(CHUNKS)

            rline = Line(act, route_act)
            act.wait_ge(out_dve, 8)
            for t in range(TT):
                rline(act_(h2T.rearrange("p c n -> p (c n)")[:, 0:D], x_sb[:, t, :], ACT.Square, accum_out=ss[:, t:t + 1]))
            rline(act_(rstd, ss, ACT.Sqrt, bias=eps_c[:, 0:1], scale=1.0 / D))
            act.wait_ge(route_dve, 1)
            for t in range(TT):
                for u in range(2):
                    rline(act_(h2_part[0][:, t, 8 * u:8 * u + 8, :], x_sb[:, t, 1024 * u:1024 * u + 1024].rearrange("p (q c) -> p c q", c=8),
                               ACT.Copy, scale=rstd[:, t:t + 1]))
            act.wait_ge(route_dve, GROUP_MAX)
            rline(act_(rt[:, 0, :, 0:NG], rt[:, 0, :, 0:NG], ACT.Exp))
            act.wait_ge(route_dve, TOP_TWO)
            rline(act_(rs1[:, 7, :], rs1[:, 7, :], ACT.Exp))
            assert rline.n == ROUTE_ACT

            def copy_part(X, m):
                act.wait_ge(unit_free[m], 2 * X + 2)
                act_((g_part, u_part)[m], bank(2 + m), ACT.Copy).then_inc(gu_copied, 1)

            def silu(X):
                act.wait_ge(gu_turned, X + 1)
                act_(silu_g.rearrange("p a b -> p (a b)"), bank(4)[:, 0:T], ACT.Silu).then_inc(silu_done, 1)

            def copy_y(X, e):
                act.wait_ge(unit_free[2], 2 * X + 2)
                for j in range(4):
                    g = j % 2
                    act_(y_sb[64 * e:64 * e + 64, j, :], bank(5 + j // 2)[64 * g:64 * g + 64, :],
                         ACT.Copy).then_inc(y_copied, 1)

            def copy_weights(n):
                act.wait_ge(ws_turned, n + 1)
                act_(ws, bank(4)[:, 0:T], ACT.Copy).then_inc(ws_ready, 1)

            def pair_in_pipeline(n):
                a, b = 2 * n, 2 * n + 1
                copy_part(a, 0)
                copy_part(a, 1)
                silu(a)
                copy_part(b, 0)
                act.wait_ge(scatter_done, 8 * n + 1)
                copy_y(a, 0)
                copy_part(b, 1)
                silu(b)
                copy_y(b, 1)
                copy_weights(n)

            def pair_alone(n):
                act.wait_ge(scatter_done, 8 * n + 1)
                for e in range(2):
                    copy_part(2 * n + e, 0)
                    copy_part(2 * n + e, 1)
                    silu(2 * n + e)
                    copy_y(2 * n + e, e)
                copy_weights(n)

            act.sem_inc(gu_copied, 1)
            act.sem_inc(y_copied, 1)
            with act.Fori(0, NE // 2) as n:
                pair_in_pipeline(n)
            act.wait_ge(route_dve, ROUTE_FLAG)
            with act.If(act.value_load(over_i[0:1, 0:1], min_val=0, max_val=1) > 0):
                with act.Fori(NE // 2, ROUNDS * NE // 2) as n:
                    pair_alone(n)
            act.wait_ge(fin_dve, 2)
            act_(fin_ss, fin_ss, ACT.Sqrt, bias=eps_c[:, 0:1], scale=1.0 / D).then_inc(fin_act, 1)

        @block.gpsimd
        def _(pool):
            tt_ = nc.gpsimd.tensor_tensor
            gdn_line = Line(pool, gdn_sem["pool"])
            att_line = Line(pool, att_sem["pool"])

            def gdn_stage(b, s):
                here = slice(2 * (b % 2), 2 * (b % 2) + 2)
                if s == "norm":
                    pool.wait_ge(block_out, QKV_THERE[b // 2])
                    for e in ("dve", "act", "pe"):
                        if gdn_count.value(e, (b, s)):
                            pool.wait_ge(gdn_sem[e], gdn_count.value(e, (b, s)))
                    for i, m in enumerate((qT, kT)):
                        gdn_line(tt_(g_sq[:, i], m[:, here, :], m[:, here, :], ALU.mult))
                    return
                if not GDN[s][2]:
                    return
                pool.wait_ge(gdn_sem["pe"], gdn_count.value("pe", (b, s), 1))
                if s == "decay":
                    pool.wait_ge(gdn_sem["act"], gdn_count.value("act", (b, s), 3))
                    gdn_line(tt_(by_pair(g_E), by_pair(g_E), tri64.unsqueeze(2).broadcast_to([P, 2, 4, CH]), ALU.mult))
                elif s == "gram":
                    pool.wait_ge(gdn_sem["dve"], gdn_count.value("dve", (b, s), 3))
                    mask_level(b, 0)
                    gdn_line(tt_(g_TT.rearrange("p a b c d -> p (a b c) d"), twice.unsqueeze(1).broadcast_to([P, 8, CH]),
                                 g_UT.rearrange("p a b c d -> p (a b c) d"), ALU.subtract))
                elif s == "first":
                    mask_level(b, 1)
                elif s == "lt1":
                    es = esfx[:, :, 2 * b:2 * b + 2, :].rearrange("p d h t -> p d (h t)")
                    gdn_line(tt_(by_pair(g_KS), g_k.rearrange("p h t n -> p (h t) n").unsqueeze(1).broadcast_to([P, 2, 4, P]),
                                 es.unsqueeze(3).broadcast_to([P, 2, 4, P]), ALU.mult))
                elif s == "lt2":
                    eg_ = g_EG.rearrange("p d h t n -> p d (h t n)")
                    qh = qT[:, here, :].rearrange("p h n -> p (h n)")
                    gdn_line(tt_(eg_, eg_, qh.unsqueeze(1).broadcast_to([P, 2, 2 * T]), ALU.mult))
                elif s[:3] == "sub":
                    mask_level(b, int(s[3:]) + 1)
                elif s == "out":
                    pool.wait_ge(gdn_sem["dve"], gdn_count.value("dve", (b, s), 6))
                    o4 = g_o.rearrange("p t h n -> p (t h) n")
                    gdn_line(tt_(o4, o4, gdn_w.unsqueeze(1).broadcast_to([P, 4, P]), ALU.mult))
                    pool.wait_ge(block_out, Z_THERE[b // 2])
                    o2 = g_o.rearrange("p t h n -> p t (h n)")
                    gdn_line(tt_(o2, o2, zs[:, :, 2 * b * P:(2 * b + 2) * P], ALU.mult))

            def by_pair(ap):
                return ap.rearrange("p d h t n -> p d (h t) n")

            def mask_level(b, lv):
                gdn_line(tt_(by_pair(g_UT), by_pair(g_LT), level[:, lv].unsqueeze(2).broadcast_to([P, 2, 4, CH]), ALU.mult))

            def att_stage(a, s):
                if a == HEADS and s == "norm":
                    pool.wait_ge(att_sem["dve"], att_count.value("dve", (a, s), 4))
                    o = a_od.rearrange("p t h n -> p (t h) n")
                    att_line(tt_(o, o, diff_w.unsqueeze(1).broadcast_to([P, TT * HEADS, P]), ALU.mult))

            pool.wait_ge(set_dve, COLS_READY)
            for what, i, s in ORDER:
                if what == "gdn":
                    gdn_stage(i, s)
                elif what == "att":
                    att_stage(i, s)
            for k in range(4):
                pool.wait_ge(merge_dve, 4 * k + 4)
                tt_(gate(0, k), gate(0, k), gate(1, k), ALU.add).then_inc(merge_pool, 1)

        @block.vector
        def _(dve):
            V = nc.vector
            tt_, ts_, stt_ = V.tensor_tensor, V.tensor_scalar, V.scalar_tensor_tensor
            line = Line(dve, set_dve)
            line(V.memset(one_c, 1.0))
            line(V.memset(eps_c, EPS))
            dve.wait_ge(set_act, 3)
            line(V.reciprocal(rstd, rstd))
            dve.wait_ge(set_pe, 1)
            dve.wait_ge(small_in, SMALL_ALL)
            for k in range(8):
                line(tt_(hT[:, 2 * k:2 * k + 2, :], bank(k).rearrange("p (c n) -> p c n", c=2),
                         spread(gmix_c[:, 2 * k:2 * k + 2], 2, T), ALU.mult))
            assert line.n == HT_READY
            fed = [0]

            def feed(upto):
                while fed[0] < min(upto, CHUNKS):
                    m = fed[0]
                    high, low = w_part[m % STAGES]
                    dve.wait_ge(split_h, m + 1)
                    tt_(low, unit(m // 4)[:, m % 4, :], high.bitcast(F32), ALU.subtract).then_inc(split_l, 1)
                    fed[0] += 1

            for k in range(8):
                dve.wait_ge(set_act, 8 + k)
                j = slice(2 * k, 2 * k + 2)
                line(tt_(h_part[1][:, j, :], hT[:, j, :], h_part[0][:, j, :].bitcast(F32), ALU.subtract))
                if k < LEAD:
                    feed(k + 1)
            dve.wait_ge(set_act, PARTS_ACT)
            line(tt_(ab_part[1], w_ab, ab_part[0].bitcast(F32), ALU.subtract))
            assert line.n == AB_PARTS
            dve.wait_ge(set_pe, 2)
            line(V.tensor_copy(conv_c, bank(4)[:, 0:120]))
            line(tt_(lam_p, lam_in[:, 0:4:2, :], lam_in[:, 1:4:2, :], ALU.mult))
            line(V.tensor_reduce(lam_s, lam_p, AX.X, ALU.add))
            line(ts_(diff_w, diff_w, 1.0 - LAM_INIT, None, ALU.mult))
            def by_head(v):
                return v.rearrange("p d h t -> p t d h")

            def log_decay():
                dve.wait_ge(set_pe, 3)
                ab_ps = bank(5)[:, 0:64].rearrange("p (t n) -> p t n", t=2)
                line(tt_(ab_x, ab_ps[:, :, 0:16], dtb.unsqueeze(1).broadcast_to([P, TT, 16]), ALU.add))
                line(stt_(ab_u, ab_x, -1.0, ab_x, ALU.mult, ALU.max))
                line(ts_(ab_x, ab_x, 0.0, None, ALU.max))
                assert line.n == AB_X
                dve.wait_ge(set_act, SET_ACT - 1)
                line(tt_(ab_x, ab_x, ab_u, ALU.add))
                line(stt_(g_log, ab_x, -1.0, alog.unsqueeze(1).broadcast_to([P, TT, 16]), ALU.mult, ALU.mult))
                assert line.n == G_READY
                line(tt_(nlam, lam_s[:, 1:2], lam_s[:, 0:1], ALU.subtract))
                line(ts_(nlam, nlam, LAM_INIT, None, ALU.subtract))
                dve.wait_ge(set_act, SET_ACT)

                line(V.tensor_copy(by_head(bcol), beta.rearrange("p t (d h) -> p t d h", d=2)))

            def decay_columns():
                dve.wait_ge(set_pe, 4)
                for v, k in ((gc, 0), (esfx, 2)):
                    for d in range(2):
                        src = bank(6)[:, (k + d) * 16:(k + d) * 16 + 16].rearrange("p (t h) -> p t h", t=2)
                        line(V.tensor_copy(v[:, d].rearrange("p h t -> p t h"), src))
                assert line.n == GC_READY
                dve.wait_ge(set_act, SET_ACT + 2)
                line(tt_(begc, begc, bcol, ALU.mult))
                assert line.n == COLS_READY

            convs = [0]

            def conv(b, k):
                kind, col, _ = BLOCKS[b]
                y = {"q": qT, "k": kT, "v": vT}[kind]
                if k == 0:
                    dve.wait_ge(chunk_used, KC * (b + 1))
                    if conv_blocks(b) == 4:
                        dve.wait_ge(gdn_sem["pe"], gdn_count.value("pe", (1, "first")))
                        dve.wait_ge(gdn_sem["pool"], gdn_count.value("pool", (1, "lt3")))
                tap = (2, 0, 1, 3, 4)[k]
                o = tap - 2
                lo, hi = max(0, -o), T - max(0, o)
                for j in range(4):
                    src = bank(PROJ + 2 * (b % 2) + j // 2)[:, (j % 2) * T:(j % 2 + 1) * T]
                    ct = (col // P) + j
                    w = conv_c[:, tap * 24 + ct:tap * 24 + ct + 1]
                    if k == 0:
                        ins = ts_(y[:, j, :], src, w, None, ALU.mult)
                    else:
                        dve.wait_ge(conv_read, convs[0] - 3)
                        ins = stt_(y[:, j, lo:hi], src[:, lo + o:hi + o], w, y[:, j, lo:hi], ALU.mult, ALU.add)
                    ins.then_inc(conv_read, 1)
                    convs[0] += 1

            gdn_line = Line(dve, gdn_sem["dve"])
            att_line = Line(dve, att_sem["dve"])
            m01 = banks[:, MIX:MIX + 2, :]
            m23 = banks[:, MIX + 2:MIX + 4, :]

            def eight(ap):
                return ap.rearrange("p a b c d -> p (a b c) d")

            def by_pair(ap):
                return ap.rearrange("p d h t n -> p d (h t) n")

            def mats(i):
                return bank(MIX + i).rearrange("p (m n) -> p m n", n=CH)

            def gdn_stage(b, s):
                if not GDN[s][0]:
                    return
                heads = (2 * b, 2 * b + 1)
                hs = slice(2 * b, 2 * b + 2)
                dve.wait_ge(gdn_sem["pe"], gdn_count.value("pe", (b, s), 1))
                if s == "norm":
                    dve.wait_ge(gdn_sem["act"], gdn_count.value("act", (b, s), 1))
                    gdn_line(V.reciprocal(rr, rn))
                    gdn_line(tt_(g_k.rearrange("p h t n -> p (h t) n"), bank(MIX).rearrange("p (a n) -> p a n", n=P),
                                 spread(rr[:, 4:8], 4, P), ALU.mult))
                    gdn_line(ts_(rr[:, 0:4], rr[:, 0:4], DK ** -0.5, None, ALU.mult))
                elif s == "decay":
                    gcol = gc[:, :, hs].rearrange("p d h t -> p d (h t)").unsqueeze(3).broadcast_to([P, 2, 4, CH])
                    gdn_line(tt_(by_pair(g_E), bank(MIX + 1).rearrange("p (d m n) -> p d m n", d=2, n=CH), gcol, ALU.subtract))
                    gdn_line(ts_(eight(g_E), eight(g_E), 0.0, None, ALU.min))
                    dve.wait_ge(gdn_sem["act"], gdn_count.value("act", (b, s), 2))
                    for d in range(2):
                        off = CH - 1 if d == 0 else 0
                        gdn_line(V.tensor_copy(glast[:, :, d], g_EG[:, d, :, :, off:P:CH]))
                elif s == "gram":
                    dve.wait_ge(gdn_sem["pool"], gdn_count.value("pool", (b, s)))
                    e2, at2, lt2 = (m.rearrange("p d h t n -> p d (h t n)") for m in (g_E, g_AT, g_LT))
                    kk, kq = (bank(MIX + i)[:, 0:4 * CH].unsqueeze(1).broadcast_to([P, 2, 4 * CH]) for i in range(2))
                    gdn_line(tt_(at2, kq, e2, ALU.mult))
                    gdn_line(tt_(eight(g_E), mats(2), eight(g_E), ALU.mult))
                    gdn_line(tt_(lt2, kk, e2, ALU.mult))
                elif s in ("lt1", "lt2"):
                    dst, src, cols = ((g_XV, g_v, bcol), (g_XK, g_k, begc))[s == "lt2"]
                    c = cols[:, :, hs].rearrange("p d h t -> p d (h t)").unsqueeze(3).broadcast_to([P, 2, 4, P])
                    gdn_line(tt_(by_pair(dst), src.rearrange("p h t n -> p (h t) n").unsqueeze(1).broadcast_to([P, 2, 4, P]),
                                 c, ALU.mult))
                elif s[:3] == "sub":
                    gdn_line(tt_(eight(g_TT), eight(g_TT), mats(2), ALU.subtract))
                    if s != f"sub{LEVELS - 1}":
                        gdn_line(tt_(eight(g_T), eight(g_T), mats(1), ALU.subtract))
                elif s == "uw":
                    gdn_line(V.tensor_copy(eight(g_U), m01.rearrange("p b (m n) -> p (b m) n", n=P)))
                elif s[0] == "s":
                    step = int(s[1])
                    for d in range(2):
                        tile, r = chunk_of(d, step)
                        new = bank(MIX + 2 * d)[:, 0:256].rearrange("p (h n) -> p h n", h=2)
                        if step == 0:
                            gdn_line(V.tensor_copy(g_S[:, :, d, 0, :], new))
                        else:
                            for h in range(2):
                                gdn_line(stt_(g_S[:, h, d, step, :], g_S[:, h, d, step - 1, :],
                                              glast[:, h, d, tile, r:r + 1], new[:, h, :], ALU.mult, ALU.add))
                elif s[0] == "v":
                    for d in range(2):
                        tile, r = chunk_of(d, int(s[1]))
                        rows = slice(64 * r, 64 * r + 64)
                        u = g_U[rows, d, :, tile, :]
                        gdn_line(tt_(u, u, bank(MIX + 1)[rows, 0:256].rearrange("p (h n) -> p h n", h=2), ALU.subtract))
                elif s == "out":
                    for t in range(2):
                        src = bank(MIX + 2 * t)[:, 0:256].rearrange("p (h n) -> p h n", h=2)
                        q = rr[:, 0:4].rearrange("p (h t) -> p t h", h=2)[:, t]
                        gdn_line(tt_(g_o[:, t], src, spread(q, 2, P), ALU.mult))
                    o4 = g_o.rearrange("p t h n -> p (t h) n")
                    gdn_line(tt_(g_osq.rearrange("p t h n -> p (t h) n"), o4, o4, ALU.mult))
                    gdn_line(V.tensor_reduce(o_ss, g_osq.rearrange("p t h n -> p (t h) n"), AX.X, ALU.add))
                    dve.wait_ge(gdn_sem["act"], gdn_count.value("act", (b, s), 1))
                    gdn_line(V.reciprocal(o_r, o_r))
                    gdn_line(tt_(o4, o4, spread(o_r, 4, P), ALU.mult))

            def att_stage(a, s):
                if a < HEADS and not ATT[s][0] or a == HEADS and not ATT_END[s][0]:
                    return
                dve.wait_ge(att_sem["pe"], att_count.value("pe", (a, s), 1))
                if s == "score":
                    slope = 2.0 ** (-8.0 * (a + 1) / HEADS)
                    for t in range(TT):
                        ps = banks[:, MIX + 2:MIX + 4, T * t:T * t + T]
                        dd = dist[:, t].unsqueeze(1).broadcast_to([P, 2, T])
                        att_line(stt_(a_s[:, t], dd, -slope * DH ** 0.5, ps, ALU.mult, ALU.add))
                    att_line(V.tensor_reduce(mx, a_s.rearrange("p t m n -> p (t m) n"), AX.X, ALU.max))
                    att_line(ts_(nmx, mx, -DH ** -0.5, None, ALU.mult))
                    dve.wait_ge(att_sem["act"], att_count.value("act", (a, s), 4))
                    att_line(V.reciprocal(rs, sums))
                    att_line(ts_(rl, rs[:, 1:4:2], nlam[:, 0:1], None, ALU.mult))
                    if a:
                        dve.wait_ge(att_sem["pe"], att_count.value("pe", (a - 1, "pT"), 1))
                    for t in range(TT):
                        att_line(ts_(a_p[:, t, :], a_s[:, t, 0, :], rs[:, 2 * t:2 * t + 1], None, ALU.mult))
                        att_line(stt_(a_p[:, t, :], a_s[:, t, 1, :], rl[:, t:t + 1], a_p[:, t, :], ALU.mult, ALU.add))
                elif s == "pv":
                    att_line(V.tensor_copy(a_od[:, :, a, :], bank(MIX + 1)[:, 0:256].rearrange("p (t n) -> p t n", t=2)))
                elif s == "norm":
                    o = a_od.rearrange("p t h n -> p (t h) n")
                    att_line(tt_(a_sq, o, o, ALU.mult))
                    att_line(V.tensor_reduce(od_ss, a_sq, AX.X, ALU.add))
                    dve.wait_ge(att_sem["act"], att_count.value("act", (a, s), 1))
                    att_line(V.reciprocal(od_r, od_r))
                    att_line(tt_(o, o, spread(od_r, 16, P), ALU.mult))

            for what, i, s in ORDER:
                if what == "pair":
                    feed(KC * i + 2 * s + 2 + LEAD)
                elif what == "conv" and s < TAPS:
                    conv(i, s)
                elif what == "end":
                    if i == 0:
                        log_decay()
                    if i == 1:
                        decay_columns()
                elif what == "gdn":
                    gdn_stage(i, s)
                elif what == "att":
                    att_stage(i, s)

            for br, y in enumerate((ya, yd)):
                for i in range(2):
                    j = slice(4 * i, 4 * i + 4)
                    dve.wait_ge(y_split_h, 2 * br + i + 1)
                    tt_(y_part[br][1][:, j, :], y[:, j, :], y_part[br][0][:, j, :].bitcast(F32), ALU.subtract).then_inc(y_split_l, 1)
            for k in range(4):
                for br in range(2):
                    n = M0 + (2 * k + br + 1) * HEADS
                    feed(n + LEAD)
                    dve.wait_ge(chunk_used, n)
                    if k == 0:
                        dve.wait_ge(block_out, len(BLOCKS))
                    for i in range(2):
                        g = gate(br, k)[:, 512 * i:512 * i + 512]
                        tt_(g, bank(4 * (k % 2) + 2 * br + i), g, ALU.mult).then_inc(merge_dve, 1)
            for k in range(4):
                dve.wait_ge(m_split_h, k + 1)
                j = slice(4 * k, 4 * k + 4)
                tt_(h_part[1][:, j, :], gate(0, k).rearrange("p (a n) -> p a n", n=T), h_part[0][:, j, :].bitcast(F32),
                    ALU.subtract).then_inc(m_split_l, 1)
            for k in range(4):
                feed(O0 + KC * (k + 1) + LEAD)
                dve.wait_ge(x_again, 16)
                dve.wait_ge(chunk_used, O0 + KC * (k + 1))
                for t in range(TT):
                    y = x_sb[:, t, NB * k:NB * k + NB]
                    tt_(y, y, bank(2 * (k % 2) + t), ALU.add).then_inc(out_dve, 1)

            rline = Line(dve, route_dve)
            dve.wait_ge(route_act, 3)
            rline(V.reciprocal(rstd, rstd))
            rline(V.tensor_copy(ident_r, ident))
            for t in range(TT):
                for u in range(2):
                    dve.wait_ge(route_act, 4 + 2 * t + u)
                    c = slice(8 * u, 8 * u + 8)
                    rline(stt_(h2_part[1][:, t, c, :], x_sb[:, t, 1024 * u:1024 * u + 1024].rearrange("p (q c) -> p c q", c=8),
                               rstd[:, t:t + 1], h2_part[0][:, t, c, :].bitcast(F32), ALU.mult, ALU.subtract))
            dve.wait_ge(route_pe, 1)
            for k in range(8):
                rline(tt_(h2T[:, 2 * k:2 * k + 2, :], bank(k).rearrange("p (c n) -> p c n", c=2),
                          spread(gffn_c[:, 2 * k:2 * k + 2], 2, T), ALU.mult))
            assert rline.n == H2T_READY
            dve.wait_ge(route_pe, 2)
            rline(tt_(logits, bank(0)[:, 0:2 * (NG + NE)].rearrange("p (t n) -> p t n", t=2),
                      bias_r.unsqueeze(1).broadcast_to([P, TT, NG + NE]), ALU.add))
            glog = logits[:, :, 0:NG]
            BIG = 1024.0

            def per_tile(v, n):
                return v.unsqueeze(2).broadcast_to([P, TT, n])

            def first_max(vals, n, top, hot, tmp):
                iot = iota[:, 0:n].unsqueeze(1).broadcast_to([P, TT, n])
                rline(V.tensor_reduce(top, vals, AX.X, ALU.max))
                rline(tt_(tmp, vals, per_tile(top, n), ALU.is_equal))
                rline(stt_(tmp, tmp, -BIG, iot, ALU.mult, ALU.add))
                rline(V.tensor_reduce(rs1[:, 15, :], tmp, AX.X, ALU.min))
                rline(tt_(hot, tmp, per_tile(rs1[:, 15, :], n), ALU.is_equal))

            ghot = rt[:, 1, :, 0:NG]
            first_max(glog, NG, rs1[:, 0, :], ghot, rt[:, 2, :, 0:NG])
            rline(tt_(rt[:, 0, :, 0:NG], glog, per_tile(rs1[:, 0, :], NG), ALU.subtract))
            assert rline.n == GROUP_MAX
            ehot = rt[:, 3].rearrange("p t (g e) -> p t g e", g=NG)
            el = logits[:, :, NG:NG + NE].rearrange("p t (g e) -> p t g e", g=NG)
            for t in range(TT):
                rline(tt_(ehot[:, t], el[:, t], ghot[:, t, :].unsqueeze(2).broadcast_to([P, NG, EPG]), ALU.mult))
            esel = rt[:, 4, :, 0:EPG]
            for t in range(TT):
                rline(V.tensor_reduce(esel[:, t], ehot[:, t].rearrange("p g e -> p e g"), AX.X, ALU.add))
            hot1, hot2, tmp8 = (rt[:, i, :, 0:EPG] for i in (5, 6, 2))
            first_max(esel, EPG, rs1[:, 1, :], hot1, tmp8)
            rline(stt_(esel, hot1, -1e30, esel, ALU.mult, ALU.add))
            first_max(esel, EPG, rs1[:, 2, :], hot2, tmp8)
            rline(tt_(rs1[:, 7, :], rs1[:, 2, :], rs1[:, 1, :], ALU.subtract))
            assert rline.n == TOP_TWO
            dve.wait_ge(route_act, ROUTE_ACT)
            rline(V.tensor_reduce(rs1[:, 3, :], rt[:, 0, :, 0:NG], AX.X, ALU.add))
            rline(ts_(rs1[:, 4, :], rs1[:, 7, :], 1.0, None, ALU.add))
            rline(tt_(rs1[:, 5, :], rs1[:, 3, :], rs1[:, 4, :], ALU.mult))
            rline(V.reciprocal(rs1[:, 5, :], rs1[:, 5, :]))
            rline(tt_(rs1[:, 6, :], rs1[:, 5, :], rs1[:, 7, :], ALU.mult))
            rline(tt_(rt[:, 7, :, 0:EPG], hot1, per_tile(rs1[:, 5, :], EPG), ALU.mult))
            rline(tt_(rt[:, 7, :, 8:8 + EPG], hot2, per_tile(rs1[:, 6, :], EPG), ALU.mult))
            rline(tt_(rt[:, 7, :, 0:EPG], rt[:, 7, :, 0:EPG], rt[:, 7, :, 8:8 + EPG], ALU.add))
            rline(tt_(hot1, hot1, hot2, ALU.add))
            for dst, src in ((m_weight[:, :, 0:NE], rt[:, 7, :, 0:EPG]), (m_mask, hot1)):
                for t in range(TT):
                    rline(tt_(dst[:, t].rearrange("p (g e) -> p g e", g=NG), src[:, t].unsqueeze(1).broadcast_to([P, NG, EPG]),
                              ghot[:, t, :].unsqueeze(2).broadcast_to([P, NG, EPG]), ALU.mult))
            assert rline.n == MASK_READY
            dve.wait_ge(route_pe, 3)
            rank0 = m_rank[:, :, 0:NE]
            rline(stt_(rank0, bank(1)[:, 0:2 * NE].rearrange("p (t n) -> p t n", t=2), 1.0, m_mask, ALU.add, ALU.mult))
            rline(ts_(rank0, rank0, 1.0, None, ALU.subtract))
            for r in range(1, ROUNDS):
                rline(ts_(m_rank[:, :, NE * r:NE * r + NE], rank0, float(SLOTS * r), None, ALU.subtract))
                rline(V.tensor_copy(m_weight[:, :, NE * r:NE * r + NE], m_weight[:, :, 0:NE]))
            rline(V.tensor_reduce(over_f, bank(1)[:, 2 * NE:3 * NE], AX.X, ALU.max))
            rline(ts_(over_f, over_f, float(SLOTS), None, ALU.is_gt))
            rline(V.tensor_copy(over_i, over_f))
            assert rline.n == ROUTE_FLAG

            def picks(n):
                for t in range(TT):
                    r = m_rank[:, t, bass.ds(2 * n, 2)].unsqueeze(2).broadcast_to([P, 2, SLOTS])
                    tt_(pick[:, t], iota.unsqueeze(1).broadcast_to([P, 2, SLOTS]), r, ALU.is_equal).then_inc(pick_ready, 1)

            def weighted_picks(n):
                dve.wait_ge(pick_ready, 4 * n + 2)
                for t in range(TT):
                    w = m_weight[:, t, bass.ds(2 * n, 2)].unsqueeze(2).broadcast_to([P, 2, SLOTS])
                    tt_(pick_w[:, t], pick[:, t].bitcast(F32), w, ALU.mult).then_inc(pick_ready, 1)

            def read_gathered(n, groups):
                for k in groups:
                    dve.wait_ge(gathered, 4 * n + k + 2)
                    tt_(xe[:, 4 * k:4 * k + 4, :], bank(k % 2).rearrange("p (c n) -> p c n", c=4),
                        spread(gffn_c[:, 4 * k:4 * k + 4], 4, P), ALU.mult).then_inc(gather_read, 1)

            def hidden(X):
                dve.wait_ge(silu_done, X + 1)
                tt_(hid.rearrange("p a b -> p (a b)"), silu_g.rearrange("p a b -> p (a b)"), bank(4)[:, T:2 * T],
                    ALU.mult).then_inc(hid_ready, 1)

            def add_scattered(n):
                dve.wait_ge(added, 8 * n + 2)
                for q in range(8):
                    t, j = divmod(q, 4)
                    dve.wait_ge(scatter_done, 8 * n + q + 2)
                    y = x_sb[:, t, NB * j:NB * j + NB]
                    tt_(y, y, bank(0 if q % 2 else 7), ALU.add).then_inc(added, 1)

            def pair_in_pipeline(n, first=False, last=False):
                if not first:
                    dve.wait_ge(ws_turned, n)
                weighted_picks(n)
                if not last:
                    dve.wait_ge(gathered, 4 * n + 5)
                    dve.wait_ge(pick_ready, 4 * n + 4)
                    picks(n + 1)
                if not first:
                    add_scattered(n - 1)
                hidden(2 * n)
                if not last:
                    read_gathered(n + 1, (0, 1))
                hidden(2 * n + 1)
                if not last:
                    read_gathered(n + 1, (2, 3))

            def pair_alone(n):
                dve.wait_ge(gathered, 4 * n + 1)
                picks(n)
                dve.wait_ge(ws_turned, n)
                weighted_picks(n)
                read_gathered(n, range(4))
                hidden(2 * n)
                hidden(2 * n + 1)
                add_scattered(n)

            PAIRS = NE // 2
            dve.sem_inc(gather_read, 2)
            dve.sem_inc(added, 2)
            dve.sem_inc(hid_ready, 1)
            picks(0)
            read_gathered(0, range(4))
            pair_in_pipeline(0, first=True)
            with dve.Fori(1, PAIRS - 1) as n:
                pair_in_pipeline(n)
            pair_in_pipeline(PAIRS - 1, last=True)
            add_scattered(PAIRS - 1)
            with dve.If(dve.value_load(over_i[0:1, 0:1], min_val=0, max_val=1) > 0):
                with dve.Fori(PAIRS, ROUNDS * PAIRS) as n:
                    pair_alone(n)
            fline = Line(dve, fin_dve)
            for t in range(TT):
                fline(V.tensor_tensor_reduce(out=junk[t], in0=x_sb[:, t, :], in1=x_sb[:, t, :],
                                             scale=1.0, scalar=0.0, op0=ALU.mult, op1=ALU.add, accum_out=fin_ss[:, t:t + 1]))
            dve.wait_ge(fin_act, 1)
            fline(V.reciprocal(fin_ss, fin_ss))
            dve.wait_ge(final_in, 16)
            for t in range(TT):
                fline(stt_(x_sb[:, t, :], x_sb[:, t, :], fin_ss[:, t:t + 1], g_last, ALU.mult, ALU.mult))
            assert fline.n == FINAL_ROWS


_INS = ["x", "g_mix", "w_in", "conv_w", "a_log", "dt_bias", "gdn_norm_w", "diff_lambda", "diff_norm_w",
        "w_branch_a", "w_branch_d", "w_out", "g_ffn", "w_group", "b_group", "w_router", "b_router",
        "w_exp_gate", "w_exp_up", "w_exp_down", "g_final"]


def kernel(**inputs):
    import numpy as _np
    import concourse.bacc as _bacc
    from concourse import mybir as _mybir
    from concourse.bass_utils import run_bass_kernel_spmd as _run

    nc = _bacc.Bacc("TRN2", target_bir_lowering=False, num_devices=1)
    arrays = {f"in_{name}_dram": _np.ascontiguousarray(inputs[name]) for name in _INS}
    arrays["in_tables_dram"] = constants()
    args = [nc.dram_tensor(name, a.shape, _mybir.dt.from_np(a.dtype), kind="ExternalInput").ap()
            for name, a in arrays.items()]
    args.append(nc.dram_tensor("out_dram", (1, T, D), F32, kind="ExternalOutput").ap())
    encoder(nc, *args)
    r = _run(nc, [arrays], core_ids=[0])
    return r.results[0]["out_dram"]
```

```python
import math
from contextlib import ExitStack

import concourse.bass as bass
from concourse import mybir

F32 = mybir.dt.float32
F32R = mybir.dt.float32r
I32 = mybir.dt.int32
ALU = mybir.AluOpType
ACT = mybir.ActivationFunctionType
AX = mybir.AxisListType

P = 128
D = 2048
T = 256
TT = T // P
KC = D // P
HEADS = 8
DK = 128
CH = 64
DH = 64
NG, EPG = 4, 8
NE = NG * EPG
NR = NG + NE
FE = 512
SLOTS = 64
ROUNDS = T // SLOTS
EPS = 1e-6
LAM_INIT = 0.8 - 0.6 * math.exp(-0.3 * 0)

QK = HEADS * DK
OFF_Q, OFF_K, OFF_V, OFF_Z = 0, QK, 2 * QK, 3 * QK
OFF_AB = 4 * QK
OFF_AQ = OFF_AB + 4 * HEADS
OFF_AK, OFF_AV = OFF_AQ + QK, OFF_AQ + 2 * QK
OFF_GA = OFF_AQ + 3 * QK
OFF_GD = OFF_GA + D
NB = 512

BLOCKS = [("q", OFF_Q, 0), ("k", OFF_K, 0), ("v", OFF_V, 0), ("z", OFF_Z, 0), ("z", OFF_Z + NB, 1),
          ("aq", OFF_AQ, 0), ("aq", OFF_AQ + NB, 1),
          ("q", OFF_Q + NB, 1), ("k", OFF_K + NB, 1), ("v", OFF_V + NB, 1),
          ("ak", OFF_AK, 0), ("ak", OFF_AK + NB, 1), ("av", OFF_AV, 0), ("av", OFF_AV + NB, 1)]
BLOCKS += [("ga", OFF_GA + NB * i, i) for i in range(4)] + [("gd", OFF_GD + NB * i, i) for i in range(4)]
QKV_THERE = (3, 10)
Z_THERE = (4, 5)
MIX_FROM, GDN_AGAIN, ATT_FROM = 3, 10, 16
CONV = ("q", "k", "v")
TAPS = 5
TOKEN_MAJOR = ("z", "av")

LEVELS = 6
GDN = {"norm": (3, 2, 2), "decay": (4, 3, 1), "gram": (5, 0, 0), "first": (0, 1, 1)}
for _l in range(1, LEVELS):
    GDN[f"lt{_l}"] = (1, 1, 1) if _l <= 2 else (0, 1, 0)
    GDN[f"sub{_l}"] = (2, 0, 1) if _l < LEVELS - 1 else (1, 0, 0)
GDN |= {"uw": (1, 1, 0), "s0": (2, 0, 0), "v1": (2, 0, 0), "s1": (4, 0, 0), "v2": (2, 0, 0),
        "s2": (4, 0, 0), "v3": (2, 0, 0), "out": (6, 1, 1), "turn": (0, 1, 0)}
ATT = {"score": (10, 4, 0), "pT": (0, 1, 0), "pv": (3, 0, 0)}
ATT_END = {"norm": (2, 1, 0), "turn": (0, 1, 0)}
GDN_BATCHES = HEADS // 2
RESTS, ATT_RESTS = {"out": 2}, {"norm": 4}

DIAG = 7
HT_MADE = [DIAG + 3] + [DIAG + 5 + 3 * k for k in range(7)]
HT_LOW = [DIAG + 6 + 3 * k for k in range(7)] + [DIAG + 25]
PARTS_ACT, SET_ACT = 12, 17
AB_SUMS, AB_X, G_READY, GC_READY, COLS_READY = 38, 41, 43, 50, 51
SMALL_ALL = 16 * 10
ROUTE_ACT = 15
LG_COPIED, GROUP_MAX, TOP_TWO, MASK_READY, RANK_READ, LOW_READY, ROUTE_FLAG = 5, 13, 29, 32, 37, 39, 57
FINAL_ROWS = 7
SCATTER = [(t, j) for j in range(4) for t in range(TT)]


def conv_blocks(b):
    return sum(kind in CONV for kind, _, _ in BLOCKS[:b + 1])


def chunk_of(direction, step):
    return divmod(step if direction == 0 else T // CH - 1 - step, 2)


class StageCounts:

    def __init__(self, stages):
        self.before = {}
        at = [0, 0, 0, 0]
        for key, ops in stages:
            self.before[key] = tuple(at)
            at = [a + b for a, b in zip(at, (*ops, 1))]
        self.total = tuple(at)

    def value(self, engine, key, k=0):
        return self.before[key][("dve", "act", "pool", "pe").index(engine)] + k


GDN_STAGES = [((b, s), ops) for b in range(GDN_BATCHES) for s, ops in GDN.items()]
ATT_STAGES = [((0, "score"), ATT["score"])]
for _a in range(HEADS):
    if _a < HEADS - 1:
        ATT_STAGES.append(((_a + 1, "score"), ATT["score"]))
    ATT_STAGES += [((_a, s), ATT[s]) for s in ("pT", "pv")]
ATT_STAGES += [((HEADS, s), ops) for s, ops in ATT_END.items()]


def stage_order():
    gdn = [("gdn", *key) for key, _ in GDN_STAGES]
    att = [("att", *key) for key, _ in ATT_STAGES]
    order = []
    conv = []
    rest = 0
    for b in range(len(BLOCKS)):
        for s in range(KC // 2):
            order.append(("pair", b, s))
            if conv:
                order.append(conv.pop(0))
            if gdn and (gdn[0][1] < 2 or b >= GDN_AGAIN) and (b, s) >= (MIX_FROM, TAPS):
                todo = gdn if b != GDN_AGAIN and gdn[0][1] < 2 or b > GDN_AGAIN or s >= TAPS else None
            else:
                todo = att if b >= ATT_FROM and not gdn else None
            if rest:
                rest -= 1
            elif todo:
                order.append(todo.pop(0))
                rest = RESTS.get(order[-1][2], 0) if order[-1][1] < HEADS else ATT_RESTS.get(order[-1][2], 0)
                if order[-1][0] == "att" and order[-1][2] == "score":
                    rest = int(order[-1][1] < HEADS - 1)
        order.append(("end", b, 0))
        if BLOCKS[b][0] in CONV:
            conv = [("conv", b, k) for k in range(TAPS + 1)]
    assert not gdn and not att
    return order


ORDER = stage_order()

SLOT = 4096
RING = 0
SETUP = 4096
G_E, G_LT, G_EG, G_AT, G_UT, G_T, G_TT, G_Z = 0, 512, 1024, 2048, 2560, 3072, 3584, 4096
G_XV, G_XK, G_KS, G_U, G_WT = (4608 + 1024 * i for i in range(5))
G_S = G_WT + 1024
G_KTM = G_S + 1536
G_VTM = G_KTM + 512
A_OD = 8192
A_TMP = A_OD + 2048
UNIT = 2048
UNIT_RING = 12288
QKV = UNIT_RING + 3 * UNIT
ZS = QKV + 3072
AQK = ZS + 2048
X2 = AQK + 2048
YA = AQK + 6144
YD = YA + 2048
CONST = YD + 2048
W_ROUTE = 6 * SLOT
MOE = YA
LATE = CONST + 512
SMALL = LATE + 2560
WORDS = 37520
PARTS = 2 * 4096
STAGE = 1024
STAGES = 7
R_STAGE = PARTS
R_PICK = R_STAGE + STAGES * STAGE
R_WORDS = R_PICK + 256
LEAD = 7

C_IDENT, C_BEFORE, C_ONES, C_IOTA = 0, 128, 256, 384
C_TWICE = C_IOTA + 64
C_TRI = C_TWICE + 64
C_TRI64 = C_TRI + 512
C_LEVEL = C_TRI64 + 128
C_DIST = C_LEVEL + 2 * LEVELS * CH
C_FOLD = C_DIST + 512
N_CONST = C_FOLD + 32
assert CONST + C_TRI == LATE and CONST + N_CONST <= SMALL


def constants():
    import numpy as np
    c = np.zeros((P, N_CONST), np.float32)
    i = np.arange(P)
    r, n = i[:, None], i[None, :]
    same = (r // CH) == (n // CH)
    c[:, C_IDENT:C_IDENT + 128] = r == n
    for k, m in enumerate([r <= n, r >= n, r > n, r < n]):
        c[:, C_TRI + 128 * k:C_TRI + 128 * (k + 1)] = same & m
    r, n = (i % CH)[:, None], np.arange(CH)[None, :]
    for k, m in enumerate([r <= n, r >= n]):
        c[:, C_TRI64 + CH * k:C_TRI64 + CH * (k + 1)] = m
    for lv in range(LEVELS):
        m = 1 << lv
        block = (r // (2 * m)) == (n // (2 * m))
        low_r, low_n = (r // m) % 2 == 0, (n // m) % 2 == 0
        for d, mask in enumerate([low_r & ~low_n, ~low_r & low_n]):
            at = C_LEVEL + (lv * 2 + d) * CH
            c[:, at:at + CH] = block & mask
    r, n = i[:, None], i[None, :]
    for t in range(TT):
        c[:, C_DIST + 256 * t:C_DIST + 256 * (t + 1)] = np.abs(i[:, None] + 128 * t - np.arange(T)[None, :])
    c[:, C_BEFORE:C_BEFORE + 128] = r < n
    c[:, C_ONES:C_ONES + 128] = 1.0
    c[:, C_IOTA:C_IOTA + 64] = np.arange(64)[None, :]
    c[:, C_TWICE:C_TWICE + 64] = (i % 64)[:, None] == np.arange(64)[None, :]
    c[:, C_FOLD:C_FOLD + 32] = (i % 32)[:, None] == np.arange(32)[None, :]
    return c


def encoder(nc, x, g_mix, w_in, conv_w, a_log, dt_bias, gdn_norm_w, diff_lambda, diff_norm_w,
            w_branch_a, w_branch_d, w_out, g_ffn, w_group, b_group, w_router, b_router,
            w_exp_gate, w_exp_up, w_exp_down, g_final, const_tables, out):
    ctx = ExitStack()
    with ctx:
        def sem(name):
            return ctx.enter_context(nc.semaphore(name))

        arena = ctx.enter_context(nc.sbuf_tensor("arena", [P, WORDS], F32))
        rounded = ctx.enter_context(nc.sbuf_tensor("rounded", [P, R_WORDS], F32R))
        banks = ctx.enter_context(nc.psum_tensor("banks", [P, 8, 512], F32))
        PROJ, MIX = 0, 4

        def at(off, *shape, tensor=None):
            n = math.prod(shape)
            v = (arena if tensor is None else tensor)[:, off:off + n]
            names = "abcde"[:len(shape)]
            if len(shape) > 1:
                v = v.rearrange(f"p ({' '.join(names)}) -> p {' '.join(names)}",
                                **dict(zip(names[:-1], shape[:-1])))
            return v

        def bank(i):
            return banks[:, i, :]

        def spread(ap, *shape):
            return ap.unsqueeze(len(shape)).broadcast_to([P, *shape])

        ident = at(CONST + C_IDENT, 128)
        tri = at(CONST + C_TRI, 4, 128)
        tri64 = at(CONST + C_TRI64, 2, CH)
        fold = at(CONST + C_FOLD, 32)
        level = at(CONST + C_LEVEL, LEVELS, 2, CH)
        dist = at(CONST + C_DIST, TT, T)
        before = at(CONST + C_BEFORE, 128)
        ones = at(CONST + C_ONES, 128)
        iota = at(CONST + C_IOTA, 64)
        twice = at(CONST + C_TWICE, 64)
        small = [SMALL]
        early = [CONST + N_CONST]

        def take(*shape):
            v = at(small[0], *shape)
            small[0] += math.prod(shape)
            assert small[0] <= WORDS
            return v

        def take_early(*shape):
            v = at(early[0], *shape)
            early[0] += math.prod(shape)
            assert early[0] <= SMALL
            return v

        gmix_c, gffn_c = take(KC), take(KC)
        conv_c, gffn_n = take_early(5 * 24), take(KC + 2)
        dtb, alog = take_early(16), take_early(16)
        gdn_w, diff_w = gffn_n[:, KC:KC + 1], gffn_n[:, KC + 1:KC + 2]
        bias_r = take(NG + NE)
        eps_c, one_c, nlam = take(1), take(1), take(1)
        ss, rstd, ss_half = take(2), take(2), take(2)
        ab_x, ab_u = take(TT, 16), take(TT, 16)
        g_log, beta = take_early(TT, 16), take_early(TT, 16)
        gc, begc, esfx, bcol = (take_early(2, HEADS, 2) for _ in range(4))
        lam_s = take(2)
        rn, rr = take(8), take(8)
        glast = take(2, 2, 2, 2)
        o_ss, o_r = take(4), take(4)
        mx, nmx, sums, rs, rl = take(4), take(4), take(4), take(4), take(2)
        od_ss, od_r = take(16), take(16)
        w_route = at(W_ROUTE, KC, NG + NE)

        x_sb = at(X2, TT, D)
        row_diag, rstd_row = at(RING, TT, P), at(RING + T, T)
        set_junk = [at(SETUP + 2048 * (t + 1), D) for t in range(TT)]
        w_ab = at(SETUP, KC, 32)
        conv_rows, gffn_rows = at(SETUP + 512, P), at(SETUP + 640, P)
        ab_sums = at(SETUP + 1280, T)
        lam_in, lam_p = at(SETUP + 768, 4, 64), at(SETUP + 1024, 2, 64)
        hT = at(YA, KC, T)
        h_part = [at(4096 * i, KC, T, tensor=rounded) for i in range(2)]
        y_part = [[at(4096 * i + 2048 * br, HEADS, T, tensor=rounded) for i in range(2)] for br in range(2)]
        w_part = [[at(R_STAGE + STAGE * i + 512 * k, NB, tensor=rounded) for k in range(2)] for i in range(STAGES)]
        qT, kT, vT = (at(QKV + 1024 * i, HEADS // 2, T) for i in range(3))
        zs = at(ZS, TT, QK)
        aq, ak = at(AQK, HEADS, T), at(AQK + 2048, HEADS, T)
        av = at(AQK + 4096, TT, QK)

        def gate(br, k):
            n = 4 * br + k
            return at(QKV + 1024 * n if n < 2 else 1024 * (n - 2), 4 * T)

        ya, yd = at(YA, HEADS, T), at(YD, HEADS, T)

        g_sq = at(G_KS, 2, 2, T)
        g_E, g_LT, g_AT, g_UT, g_T, g_TT, g_Z = (
            at(o, 2, 2, 2, CH) for o in (G_E, G_LT, G_AT, G_UT, G_T, G_TT, G_Z))
        g_EG, g_XV, g_XK, g_KS, g_U = (at(o, 2, 2, 2, P) for o in (G_EG, G_XV, G_XK, G_KS, G_U))
        g_WT = at(G_WT, 2, 2, 2, 2, CH)
        g_S = at(G_S, 2, 2, 3, P)
        g_k, g_v = at(G_KTM, 2, 2, P), at(G_VTM, 2, 2, P)
        g_kT = at(G_U, 2, T)
        g_o, g_osq = at(G_XV, 2, 2, P), at(G_XV + 512, 2, 2, P)

        a_od = at(A_OD, TT, HEADS, P)
        a_s = at(A_TMP, TT, 2, T)
        a_p, a_pT = at(A_TMP + 1024, TT, T), at(A_TMP + 1536, 2, TT, P)
        a_sq = at(A_OD - 2 * P, TT, P)

        h2_part = [at(4096 * i, TT, KC, P, tensor=rounded) for i in range(2)]
        h2T = at(YA, KC, T)
        pick = at(R_PICK, TT, 2, SLOTS, tensor=rounded)
        y_sb = at(LATE, 4, 512)
        sq_junk, lg_T = at(LATE, 512), at(LATE + 512, T)
        g_last = at(RING, D)
        junk = [at(RING + SLOT * (1 + t), D) for t in range(TT)]
        moe_at = [MOE]

        def moe(*shape):
            v = at(moe_at[0], *shape)
            moe_at[0] += math.prod(shape)
            assert moe_at[0] <= CONST
            return v

        xe = moe(KC, 2 * SLOTS)
        g_part, u_part = moe(FE), moe(FE)
        silu_g, hid = moe(4, SLOTS), moe(4, SLOTS)
        pick_w, ws = moe(TT, 2, SLOTS), moe(T)
        rt = at(LATE + 2048, 8, TT, NE)
        logits = take(TT, NG + NE)
        rs1 = take(16, TT)
        m_mask, m_weight = at(W_ROUTE + KC * (NG + NE), TT, NE), at(W_ROUTE + KC * (NG + NE) + TT * NE, TT, ROUNDS * NE)
        m_rank = take(TT, ROUNDS * NE)
        fit = W_ROUTE + KC * (NG + NE) + TT * NE * (1 + ROUNDS)
        assert fit <= X2
        fin_ss, ss_part = take(TT), take(TT, 4)
        over_f, over_i = take(1), take(1).bitcast(I32)

        x_in = [sem(f"x_in{t}") for t in range(TT)]
        table_in, masks_in, small_in, wab_in = sem("table_in"), sem("masks_in"), sem("small_in"), sem("wab_in")
        gmix_in = sem("gmix_in")
        set_act, set_dve, set_pe = sem("set_act"), sem("set_dve"), sem("set_pe")
        unit_in = [sem(f"unit_in{i}") for i in range(3)]
        split_h, split_l = sem("split_h"), sem("split_l")
        chunk_used = sem("chunk_used")
        y_split_h, y_split_l = sem("y_split_h"), sem("y_split_l")
        m_split_h, m_split_l = sem("m_split_h"), sem("m_split_l")
        conv_read = sem("conv_read")
        block_out = sem("block_out")
        gdn_sem = {e: sem(f"gdn_{e}") for e in ("dve", "act", "pool", "pe")}
        att_sem = {e: sem(f"att_{e}") for e in ("dve", "act", "pool", "pe")}
        merge_dve, merge_pool = sem("merge_dve"), sem("merge_pool")
        x_again, out_dve = sem("x_again"), sem("out_dve")
        route_in, turned_read = sem("route_in"), sem("turned_read")
        route_pe, route_dve, route_act = sem("route_pe"), sem("route_dve"), sem("route_act")
        full = [sem(f"expert_unit_in{i}") for i in range(6)]
        unit_free = [sem(f"{w}_used") for w in ("gate", "up", "down")]
        pick_ready, ws_turned, ws_ready = sem("pick_ready"), sem("ws_turned"), sem("ws_ready")
        gathered, gather_read = sem("gathered"), sem("gather_read")
        gu_copied, gu_turned = sem("gu_copied"), sem("gu_turned")
        silu_done, hid_ready, y_copied = sem("silu_done"), sem("hid_ready"), sem("y_copied")
        scatter_done, added = sem("scatter_done"), sem("added")
        final_in, fin_act, fin_dve, stored = sem("final_in"), sem("fin_act"), sem("fin_dve"), sem("stored")

        gdn_count = StageCounts(GDN_STAGES)
        att_count = StageCounts(ATT_STAGES)

        def wait_part(eng, sems, counts, me, key, offsets=()):
            off = dict(offsets)
            for e in ("dve", "act", "pool", "pe"):
                n = counts.value(e, key, off.get(e, 0))
                if n > 0:
                    eng.wait_ge(sems[e], n)

        class Line:

            def __init__(self, eng, s):
                self.eng, self.sem, self.n = eng, s, 0

            def __call__(self, ins):
                self.n += 1
                ins.then_inc(self.sem, 1)
                self.eng.wait_ge(self.sem, self.n)

        block = ctx.enter_context(nc.Block())

        wi = w_in[0].rearrange("(u p c) n -> u p c n", u=2, c=8)
        wa, wd = (w[0].rearrange("(c p) n -> p c n", p=P) for w in (w_branch_a, w_branch_d))
        wo = w_out[0].rearrange("(c p) n -> p c n", p=P)
        xt = x[0].rearrange("(t p) d -> p t d", p=P)
        M0 = KC * len(BLOCKS)
        O0 = M0 + 4 * 2 * HEADS
        CHUNKS = O0 + 4 * KC
        UNITS = CHUNKS // 4

        def unit_source(n):
            c = 4 * n
            if c < M0:
                col = BLOCKS[c // KC][1]
                return wi[c % KC // 8, :, c % 8:c % 8 + 4, col:col + NB]
            if c < O0:
                k, br = divmod((c - M0) // HEADS, 2)
                return (wa, wd)[br][:, c % HEADS:c % HEADS + 4, NB * k:NB * k + NB]
            k = (c - O0) // KC
            return wo[:, c % KC:c % KC + 4, NB * k:NB * k + NB]

        def unit(n):
            return at(UNIT_RING + UNIT * (n % 3), 4, NB)

        eg = w_exp_gate[0].rearrange("e (u p c) f -> e u p c f", u=2, c=8)
        eu = w_exp_up[0].rearrange("e (u p c) f -> e u p c f", u=2, c=8)
        ed = w_exp_down[0].rearrange("e (k p) (u d) -> e u p k d", u=2, p=P)

        def expert_unit(s, *shape):
            return at(RING + SLOT * s, *shape)

        def expert_source(e, s):
            return (eg, eu, ed)[s // 2][e, s % 2]

        def expert_target(s):
            return expert_unit(s, 8, FE) if s < 4 else expert_unit(s, 4, D // 2)

        @block.sync
        def _(sp):
            def small_loads():
                for dst, src in ((gffn_c.rearrange("p (u c) -> p u c", u=2), g_ffn[0].rearrange("(u p c) -> p u c", u=2, c=8)),
                                 (gffn_rows[0:KC, :], g_ffn[0].rearrange("(c p) -> c p", p=P)),
                                 (conv_rows[0:120, :], conv_w[0].rearrange("k (t p) -> (k t) p", p=P)),
                                 (dtb, dt_bias[0].rearrange("a b -> (a b)").partition_broadcast(P)),
                                 (alog, a_log[0].rearrange("a b -> (a b)").partition_broadcast(P)),
                                 (gffn_rows[KC:KC + 1, :], gdn_norm_w),
                                 (gffn_rows[KC + 1:KC + 2, :], diff_norm_w),
                                 (lam_in.rearrange("p a b -> p (a b)"), diff_lambda[0].rearrange("a b -> (a b)").partition_broadcast(P)),
                                 (bias_r[:, 0:NG], b_group[0].partition_broadcast(P)),
                                 (bias_r[:, NG:NG + NE], b_router[0].partition_broadcast(P))):
                    sp.dma_start(dst, src).then_inc(small_in, 16)
                for u in range(2):
                    sp.dma_start(w_ab[:, 8 * u:8 * u + 8, :], wi[u, :, :, OFF_AB:OFF_AB + 32]).then_inc(wab_in, 16)

            sp.dma_start(at(CONST, C_TRI), const_tables[:, 0:C_TRI]).then_inc(table_in, 16)
            for t in range(TT):
                sp.dma_start(x_sb[:, t], xt[:, t]).then_inc(x_in[t], 16)
            for n in range(UNITS):
                if n >= 3:
                    sp.wait_ge(split_l, 4 * (n - 2))
                sp.dma_start(unit(n), unit_source(n)).then_inc(unit_in[n % 3], 16)
                if n == 2:
                    sp.dma_start(at(CONST + C_TRI, N_CONST - C_TRI), const_tables[:, C_TRI:N_CONST]).then_inc(masks_in, 16)
                    small_loads()
                if n == M0 // 4 + 2:
                    sp.wait_ge(att_sem["pe"], att_count.total[3])
                    sp.wait_ge(att_sem["act"], att_count.total[1])
                    sp.dma_start(x_sb, xt).then_inc(x_again, 16)
                    for w, a, b in ((w_group, 0, NG), (w_router, NG, NG + NE)):
                        sp.dma_start(w_route[:, :, a:b], w[0].rearrange("(c p) n -> p c n", p=P)).then_inc(route_in, 16)
                if n in (M0 // 4 + 6, M0 // 4 + 10):
                    s = 2 if n == M0 // 4 + 6 else 5
                    sp.dma_start(expert_target(s), expert_source(0, s)).then_inc(full[s], 16)
                if n in (O0 // 4 + 5, O0 // 4 + 9):
                    sp.wait_ge(m_split_l, 8)
                    s = 0 if n == O0 // 4 + 5 else 1
                    sp.dma_start(expert_target(s), expert_source(0, s)).then_inc(full[s], 16)
            sp.wait_ge(split_l, CHUNKS)
            for s in (3, 4):
                sp.dma_start(expert_target(s), expert_source(0, s)).then_inc(full[s], 16)

            def load_expert(n, e):
                for s in range(6):
                    sp.wait_ge(unit_free[s // 2], 2 * n + (s % 2 - 1))
                    sp.dma_start(expert_target(s), expert_source(e, s)).then_inc(full[s], 16)

            with sp.Fori(1, NE) as e:
                load_expert(e, e)
            sp.wait_ge(route_dve, ROUTE_FLAG)
            sp_over = sp.value_load(over_i[0:1, 0:1], min_val=0, max_val=1)
            sp.wait_ge(unit_free[0], 2 * NE - 1)
            sp.dma_start(g_last, g_final.partition_broadcast(P)).then_inc(final_in, 16)
            with sp.If(sp_over > 0):
                sp.wait_ge(final_in, 16)
                with sp.Fori(1, ROUNDS) as r:
                    with sp.Fori(0, NE) as e:
                        load_expert(r * NE + e, e)
                sp.wait_ge(added, 8 * ROUNDS * (NE // 2) + 2)
                sp.dma_start(g_last, g_final.partition_broadcast(P)).then_inc(final_in, 16)
            for t in range(TT):
                for u in range(2):
                    sp.wait_ge(fin_dve, FINAL_ROWS - 3 + 2 * t + u)
                    c = slice(1024 * u, 1024 * u + 1024)
                    sp.dma_start(out[0].rearrange("(t p) d -> p t d", p=P)[:, t, c], x_sb[:, t, c]).then_inc(stored, 16)
            sp.wait_ge(stored, 64)

        @block.tensor
        def _(pe):
            mm = nc.tensor.matmul
            turn = nc.tensor.transpose

            def turn_x(t, chunks):
                for c in chunks:
                    b = 2 + c // 2 if c < 12 else (c - 12) // 2 + 2
                    last = turn(bank(b)[:, (c % 2) * T + t * P:(c % 2) * T + t * P + P],
                                x_sb[:, t, 1024 * (c // 8):1024 * (c // 8) + 1024].rearrange("p (q c) -> p c q", c=8)[:, c % 8, :],
                                ident)
                return last

            pe.wait_ge(table_in, 16)
            for t in range(TT):
                pe.wait_ge(x_in[t], 16)
                last = turn_x(t, range(12))
            last.then_inc(set_pe, 1)
            pe.wait_ge(set_dve, DIAG)
            for t in range(TT):
                last = mm(bank(0)[:, t * P:(t + 1) * P], ones, row_diag[:, t, :], start=True, stop=True)
            last.then_inc(set_pe, 1)

            def turn_small():
                pe.wait_ge(small_in, SMALL_ALL)
                turn(bank(4)[:, 0:120], conv_rows[0:120, :], ident[0:120, 0:120])
                n = KC + 2
                turn(bank(4)[:, 128:128 + n], gffn_rows[0:n, :], ident[0:n, 0:n]).then_inc(set_pe, 1)

            def thrice(out, lefts, rights, first, final, **more):
                lh, ll = lefts
                rh, rl = rights
                mm(out, lh, rh, start=first, stop=False, skip_group_check=True)
                mm(out, lh, rl, start=False, stop=False, skip_group_check=True)
                return mm(out, ll, rh, start=False, stop=final, skip_group_check=True)

            def decay_and_beta():
                pe.wait_ge(wab_in, 32)
                for c in range(KC):
                    g = 32 * (c % 4)
                    last = mm(bank(5)[g:g + 32, 0:T], w_ab[:, c, :], hT[:, c, :], start=(c < 4), stop=(c >= KC - 4))
                last.then_inc(set_pe, 1)

            def fold_quarters():
                pe.wait_ge(masks_in, 16)
                pe.wait_ge(set_dve, AB_SUMS)
                for t in range(TT):
                    last = mm(bank(7)[:, 32 * t:32 * t + 32], ab_sums[:, t * P:(t + 1) * P], fold, start=True, stop=True)
                last.then_inc(set_pe, 1)

            def decay_sums():
                pe.wait_ge(set_dve, G_READY)
                for k in range(4):
                    for t in range(TT):
                        last = mm(bank(6)[:, (k * 2 + t) * 8:(k * 2 + t) * 8 + 8], tri[:, k, :],
                                  g_log[:, t, (k % 2) * 8:(k % 2) * 8 + 8], start=True, stop=True)
                last.then_inc(set_pe, 1)

            def by_channel(m, b0, moving, first, final):
                pe.wait_ge(split_l, m + 1)
                w = w_part[m % STAGES]
                for j in range(4):
                    last = thrice(bank(b0 + j // 2)[:, (j % 2) * T:(j % 2 + 1) * T], [p[:, j * P:(j + 1) * P] for p in w],
                                  moving, first and j % 2 == 0, final)
                last.then_inc(chunk_used, 1)

            def by_token(m, b0, stationary, first, final):
                pe.wait_ge(split_l, m + 1)
                for t in range(TT):
                    last = thrice(bank(b0 + t), [p[:, t * P:(t + 1) * P] for p in stationary], w_part[m % STAGES],
                                  first, final)
                last.then_inc(chunk_used, 1)

            def pair(b, s):
                kind = BLOCKS[b][0]
                b0 = PROJ + 2 * (b % 2)
                if s == 0 and b >= 2:
                    if BLOCKS[b - 2][0] in CONV:
                        pe.wait_ge(conv_read, 20 * conv_blocks(b - 2))
                    else:
                        pe.wait_ge(block_out, b - 1)
                if b == 0:
                    pe.wait_ge(set_dve, HT_LOW[s])
                    if s == 2:
                        for t in range(TT):
                            last = turn_x(t, range(12, KC))
                        last.then_inc(set_pe, 1)
                for c in (2 * s, 2 * s + 1):
                    (by_token if kind in TOKEN_MAJOR else by_channel)(
                        KC * b + c, b0, [h[:, c, :] for h in h_part], c == 0, c == KC - 1)

            DHT = [(d, h, t) for d in range(2) for h in range(2) for t in range(2)]

            def mix(i, j=0, n=P):
                return bank(MIX + i)[:, P * j:P * j + n]

            def chunkwise(i, left, right):
                for n, (d, h, t) in enumerate(DHT):
                    for r in range(2):
                        rows = slice(CH * r, CH * r + CH)
                        last = mm(bank(MIX + i)[rows, CH * n:CH * n + CH], left(d, h, t)[rows], right(d, h, t)[rows],
                                  start=True, stop=True)
                return last

            def gdn_stage(b, s):
                if s == "gram":
                    pe.wait_ge(gdn_sem["act"], gdn_count.value("act", (b, "decay"), 2))
                    pe.wait_ge(gdn_sem["dve"], gdn_count.value("dve", (b, "decay"), 1))
                elif s == "first":
                    pe.wait_ge(gdn_sem["act"], gdn_count.value("act", (b, s)))
                    pe.wait_ge(gdn_sem["dve"], gdn_count.value("dve", (b, "gram"), 4))
                else:
                    wait_part(pe, gdn_sem, gdn_count, "pe", (b, s), {"pool": 2} if s == "norm" else {})
                heads = (2 * b, 2 * b + 1)
                single = dict(start=True, stop=True)
                if s == "norm":
                    pe.wait_ge(block_out, QKV_THERE[b // 2])
                    for k, src in enumerate((kT, vT)):
                        for h in range(2):
                            for t in range(2):
                                turn(mix(k, 2 * h + t), src[:, heads[h] % 4, t * P:(t + 1) * P], ident)
                    for qk in range(2):
                        for h in range(2):
                            for t in range(2):
                                n = qk * 4 + h * 2 + t
                                last = mm(mix(2)[:, n:n + 1], g_sq[:, qk, h, t * P:(t + 1) * P], ones[:, 0:1], **single)
                elif s == "decay":
                    if b == 0:
                        pe.wait_ge(set_dve, COLS_READY)
                    for h in range(2):
                        for t in range(2):
                            turn(mix(0, 2 * h + t), g_k[:, h, t, :], ident)
                    def log_col(d, h, t):
                        return g_log[:, t, d * 8 + heads[h]:d * 8 + heads[h] + 1]

                    chunkwise(1, lambda d, h, t: log_col(d, h, t).broadcast_to([P, CH]), lambda d, h, t: tri64[:, d, :])
                    for d, h, t in DHT:
                        last = mm(mix(2 + d, 2 * h + t), log_col(d, h, t).broadcast_to([P, P]), tri[:, d, :], **single)
                elif s == "gram":
                    for h in range(2):
                        for t in range(2):
                            for r in range(2):
                                cols = slice(P * t + CH * r, P * t + CH * r + CH)
                                o = bank(MIX)[CH * r:CH * r + CH]
                                n = CH * (2 * h + t)
                                mm(o[:, n:n + CH], g_kT[:, h, cols], g_kT[:, h, cols], **single)
                                mm(bank(MIX + 1)[CH * r:CH * r + CH, n:n + CH], g_kT[:, h, cols], qT[:, heads[h] % 4, cols], **single)
                    last = chunkwise(2, lambda d, h, t: bcol[:, d, heads[h], t:t + 1].broadcast_to([P, CH]),
                                     lambda d, h, t: twice)
                elif s == "first":
                    last = chunkwise(2, lambda *m: g_TT[:, *m, :], lambda *m: twice)
                elif s[:2] == "lt":
                    last = chunkwise(0, lambda *m: g_UT[:, *m, :], lambda *m: g_T[:, *m, :])
                elif s[:3] == "sub":
                    if s != f"sub{LEVELS - 1}":
                        chunkwise(1, lambda *m: g_TT[:, *m, :], lambda *m: g_Z[:, *m, :])
                    last = chunkwise(2, lambda *m: g_Z[:, *m, :], lambda *m: g_TT[:, *m, :])
                elif s == "uw":
                    for n, (d, h, t) in enumerate(DHT):
                        for r in range(2):
                            rows = slice(CH * r, CH * r + CH)
                            mm(mix(d, 2 * h + t)[rows], g_TT[rows, d, h, t, :], g_XV[rows, d, h, t, :], **single)
                    for n, (d, h, t) in enumerate(DHT):
                        for r in range(2):
                            rows = slice(CH * r, CH * r + CH)
                            last = mm(bank(MIX + 2 + r)[:, CH * n:CH * n + CH], g_XK[rows, d, h, t, :],
                                      g_TT[rows, d, h, t, :], **single)
                elif s[0] == "s":
                    for d in range(2):
                        tile, r = chunk_of(d, int(s[1]))
                        for h in range(2):
                            last = mm(mix(2 * d, h), g_KS[64 * r:64 * r + 64, d, h, tile, :],
                                      g_U[64 * r:64 * r + 64, d, h, tile, :], **single)
                elif s[0] == "v":
                    step = int(s[1])
                    for d in range(2):
                        tile, r = chunk_of(d, step)
                        for h in range(2):
                            last = mm(mix(1, h)[64 * r:64 * r + 64, :], g_WT[:, r, d, h, tile, :],
                                      g_S[:, h, d, step - 1, :], **single)
                elif s == "out":
                    for t in range(2):
                        for h in range(2):
                            o = mix(2 * t, h)
                            for d in range(2):
                                for r in range(2):
                                    rows = slice(CH * r, CH * r + CH)
                                    mm(o[rows], g_AT[rows, d, h, t, :], g_U[rows, d, h, t, :], start=(d == 0), stop=False,
                                       skip_group_check=True)
                            for d in range(2):
                                for r in range(2):
                                    step = 2 * t + r if d == 0 else 3 - 2 * t - r
                                    if step:
                                        last = mm(o[64 * r:64 * r + 64, :], g_EG[:, d, h, t, 64 * r:64 * r + 64],
                                                  g_S[:, h, d, step - 1, :], start=False, stop=True, skip_group_check=True)
                elif s == "turn":
                    for t in range(2):
                        for h in range(2):
                            last = turn(mix(0, 2 * h + t), g_o[:, t, h, :], ident)
                last.then_inc(gdn_sem["pe"], 1)

            def att_stage(a, s):
                if (a, s) == (0, "score"):
                    for e in ("dve", "act", "pool"):
                        pe.wait_ge(gdn_sem[e], gdn_count.total[("dve", "act", "pool").index(e)])
                    pe.wait_ge(block_out, 14)
                if s == "score" and a:
                    pe.wait_ge(att_sem["dve"], att_count.value("dve", (a - 1, s), 2))
                elif s == "pT":
                    pe.wait_ge(att_sem["dve"], att_count.value("dve", (a, "score"), 10))
                    if a:
                        pe.wait_ge(att_sem["act"], att_count.value("act", (a - 1, s), 1))
                elif s == "pv":
                    pe.wait_ge(att_sem["act"], att_count.value("act", (a, "pT"), 1))
                    if a:
                        pe.wait_ge(att_sem["dve"], att_count.value("dve", (a - 1, s), 1))
                elif a == HEADS:
                    wait_part(pe, att_sem, att_count, "pe", (a, s))
                if s == "score":
                    for t in range(TT):
                        for m in range(2):
                            rows = slice(DH * m, DH * m + DH)
                            last = mm(bank(MIX + 2 + m)[:, T * t:T * t + T], aq[rows, a, t * P:(t + 1) * P], ak[rows, a, :],
                                      start=True, stop=True)
                elif s == "pT":
                    for k in range(2):
                        for t in range(TT):
                            last = turn(mix(0, 2 * k + t), a_p[:, t, k * P:(k + 1) * P], ident)
                elif s == "pv":
                    for t in range(TT):
                        for k in range(2):
                            last = mm(mix(1, t), a_pT[:, k, t, :], av[:, k, a * P:(a + 1) * P], start=(k == 0), stop=(k == 1))
                elif s == "norm":
                    last = turn(mix(0), ident, ident)
                elif s == "turn":
                    for h in range(HEADS):
                        for t in range(TT):
                            last = turn(bank(MIX + h // 2)[:, (h % 2) * T + t * P:(h % 2) * T + t * P + P],
                                        a_od[:, t, h, :], ident)
                last.then_inc(att_sem["pe"], 1)

            for what, i, s in ORDER:
                if what == "pair":
                    pair(i, s)
                    if (i, s) == (0, KC // 2 - 1):
                        turn_small()
                        decay_and_beta()
                    if (i, s) == (1, 1):
                        fold_quarters()
                    if (i, s) == (1, KC // 2 - 1):
                        decay_sums()
                elif what == "gdn":
                    gdn_stage(i, s)
                elif what == "att":
                    att_stage(i, s)

            for k in range(4):
                b0 = 4 * (k % 2)
                if k == 0:
                    pe.wait_ge(block_out, len(BLOCKS) - 1)
                if k == 1:
                    pe.wait_ge(att_sem["act"], att_count.total[1])
                if k >= 2:
                    pe.wait_ge(merge_dve, 4 * (k - 1))
                for br in range(2):
                    if k == 0 and br:
                        pe.wait_ge(block_out, len(BLOCKS))
                    for c in range(HEADS):
                        if k == 0:
                            pe.wait_ge(y_split_l, 4 * br + c // 2 + 1)
                        by_channel(M0 + (2 * k + br) * HEADS + c, b0 + 2 * br, [y[:, c, :] for y in y_part[br]],
                                   c == 0, c == HEADS - 1)

            def turn_sum(k):
                pe.wait_ge(out_dve, 2 * (k + 1))
                pe.wait_ge(turned_read, k) if k else pe.wait_ge(merge_dve, 16)
                for c in range(4):
                    for t in range(TT):
                        last = turn(bank(4 + c // 2)[:, (c % 2) * T + t * P:(c % 2) * T + t * P + P],
                                    x_sb[:, t, NB * k + c * P:NB * k + c * P + P], ident)
                last.then_inc(route_pe, 1)

            def route_logits(k):
                pe.wait_ge(turned_read, k + 1)
                pe.wait_ge(route_in, 32)
                for c in range(4 * k, 4 * k + 4):
                    g = 64 * (c % 2)
                    last = mm(bank(6)[g:g + NR, 0:T], w_route[:, c, :], h2T[:, c, :], start=(c < 2), stop=(c >= KC - 2))
                last.then_inc(route_pe, 1)

            pe.wait_ge(merge_dve, 12)
            for k in range(4):
                if k >= 2:
                    pe.wait_ge(out_dve, 2 * (k - 1))
                for c in range(KC):
                    if k == 0:
                        pe.wait_ge(m_split_l, c // 2 + 1)
                    by_token(O0 + KC * k + c, 2 * (k % 2), [h[:, c, :] for h in h_part], c == 0, c == KC - 1)
                    if k and c == 4:
                        turn_sum(k - 1)
                    if k and c == 10:
                        route_logits(k - 1)
            turn_sum(3)
            route_logits(3)
            pe.wait_ge(route_dve, LG_COPIED)
            for t in range(TT):
                last = mm(bank(7)[:, NR * t:NR * t + NR], lg_T[:, t * P:(t + 1) * P], twice[:, 0:NR], start=True, stop=True)
            last.then_inc(route_pe, 1)
            pe.wait_ge(route_dve, MASK_READY)
            mm(bank(1)[:, 0:NE], before, m_mask[:, 0, :], start=True, stop=True)
            mm(bank(1)[:, NE:2 * NE], before, m_mask[:, 1, :], start=True, stop=False)
            mm(bank(1)[:, NE:2 * NE], ones, m_mask[:, 0, :], start=False, stop=True)
            mm(bank(1)[:, 2 * NE:3 * NE], ones, m_mask[:, 0, :], start=True, stop=False)
            mm(bank(1)[:, 2 * NE:3 * NE], ones, m_mask[:, 1, :], start=False, stop=True).then_inc(route_pe, 1)

            def turn_weights(n):
                pe.wait_ge(pick_ready, 4 * n + 4)
                pe.wait_ge(hid_ready, 2 * n + 3)
                for t in range(TT):
                    last = turn(bank(4)[:, t * P:(t + 1) * P], pick_w[:, t].rearrange("p a b -> p (a b)"), ident)
                last.then_inc(ws_turned, 1)

            def gather(n, groups, sums=None):
                pe.wait_ge(pick_ready, 4 * n + 2)
                for k in groups:
                    pe.wait_ge(gather_read, 4 * n + k + 1)
                    if k == 0 and sums is not None:
                        pe.wait_ge(added, sums + 2)
                    for c in range(4 * k, 4 * k + 4):
                        for i, (t, h2) in enumerate((t, h2) for t in range(TT) for h2 in h2_part):
                            last = mm(bank(k % 2)[:, (c % 4) * P:(c % 4 + 1) * P], h2[:, t, c, :],
                                      pick[:, t].rearrange("p a b -> p (a b)"), start=(i == 0), stop=(i == 2 * TT - 1))
                    last.then_inc(gathered, 1)

            def gate_or_up(X, e, m, halves=(0, 1)):
                pe.wait_ge(gu_copied, 2 * X + 1)
                for u in halves:
                    pe.wait_ge(full[2 * m + u], 16 * X + 16)
                    for c in range(8):
                        g = c % 2
                        last = mm(bank(2 + m)[64 * g:64 * g + 64, :],
                                  xe[:, 8 * u + c, SLOTS * e:SLOTS * e + SLOTS],
                                  expert_unit(2 * m + u, 8, FE)[:, c, :],
                                  start=(u == 0 and c < 2), stop=(u == 1 and c >= 6))
                    last.then_inc(unit_free[m], 1)

            def turn_part(X, m):
                pe.wait_ge(gu_copied, 2 * X + 2 + m)
                for f in range(4):
                    last = mm(bank(4)[:, (4 * m + f) * SLOTS:(4 * m + f + 1) * SLOTS],
                              (g_part, u_part)[m][:, f * P:(f + 1) * P], twice, start=True, stop=True)
                if m:
                    last.then_inc(gu_turned, 1)

            def down(X, halves=(0, 1)):
                pe.wait_ge(hid_ready, X + 2)
                pe.wait_ge(y_copied, 4 * X + 1)
                for u in halves:
                    pe.wait_ge(full[4 + u], 16 * X + 16)
                    for f in range(4):
                        for g in range(2):
                            last = mm(bank(5 + u)[64 * g:64 * g + 64, :], hid[:, f, :],
                                      expert_unit(4 + u, 4, D // 2)[:, f, 512 * g:512 * g + 512],
                                      start=(f == 0), stop=(f == 3))
                    last.then_inc(unit_free[2], 1)

            def scatter(n, blocks, copied=4):
                pe.wait_ge(y_copied, 8 * n + 5 + copied)
                pe.wait_ge(ws_ready, n + 1)
                for t, j in blocks:
                    q = SCATTER.index((t, j))
                    pe.wait_ge(added, 8 * n + q + 1)
                    mm(bank(0 if q % 2 else 7), ws[:, t * P:(t + 1) * P], y_sb[:, j, :],
                       start=True, stop=True).then_inc(scatter_done, 1)

            def pair_in_pipeline(n, first=False, last=False):
                a, b = 2 * n, 2 * n + 1
                if first:
                    gather(n, (0, 1))
                    pe.wait_ge(gather_read, 4)
                    gate_or_up(a, 0, 0, (0,))
                    pe.wait_ge(route_dve, LOW_READY)
                    gather(n, (2, 3))
                    pe.wait_ge(gather_read, 6)
                    gate_or_up(a, 0, 0, (1,))
                else:
                    pe.wait_ge(gather_read, 4 * n + 6)
                    gate_or_up(a, 0, 0)
                    scatter(n - 1, SCATTER[:4])
                gate_or_up(a, 0, 1)
                pe.wait_ge(hid_ready, a + 1)
                turn_part(a, 0)
                if not first:
                    scatter(n - 1, SCATTER[4:])
                turn_part(a, 1)
                gate_or_up(b, 1, 0)
                down(a)
                gate_or_up(b, 1, 1)
                turn_part(b, 0)
                if not last:
                    gather(n + 1, (0, 1), sums=8 * n)
                turn_part(b, 1)
                if not last:
                    gather(n + 1, (2, 3))
                turn_weights(n)
                down(b)
                if last:
                    scatter(n, SCATTER[:4], 2)
                    scatter(n, SCATTER[4:])

            def pair_alone(n):
                gather(n, range(4), sums=8 * n)
                pe.wait_ge(gather_read, 4 * n + 6)
                for e in range(2):
                    gate_or_up(2 * n + e, e, 0)
                    gate_or_up(2 * n + e, e, 1)
                    pe.wait_ge(hid_ready, 2 * n + e + 1)
                    turn_part(2 * n + e, 0)
                    turn_part(2 * n + e, 1)
                    if e == 1:
                        turn_weights(n)
                    down(2 * n + e)
                scatter(n, SCATTER[:4])
                scatter(n, SCATTER[4:])

            pe.sem_inc(gathered, 1)
            pe.sem_inc(scatter_done, 1)
            PAIRS = NE // 2
            pair_in_pipeline(0, first=True)
            with pe.Fori(1, PAIRS - 1) as n:
                pair_in_pipeline(n)
            pair_in_pipeline(PAIRS - 1, last=True)
            pe.wait_ge(route_dve, ROUTE_FLAG)
            with pe.If(pe.value_load(over_i[0:1, 0:1], min_val=0, max_val=1) > 0):
                with pe.Fori(PAIRS, ROUNDS * PAIRS) as n:
                    pair_alone(n)

        @block.scalar
        def _(act):
            act_ = nc.scalar.activation
            line = Line(act, set_act)
            act.dma_start(gmix_c.rearrange("p (u c) -> p u c", u=2), g_mix[0].rearrange("(u p c) -> p u c", u=2, c=8)).then_inc(gmix_in, 16)
            act.wait_ge(set_dve, 2)
            line(act_(nlam, one_c, ACT.Sqrt))
            act.wait_ge(x_in[0], 16)
            line(act_(set_junk[0], x_sb[:, 0, :], ACT.Square, accum_out=ss[:, 0:1]))
            act.wait_ge(x_in[1], 16)
            line(act_(set_junk[0][:, 0:D // 2], x_sb[:, 1, 0:D // 2], ACT.Square, accum_out=ss_half[:, 0:1]))
            act.wait_ge(set_dve, 4)
            line(act_(rstd, ss, ACT.Sqrt, bias=eps_c[:, 0:1], scale=1.0 / D))
            fed = [0]

            def feed(upto):
                while fed[0] < min(upto, CHUNKS):
                    m = fed[0]
                    if m % 4 == 0:
                        act.wait_ge(unit_in[m // 4 % 3], 16 * (m // 12 + 1))
                    if m >= STAGES:
                        act.wait_ge(chunk_used, m - STAGES + 1)
                    act_(w_part[m % STAGES][0], unit(m // 4)[:, m % 4, :], ACT.Copy).then_inc(split_h, 1)
                    fed[0] += 1

            for k in range(8):
                act.wait_ge(set_dve, HT_MADE[k])
                line(act_(h_part[0][:, 2 * k:2 * k + 2, :], hT[:, 2 * k:2 * k + 2, :], ACT.Copy))
                feed(2 * k + 2)
            assert line.n == PARTS_ACT

            def softplus():
                act.wait_ge(set_dve, AB_X)
                line(act_(ab_u, ab_u, ACT.Exp, scale=-1.0))
                line(act_(alog, alog, ACT.Exp))
                line(act_(lam_s, lam_s, ACT.Exp))
                line(act_(ab_u, ab_u, ACT.Ln, bias=one_c[:, 0:1]))
                line(act_(beta, bank(7)[:, 0:64].rearrange("p (t n) -> p t n", t=2)[:, :, 16:32], ACT.Sigmoid))
                assert line.n == SET_ACT

            def decay_exp():
                act.wait_ge(set_dve, GC_READY)
                line(act_(esfx, esfx, ACT.Exp))
                line(act_(begc, gc, ACT.Exp))

            gdn_line = Line(act, gdn_sem["act"])
            att_line = Line(act, att_sem["act"])
            banks_m = banks[:, MIX:MIX + 4, :]
            m01 = banks[:, MIX:MIX + 2, :]
            m23 = banks[:, MIX + 2:MIX + 4, :]

            def flat(ap):
                return ap.rearrange("p a b c d -> p (a b c d)").rearrange("p (x n) -> p x n", n=512)

            def block_end(b):
                kind, _, i = BLOCKS[b]
                src = banks[:, PROJ + 2 * (b % 2):PROJ + 2 * (b % 2) + 2, :]
                if kind in CONV:
                    act.wait_ge(conv_read, 20 * conv_blocks(b))
                    y = {"q": qT, "k": kT, "v": vT}[kind]
                    ins = act_(y, y, ACT.Silu)
                else:
                    act.wait_ge(chunk_used, KC * (b + 1))
                    if kind == "ga" and i == 0:
                        act.wait_ge(gdn_sem["pe"], gdn_count.value("pe", (GDN_BATCHES - 1, "first")))
                        act.wait_ge(gdn_sem["pool"], gdn_count.value("pool", (GDN_BATCHES - 1, "lt3")))
                    if kind == "ga" and i == 2:
                        for e in ("dve", "pool", "pe"):
                            act.wait_ge(gdn_sem[e], gdn_count.total[("dve", "act", "pool", "pe").index(e)])
                    if kind == "z":
                        ins = act_(zs[:, :, NB * i:NB * i + NB], src, ACT.Silu)
                    elif kind == "av":
                        ins = act_(av[:, :, NB * i:NB * i + NB], src, ACT.Copy)
                    elif kind in ("aq", "ak"):
                        y = (aq if kind == "aq" else ak)[:, 4 * i:4 * i + 4, :].rearrange("p a n -> p (a n)")
                        ins = act_(y.rearrange("p (x n) -> p x n", n=512), src, ACT.Copy)
                    else:
                        y = gate(kind == "gd", i)
                        ins = act_(y.rearrange("p (x n) -> p x n", n=512), src, ACT.Sigmoid)
                ins.then_inc(block_out, 1)

            def gdn_stage(b, s, ahead):
                act.wait_ge(gdn_sem["pe"], gdn_count.value("pe", (b, s), 1))
                if s == "norm":
                    gdn_line(act_(rn, bank(MIX + 2)[:, 0:8], ACT.Sqrt, bias=eps_c[:, 0:1]))
                    gdn_line(act_(g_v.rearrange("p a b c -> p (a b c)"), bank(MIX + 1), ACT.Copy))
                elif s == "decay":
                    gdn_line(act_(g_kT.rearrange("p a b -> p (a b)"), bank(MIX), ACT.Copy))
                    gdn_line(act_(flat(g_EG), m23, ACT.Exp))
                    act.wait_ge(gdn_sem["dve"], gdn_count.value("dve", (b, s), 2))
                    gdn_line(act_(g_E.rearrange("p a b c d -> p (a b c d)"), g_E.rearrange("p a b c d -> p (a b c d)"), ACT.Exp))
                elif s == "first":
                    gdn_line(act_(g_T.rearrange("p a b c d -> p (a b c d)"), bank(MIX + 2), ACT.Copy))
                elif s[:2] == "lt":
                    gdn_line(act_(g_Z.rearrange("p a b c d -> p (a b c d)"), bank(MIX), ACT.Copy))
                elif s == "uw":
                    gdn_line(act_(g_WT.rearrange("p r a b c d -> p r (a b c d)"), m23, ACT.Copy))
                elif s == "out":
                    feed(ahead)
                    act.wait_ge(gdn_sem["dve"], gdn_count.value("dve", (b, s), 4))
                    gdn_line(act_(o_r, o_ss, ACT.Sqrt, bias=eps_c[:, 0:1], scale=1.0 / DK))
                elif s == "turn":
                    gdn_line(act_(ya[:, 2 * b:2 * b + 2, :].rearrange("p a b -> p (a b)"), bank(MIX), ACT.Copy, scale=gdn_w))

            def att_stage(a, s, ahead):
                act.wait_ge(att_sem["pe"], att_count.value("pe", (a, s), 1))
                if s == "score":
                    feed(ahead)
                    act.wait_ge(att_sem["dve"], att_count.value("dve", (a, s), 4))
                    for t in range(TT):
                        for m in range(2):
                            i = 2 * t + m
                            att_line(act_(a_s[:, t, m, :], a_s[:, t, m, :], ACT.Exp, bias=nmx[:, i:i + 1],
                                          scale=DH ** -0.5, accum_out=sums[:, i:i + 1]))
                elif s == "pT":
                    att_line(act_(a_pT.rearrange("p a b c -> p (a b c)"), bank(MIX), ACT.Copy))
                elif s == "norm":
                    act.wait_ge(att_sem["dve"], att_count.value("dve", (a, s)))
                    att_line(act_(od_r, od_ss, ACT.Sqrt, bias=eps_c[:, 0:1], scale=1.0 / P))
                elif s == "turn":
                    att_line(act_(yd.rearrange("p a b -> p (a b)").rearrange("p (x n) -> p x n", n=512), banks_m, ACT.Copy,
                                  scale=diff_w))

            feed(LEAD)
            for what, i, s in ORDER:
                if what == "pair":
                    fed_to = KC * i + 2 * s + 2 + LEAD
                    feed(fed_to)
                    if (i, s) == (1, 2):
                        softplus()
                elif what == "conv" and s == TAPS or what == "end" and BLOCKS[i][0] not in CONV and i < len(BLOCKS) - 1:
                    block_end(i)
                elif what == "end" and i == 1:
                    decay_exp()
                elif what == "gdn":
                    gdn_stage(i, s, min(fed_to + 2, M0 + LEAD))
                elif what == "att":
                    att_stage(i, s, min(fed_to + 2, M0 + LEAD))

            def y_high(br):
                y = (ya, yd)[br]
                for i in range(4):
                    act_(y_part[br][0][:, 2 * i:2 * i + 2, :], y[:, 2 * i:2 * i + 2, :], ACT.Copy).then_inc(y_split_h, 1)

            act.wait_ge(chunk_used, M0)
            y_high(0)
            block_end(len(BLOCKS) - 1)
            y_high(1)
            feed(O0 + LEAD - 1)
            act.wait_ge(chunk_used, O0)
            for k in range(8):
                if k == 1:
                    feed(O0 + LEAD)
                act.wait_ge(merge_pool, k // 2 + 1)
                g = gate(0, k // 2)[:, 512 * (k % 2):512 * (k % 2) + 512].rearrange("p (a n) -> p a n", n=T)
                act_(h_part[0][:, 2 * k:2 * k + 2, :], g, ACT.Copy).then_inc(m_split_h, 1)
            rline = Line(act, route_act)
            for k in range(4):
                feed(O0 + KC * (k + 1) + LEAD)
                act.wait_ge(out_dve, 2 * (k + 1))
                for t in range(TT):
                    rline(act_(sq_junk, x_sb[:, t, NB * k:NB * k + NB], ACT.Square, accum_out=ss_part[:, t, k:k + 1]))
            act.wait_ge(route_dve, 2)
            rline(act_(rstd, ss, ACT.Sqrt, bias=eps_c[:, 0:1], scale=1.0 / D))
            act.wait_ge(route_dve, 3)
            for t in range(TT):
                for u in range(2):
                    rline(act_(h2_part[0][:, t, 8 * u:8 * u + 8, :], x_sb[:, t, 1024 * u:1024 * u + 1024].rearrange("p (q c) -> p c q", c=8),
                               ACT.Copy, scale=rstd[:, t:t + 1]))
            act.wait_ge(route_dve, GROUP_MAX)
            rline(act_(rt[:, 0, :, 0:NG], rt[:, 0, :, 0:NG], ACT.Exp))
            act.wait_ge(route_dve, TOP_TWO)
            rline(act_(rs1[:, 7, :], rs1[:, 7, :], ACT.Exp))
            assert rline.n == ROUTE_ACT

            def copy_part(X, m):
                act.wait_ge(unit_free[m], 2 * X + 2)
                act_((g_part, u_part)[m], bank(2 + m), ACT.Copy).then_inc(gu_copied, 1)

            def silu(X):
                act.wait_ge(gu_turned, X + 1)
                act_(silu_g.rearrange("p a b -> p (a b)"), bank(4)[:, 0:T], ACT.Silu).then_inc(silu_done, 1)

            def copy_y(X, e):
                for j in range(4):
                    if j % 2 == 0:
                        act.wait_ge(unit_free[2], 2 * X + 1 + j // 2)
                    g = j % 2
                    act_(y_sb[64 * e:64 * e + 64, j, :], bank(5 + j // 2)[64 * g:64 * g + 64, :],
                         ACT.Copy).then_inc(y_copied, 1)

            def copy_weights(n):
                act.wait_ge(ws_turned, n + 1)
                act_(ws, bank(4)[:, 0:T], ACT.Copy).then_inc(ws_ready, 1)

            def pair_in_pipeline(n):
                a, b = 2 * n, 2 * n + 1
                copy_part(a, 0)
                copy_part(a, 1)
                silu(a)
                copy_part(b, 0)
                act.wait_ge(scatter_done, 8 * n + 1)
                copy_y(a, 0)
                copy_part(b, 1)
                silu(b)
                copy_weights(n)
                copy_y(b, 1)

            def pair_alone(n):
                act.wait_ge(scatter_done, 8 * n + 1)
                for e in range(2):
                    copy_part(2 * n + e, 0)
                    copy_part(2 * n + e, 1)
                    silu(2 * n + e)
                    if e == 1:
                        copy_weights(n)
                    copy_y(2 * n + e, e)

            act.sem_inc(gu_copied, 1)
            act.sem_inc(y_copied, 1)
            with act.Fori(0, NE // 2) as n:
                pair_in_pipeline(n)
            act.wait_ge(route_dve, ROUTE_FLAG)
            with act.If(act.value_load(over_i[0:1, 0:1], min_val=0, max_val=1) > 0):
                with act.Fori(NE // 2, ROUNDS * NE // 2) as n:
                    pair_alone(n)
            act_(nlam, one_c, ACT.Sqrt)
            act.wait_ge(added, 8 * (NE // 2) + 2)
            act.wait_ge(fin_dve, 1)
            act_(junk[0], x_sb[:, 0, :], ACT.Square, accum_out=fin_ss[:, 0:1]).then_inc(fin_act, 1)
            act.wait_ge(fin_act, 1)
            act.wait_ge(fin_dve, 2)
            act_(fin_ss, fin_ss, ACT.Sqrt, bias=eps_c[:, 0:1], scale=1.0 / D).then_inc(fin_act, 1)

        @block.gpsimd
        def _(pool):
            tt_ = nc.gpsimd.tensor_tensor
            gdn_line = Line(pool, gdn_sem["pool"])

            def gdn_stage(b, s):
                here = slice(2 * (b % 2), 2 * (b % 2) + 2)
                if s == "norm":
                    pool.wait_ge(block_out, QKV_THERE[b // 2] - 1)
                    for e in ("dve", "act", "pe"):
                        if gdn_count.value(e, (b, s)):
                            pool.wait_ge(gdn_sem[e], gdn_count.value(e, (b, s)))
                    for i, m in enumerate((qT, kT)):
                        gdn_line(tt_(g_sq[:, i], m[:, here, :], m[:, here, :], ALU.mult))
                    return
                if not GDN[s][2]:
                    return
                pool.wait_ge(gdn_sem["pe"], gdn_count.value("pe", (b, s), 1))
                if s == "decay":
                    pool.wait_ge(gdn_sem["act"], gdn_count.value("act", (b, s), 3))
                    gdn_line(tt_(by_pair(g_E), by_pair(g_E), tri64.unsqueeze(2).broadcast_to([P, 2, 4, CH]), ALU.mult))
                elif s == "first":
                    mask_level(b, 1)
                elif s == "lt1":
                    es = esfx[:, :, 2 * b:2 * b + 2, :].rearrange("p d h t -> p d (h t)")
                    gdn_line(tt_(by_pair(g_KS), g_k.rearrange("p h t n -> p (h t) n").unsqueeze(1).broadcast_to([P, 2, 4, P]),
                                 es.unsqueeze(3).broadcast_to([P, 2, 4, P]), ALU.mult))
                elif s == "lt2":
                    eg_ = g_EG.rearrange("p d h t n -> p d (h t n)")
                    qh = qT[:, here, :].rearrange("p h n -> p (h n)")
                    gdn_line(tt_(eg_, eg_, qh.unsqueeze(1).broadcast_to([P, 2, 2 * T]), ALU.mult))
                elif s[:3] == "sub":
                    mask_level(b, int(s[3:]) + 1)
                elif s == "out":
                    pool.wait_ge(gdn_sem["dve"], gdn_count.value("dve", (b, s), 6))
                    pool.wait_ge(block_out, Z_THERE[b // 2])
                    o2 = g_o.rearrange("p t h n -> p t (h n)")
                    gdn_line(tt_(o2, o2, zs[:, :, 2 * b * P:(2 * b + 2) * P], ALU.mult))

            def by_pair(ap):
                return ap.rearrange("p d h t n -> p d (h t) n")

            def mask_level(b, lv):
                gdn_line(tt_(by_pair(g_UT), by_pair(g_LT), level[:, lv].unsqueeze(2).broadcast_to([P, 2, 4, CH]), ALU.mult))

            pool.wait_ge(set_dve, COLS_READY)
            for what, i, s in ORDER:
                if what == "gdn":
                    gdn_stage(i, s)
            for k in range(4):
                pool.wait_ge(merge_dve, 4 * k + 4)
                tt_(gate(0, k), gate(0, k), gate(1, k), ALU.add).then_inc(merge_pool, 1)

        @block.vector
        def _(dve):
            V = nc.vector
            tt_, ts_, stt_ = V.tensor_tensor, V.tensor_scalar, V.scalar_tensor_tensor
            line = Line(dve, set_dve)
            line(V.memset(one_c, 1.0))
            line(V.memset(eps_c, EPS))
            dve.wait_ge(x_in[1], 16)
            right_half = x_sb[:, 1, D // 2:D]
            line(V.tensor_tensor_reduce(out=set_junk[1][:, 0:D // 2], in0=right_half, in1=right_half,
                                        scale=1.0, scalar=0.0, op0=ALU.mult, op1=ALU.add, accum_out=ss_half[:, 1:2]))
            dve.wait_ge(set_act, 3)
            line(tt_(ss[:, 1:2], ss_half[:, 0:1], ss_half[:, 1:2], ALU.add))
            dve.wait_ge(set_act, 4)
            line(V.reciprocal(rstd, rstd))
            dve.wait_ge(table_in, 16)
            for t in range(TT):
                line(ts_(row_diag[:, t, :], ident, rstd[:, t:t + 1], None, ALU.mult))
            assert line.n == DIAG
            dve.wait_ge(set_pe, 2)
            line(V.tensor_copy(rstd_row, bank(0)[:, 0:T]))
            dve.wait_ge(gmix_in, 16)
            fed = [0]

            def feed(upto):
                while fed[0] < min(upto, CHUNKS):
                    m = fed[0]
                    high, low = w_part[m % STAGES]
                    dve.wait_ge(split_h, m + 1)
                    tt_(low, unit(m // 4)[:, m % 4, :], high.bitcast(F32), ALU.subtract).then_inc(split_l, 1)
                    fed[0] += 1

            for k in range(9):
                if k < 8:
                    if k == 6:
                        dve.wait_ge(set_pe, 3)
                    for c in (2 * k, 2 * k + 1):
                        b = 2 + c // 2 if c < 12 else (c - 12) // 2 + 2
                        line(stt_(hT[:, c, :], bank(b)[:, (c % 2) * T:(c % 2) * T + T], gmix_c[:, c:c + 1], rstd_row,
                                  ALU.mult, ALU.mult))
                    assert line.n == HT_MADE[k]
                if k:
                    dve.wait_ge(set_act, 4 + k)
                    j = slice(2 * k - 2, 2 * k)
                    line(tt_(h_part[1][:, j, :], hT[:, j, :], h_part[0][:, j, :].bitcast(F32), ALU.subtract))
                    assert line.n == HT_LOW[k - 1]
                    feed(2 * k)
            dve.wait_ge(small_in, SMALL_ALL)
            dve.wait_ge(set_pe, 4)
            line(V.tensor_copy(conv_c, bank(4)[:, 0:120]))
            line(V.tensor_copy(gffn_n, bank(4)[:, 128:128 + KC + 2]))
            line(tt_(lam_p, lam_in[:, 0:4:2, :], lam_in[:, 1:4:2, :], ALU.mult))
            line(V.tensor_reduce(lam_s, lam_p, AX.X, ALU.add))
            line(ts_(diff_w, diff_w, 1.0 - LAM_INIT, None, ALU.mult))
            def by_head(v):
                return v.rearrange("p d h t -> p t d h")

            def log_decay():
                dve.wait_ge(set_pe, 6)
                ab_ps = bank(7)[:, 0:64].rearrange("p (t n) -> p t n", t=2)
                line(tt_(ab_x, ab_ps[:, :, 0:16], dtb.unsqueeze(1).broadcast_to([P, TT, 16]), ALU.add))
                line(stt_(ab_u, ab_x, -1.0, ab_x, ALU.mult, ALU.max))
                line(ts_(ab_x, ab_x, 0.0, None, ALU.max))
                assert line.n == AB_X
                dve.wait_ge(set_act, SET_ACT - 1)
                line(tt_(ab_x, ab_x, ab_u, ALU.add))
                line(stt_(g_log, ab_x, -1.0, alog.unsqueeze(1).broadcast_to([P, TT, 16]), ALU.mult, ALU.mult))
                assert line.n == G_READY
                line(tt_(nlam, lam_s[:, 1:2], lam_s[:, 0:1], ALU.subtract))
                line(ts_(nlam, nlam, LAM_INIT, None, ALU.subtract))
                dve.wait_ge(set_act, SET_ACT)

                line(V.tensor_copy(by_head(bcol), beta.rearrange("p t (d h) -> p t d h", d=2)))

            def decay_columns():
                dve.wait_ge(set_pe, 7)
                for v, k in ((gc, 0), (esfx, 2)):
                    for d in range(2):
                        src = bank(6)[:, (k + d) * 16:(k + d) * 16 + 16].rearrange("p (t h) -> p t h", t=2)
                        line(V.tensor_copy(v[:, d].rearrange("p h t -> p t h"), src))
                assert line.n == GC_READY
                dve.wait_ge(set_act, SET_ACT + 2)
                line(tt_(begc, begc, bcol, ALU.mult))
                assert line.n == COLS_READY

            convs = [0]

            def conv(b, k):
                kind, col, _ = BLOCKS[b]
                y = {"q": qT, "k": kT, "v": vT}[kind]
                if k == 0:
                    dve.wait_ge(chunk_used, KC * (b + 1))
                    if conv_blocks(b) == 4:
                        dve.wait_ge(gdn_sem["pe"], gdn_count.value("pe", (1, "first")))
                        dve.wait_ge(gdn_sem["pool"], gdn_count.value("pool", (1, "lt3")))
                tap = (2, 0, 1, 3, 4)[k]
                o = tap - 2
                lo, hi = max(0, -o), T - max(0, o)
                for j in range(4):
                    src = bank(PROJ + 2 * (b % 2) + j // 2)[:, (j % 2) * T:(j % 2 + 1) * T]
                    ct = (col // P) + j
                    w = conv_c[:, tap * 24 + ct:tap * 24 + ct + 1]
                    if k == 0:
                        ins = ts_(y[:, j, :], src, w, None, ALU.mult)
                    else:
                        dve.wait_ge(conv_read, convs[0] - 3)
                        ins = stt_(y[:, j, lo:hi], src[:, lo + o:hi + o], w, y[:, j, lo:hi], ALU.mult, ALU.add)
                    ins.then_inc(conv_read, 1)
                    convs[0] += 1

            gdn_line = Line(dve, gdn_sem["dve"])
            att_line = Line(dve, att_sem["dve"])
            m01 = banks[:, MIX:MIX + 2, :]
            m23 = banks[:, MIX + 2:MIX + 4, :]

            def eight(ap):
                return ap.rearrange("p a b c d -> p (a b c) d")

            def by_pair(ap):
                return ap.rearrange("p d h t n -> p d (h t) n")

            def mats(i):
                return bank(MIX + i).rearrange("p (m n) -> p m n", n=CH)

            def gdn_stage(b, s, ahead):
                if not GDN[s][0]:
                    return
                heads = (2 * b, 2 * b + 1)
                hs = slice(2 * b, 2 * b + 2)
                dve.wait_ge(gdn_sem["pe"], gdn_count.value("pe", (b, s), 1))
                if s == "norm":
                    dve.wait_ge(gdn_sem["act"], gdn_count.value("act", (b, s), 1))
                    gdn_line(V.reciprocal(rr, rn))
                    gdn_line(tt_(g_k.rearrange("p h t n -> p (h t) n"), bank(MIX).rearrange("p (a n) -> p a n", n=P),
                                 spread(rr[:, 4:8], 4, P), ALU.mult))
                    gdn_line(ts_(rr[:, 0:4], rr[:, 0:4], DK ** -0.5, None, ALU.mult))
                elif s == "decay":
                    gcol = gc[:, :, hs].rearrange("p d h t -> p d (h t)").unsqueeze(3).broadcast_to([P, 2, 4, CH])
                    gdn_line(tt_(by_pair(g_E), bank(MIX + 1).rearrange("p (d m n) -> p d m n", d=2, n=CH), gcol, ALU.subtract))
                    gdn_line(ts_(eight(g_E), eight(g_E), 0.0, None, ALU.min))
                    dve.wait_ge(gdn_sem["act"], gdn_count.value("act", (b, s), 2))
                    for d in range(2):
                        off = CH - 1 if d == 0 else 0
                        gdn_line(V.tensor_copy(glast[:, :, d], g_EG[:, d, :, :, off:P:CH]))
                elif s == "gram":
                    dve.wait_ge(gdn_sem["pool"], gdn_count.value("pool", (b, s)))
                    e2, at2, lt2 = (m.rearrange("p d h t n -> p d (h t n)") for m in (g_E, g_AT, g_LT))
                    kk, kq = (bank(MIX + i)[:, 0:4 * CH].unsqueeze(1).broadcast_to([P, 2, 4 * CH]) for i in range(2))
                    gdn_line(tt_(eight(g_LT), mats(2), eight(g_E), ALU.mult))
                    gdn_line(tt_(lt2, kk, lt2, ALU.mult))
                    gdn_line(tt_(by_pair(g_UT), by_pair(g_LT), level[:, 0].unsqueeze(2).broadcast_to([P, 2, 4, CH]), ALU.mult))
                    gdn_line(tt_(eight(g_TT), twice.unsqueeze(1).broadcast_to([P, 8, CH]), eight(g_UT), ALU.subtract))
                    gdn_line(tt_(at2, kq, e2, ALU.mult))
                elif s in ("lt1", "lt2"):
                    dst, src, cols = ((g_XV, g_v, bcol), (g_XK, g_k, begc))[s == "lt2"]
                    c = cols[:, :, hs].rearrange("p d h t -> p d (h t)").unsqueeze(3).broadcast_to([P, 2, 4, P])
                    gdn_line(tt_(by_pair(dst), src.rearrange("p h t n -> p (h t) n").unsqueeze(1).broadcast_to([P, 2, 4, P]),
                                 c, ALU.mult))
                elif s[:3] == "sub":
                    gdn_line(tt_(eight(g_TT), eight(g_TT), mats(2), ALU.subtract))
                    if s != f"sub{LEVELS - 1}":
                        gdn_line(tt_(eight(g_T), eight(g_T), mats(1), ALU.subtract))
                elif s == "uw":
                    gdn_line(V.tensor_copy(eight(g_U), m01.rearrange("p b (m n) -> p (b m) n", n=P)))
                elif s[0] == "s":
                    step = int(s[1])
                    for d in range(2):
                        tile, r = chunk_of(d, step)
                        new = bank(MIX + 2 * d)[:, 0:256].rearrange("p (h n) -> p h n", h=2)
                        if step == 0:
                            gdn_line(V.tensor_copy(g_S[:, :, d, 0, :], new))
                        else:
                            for h in range(2):
                                gdn_line(stt_(g_S[:, h, d, step, :], g_S[:, h, d, step - 1, :],
                                              glast[:, h, d, tile, r:r + 1], new[:, h, :], ALU.mult, ALU.add))
                elif s[0] == "v":
                    for d in range(2):
                        tile, r = chunk_of(d, int(s[1]))
                        rows = slice(64 * r, 64 * r + 64)
                        u = g_U[rows, d, :, tile, :]
                        gdn_line(tt_(u, u, bank(MIX + 1)[rows, 0:256].rearrange("p (h n) -> p h n", h=2), ALU.subtract))
                elif s == "out":
                    for t in range(2):
                        src = bank(MIX + 2 * t)[:, 0:256].rearrange("p (h n) -> p h n", h=2)
                        q = rr[:, 0:4].rearrange("p (h t) -> p t h", h=2)[:, t]
                        gdn_line(tt_(g_o[:, t], src, spread(q, 2, P), ALU.mult))
                    o4 = g_o.rearrange("p t h n -> p (t h) n")
                    gdn_line(tt_(g_osq.rearrange("p t h n -> p (t h) n"), o4, o4, ALU.mult))
                    gdn_line(V.tensor_reduce(o_ss, g_osq.rearrange("p t h n -> p (t h) n"), AX.X, ALU.add))
                    feed(ahead)
                    dve.wait_ge(gdn_sem["act"], gdn_count.value("act", (b, s), 1))
                    gdn_line(V.reciprocal(o_r, o_r))
                    gdn_line(tt_(o4, o4, spread(o_r, 4, P), ALU.mult))

            def att_stage(a, s, ahead):
                if a < HEADS and not ATT[s][0] or a == HEADS and not ATT_END[s][0]:
                    return
                dve.wait_ge(att_sem["pe"], att_count.value("pe", (a, s), 1))
                if s == "score":
                    slope = 2.0 ** (-8.0 * (a + 1) / HEADS)
                    for t in range(TT):
                        ps = banks[:, MIX + 2:MIX + 4, T * t:T * t + T]
                        dd = dist[:, t].unsqueeze(1).broadcast_to([P, 2, T])
                        att_line(stt_(a_s[:, t], dd, -slope * DH ** 0.5, ps, ALU.mult, ALU.add))
                    att_line(V.tensor_reduce(mx, a_s.rearrange("p t m n -> p (t m) n"), AX.X, ALU.max))
                    att_line(ts_(nmx, mx, -DH ** -0.5, None, ALU.mult))
                    feed(ahead)
                    dve.wait_ge(att_sem["act"], att_count.value("act", (a, s), 4))
                    att_line(V.reciprocal(rs, sums))
                    att_line(ts_(rl, rs[:, 1:4:2], nlam[:, 0:1], None, ALU.mult))
                    if a:
                        dve.wait_ge(att_sem["pe"], att_count.value("pe", (a - 1, "pT"), 1))
                    for t in range(TT):
                        att_line(ts_(a_p[:, t, :], a_s[:, t, 0, :], rs[:, 2 * t:2 * t + 1], None, ALU.mult))
                        att_line(stt_(a_p[:, t, :], a_s[:, t, 1, :], rl[:, t:t + 1], a_p[:, t, :], ALU.mult, ALU.add))
                elif s == "pv":
                    o = a_od[:, :, a, :]
                    att_line(V.tensor_copy(o, bank(MIX + 1)[:, 0:256].rearrange("p (t n) -> p t n", t=2)))
                    att_line(tt_(a_sq, o, o, ALU.mult))
                    att_line(V.tensor_reduce(od_ss.rearrange("p (t h) -> p t h", t=2)[:, :, a], a_sq, AX.X, ALU.add))
                elif s == "norm":
                    o = a_od.rearrange("p t h n -> p (t h) n")
                    dve.wait_ge(att_sem["act"], att_count.value("act", (a, s), 1))
                    att_line(V.reciprocal(od_r, od_r))
                    att_line(tt_(o, o, spread(od_r, 16, P), ALU.mult))

            for what, i, s in ORDER:
                if what == "pair":
                    fed_to = KC * i + 2 * s + 2 + LEAD
                    feed(fed_to)
                    if (i, s) == (1, 2):
                        log_decay()
                elif what == "conv" and s < TAPS:
                    conv(i, s)
                elif what == "end":
                    if i == 0:
                        dve.wait_ge(set_pe, 5)
                        line(V.tensor_copy(ab_sums, bank(5)[:, 0:T]))
                        assert line.n == AB_SUMS
                    if i == 1:
                        decay_columns()
                elif what == "gdn":
                    gdn_stage(i, s, min(fed_to + 2, M0 + LEAD))
                elif what == "att":
                    att_stage(i, s, min(fed_to + 2, M0 + LEAD))

            for br, y in enumerate((ya, yd)):
                for i in range(4):
                    j = slice(2 * i, 2 * i + 2)
                    dve.wait_ge(y_split_h, 4 * br + i + 1)
                    tt_(y_part[br][1][:, j, :], y[:, j, :], y_part[br][0][:, j, :].bitcast(F32), ALU.subtract).then_inc(y_split_l, 1)
            def merged_low(k):
                dve.wait_ge(m_split_h, k + 1)
                j = slice(2 * k, 2 * k + 2)
                g = gate(0, k // 2)[:, 512 * (k % 2):512 * (k % 2) + 512].rearrange("p (a n) -> p a n", n=T)
                tt_(h_part[1][:, j, :], g, h_part[0][:, j, :].bitcast(F32), ALU.subtract).then_inc(m_split_l, 1)

            for k in range(4):
                for br in range(2):
                    n = M0 + (2 * k + br + 1) * HEADS
                    feed(n + LEAD - (n == O0))
                    dve.wait_ge(chunk_used, n)
                    if k == 0:
                        dve.wait_ge(block_out, len(BLOCKS))
                    if n == O0:
                        merged_low(0)
                        feed(n + LEAD)
                    for i in range(2):
                        g = gate(br, k)[:, 512 * i:512 * i + 512]
                        tt_(g, bank(4 * (k % 2) + 2 * br + i), g, ALU.mult).then_inc(merge_dve, 1)
            for k in range(1, 8):
                merged_low(k)
            rline = Line(dve, route_dve)
            rline(V.memset(lg_T, 0.0))
            for k in range(4):
                feed(O0 + KC * (k + 1) + LEAD)
                dve.wait_ge(x_again, 16)
                dve.wait_ge(chunk_used, O0 + KC * (k + 1))
                for t in range(TT):
                    y = x_sb[:, t, NB * k:NB * k + NB]
                    tt_(y, y, bank(2 * (k % 2) + t), ALU.add).then_inc(out_dve, 1)
                if k < 3:
                    feed(O0 + KC * (k + 1) + 5 + LEAD)
                dve.wait_ge(route_pe, 2 * k + 1)
                tt_(h2T[:, 4 * k:4 * k + 4, :], banks[:, 4:6, :].rearrange("p b (c n) -> p (b c) n", c=2),
                    spread(gffn_n[:, 4 * k:4 * k + 4], 4, T), ALU.mult).then_inc(turned_read, 1)

            dve.wait_ge(route_act, 8)
            rline(V.tensor_reduce(ss, ss_part, AX.X, ALU.add))
            dve.wait_ge(route_act, 9)
            rline(V.reciprocal(rstd, rstd))
            dve.wait_ge(route_pe, 8)
            for g in (0, 64):
                rline(V.tensor_copy(lg_T[g:g + NR, :], bank(6)[g:g + NR, 0:T]))
            assert rline.n == LG_COPIED

            def low_part(t, u):
                dve.wait_ge(route_act, 10 + 2 * t + u)
                c = slice(8 * u, 8 * u + 8)
                rline(stt_(h2_part[1][:, t, c, :], x_sb[:, t, 1024 * u:1024 * u + 1024].rearrange("p (q c) -> p c q", c=8),
                           rstd[:, t:t + 1], h2_part[0][:, t, c, :].bitcast(F32), ALU.mult, ALU.subtract))

            dve.wait_ge(route_pe, 9)
            for t in range(TT):
                rline(stt_(logits[:, t], bank(7)[:, NR * t:NR * t + NR], rstd[:, t:t + 1], bias_r, ALU.mult, ALU.add))
            glog = logits[:, :, 0:NG]
            BIG = 1024.0

            def per_tile(v, n):
                return v.unsqueeze(2).broadcast_to([P, TT, n])

            def first_max(vals, n, top, hot, tmp):
                iot = iota[:, 0:n].unsqueeze(1).broadcast_to([P, TT, n])
                rline(V.tensor_reduce(top, vals, AX.X, ALU.max))
                rline(tt_(tmp, vals, per_tile(top, n), ALU.is_equal))
                rline(stt_(tmp, tmp, -BIG, iot, ALU.mult, ALU.add))
                rline(V.tensor_reduce(rs1[:, 15, :], tmp, AX.X, ALU.min))
                rline(tt_(hot, tmp, per_tile(rs1[:, 15, :], n), ALU.is_equal))

            ghot = rt[:, 1, :, 0:NG]
            first_max(glog, NG, rs1[:, 0, :], ghot, rt[:, 2, :, 0:NG])
            rline(tt_(rt[:, 0, :, 0:NG], glog, per_tile(rs1[:, 0, :], NG), ALU.subtract))
            assert rline.n == GROUP_MAX
            ehot = rt[:, 3].rearrange("p t (g e) -> p t g e", g=NG)
            el = logits[:, :, NG:NG + NE].rearrange("p t (g e) -> p t g e", g=NG)
            for t in range(TT):
                rline(tt_(ehot[:, t], el[:, t], ghot[:, t, :].unsqueeze(2).broadcast_to([P, NG, EPG]), ALU.mult))
            esel = rt[:, 4, :, 0:EPG]
            for t in range(TT):
                rline(V.tensor_reduce(esel[:, t], ehot[:, t].rearrange("p g e -> p e g"), AX.X, ALU.add))
            hot1, hot2, tmp8 = (rt[:, i, :, 0:EPG] for i in (5, 6, 2))
            first_max(esel, EPG, rs1[:, 1, :], hot1, tmp8)
            rline(stt_(esel, hot1, -1e30, esel, ALU.mult, ALU.add))
            first_max(esel, EPG, rs1[:, 2, :], hot2, tmp8)
            rline(tt_(rs1[:, 7, :], rs1[:, 2, :], rs1[:, 1, :], ALU.subtract))
            assert rline.n == TOP_TWO
            hot12 = rt[:, 2, :, 8:8 + EPG]

            def on_experts(dst, src):
                for t in range(TT):
                    rline(tt_(dst[:, t].rearrange("p (g e) -> p g e", g=NG), src[:, t].unsqueeze(1).broadcast_to([P, NG, EPG]),
                              ghot[:, t, :].unsqueeze(2).broadcast_to([P, NG, EPG]), ALU.mult))

            rline(tt_(hot12, hot1, hot2, ALU.add))
            on_experts(m_mask, hot12)
            assert rline.n == MASK_READY
            low_part(0, 0)
            low_part(1, 0)
            dve.wait_ge(route_pe, 10)
            rank0 = m_rank[:, :, 0:NE]
            rline(stt_(rank0, bank(1)[:, 0:2 * NE].rearrange("p (t n) -> p t n", t=2), 1.0, m_mask, ALU.add, ALU.mult))
            rline(ts_(rank0, rank0, 1.0, None, ALU.subtract))
            rline(V.tensor_reduce(over_f, bank(1)[:, 2 * NE:3 * NE], AX.X, ALU.max))
            assert rline.n == RANK_READ

            def finish_routing():
                rline(ts_(over_f, over_f, float(SLOTS), None, ALU.is_gt))
                rline(V.tensor_copy(over_i, over_f))
                dve.wait_ge(route_act, ROUTE_ACT)
                rline(V.tensor_reduce(rs1[:, 3, :], rt[:, 0, :, 0:NG], AX.X, ALU.add))
                rline(ts_(rs1[:, 4, :], rs1[:, 7, :], 1.0, None, ALU.add))
                rline(tt_(rs1[:, 5, :], rs1[:, 3, :], rs1[:, 4, :], ALU.mult))
                rline(V.reciprocal(rs1[:, 5, :], rs1[:, 5, :]))
                rline(tt_(rs1[:, 6, :], rs1[:, 5, :], rs1[:, 7, :], ALU.mult))
                rline(tt_(rt[:, 7, :, 0:EPG], hot1, per_tile(rs1[:, 5, :], EPG), ALU.mult))
                rline(tt_(rt[:, 7, :, 8:8 + EPG], hot2, per_tile(rs1[:, 6, :], EPG), ALU.mult))
                rline(tt_(rt[:, 7, :, 0:EPG], rt[:, 7, :, 0:EPG], rt[:, 7, :, 8:8 + EPG], ALU.add))
                on_experts(m_weight[:, :, 0:NE], rt[:, 7, :, 0:EPG])
                for r in range(1, ROUNDS):
                    rline(ts_(m_rank[:, :, NE * r:NE * r + NE], rank0, float(SLOTS * r), None, ALU.subtract))
                    rline(V.tensor_copy(m_weight[:, :, NE * r:NE * r + NE], m_weight[:, :, 0:NE]))
                assert rline.n == ROUTE_FLAG

            def picks(n):
                for t in range(TT):
                    r = m_rank[:, t, bass.ds(2 * n, 2)].unsqueeze(2).broadcast_to([P, 2, SLOTS])
                    tt_(pick[:, t], iota.unsqueeze(1).broadcast_to([P, 2, SLOTS]), r, ALU.is_equal).then_inc(pick_ready, 1)

            def weighted_picks(n):
                dve.wait_ge(pick_ready, 4 * n + 2)
                for t in range(TT):
                    w = m_weight[:, t, bass.ds(2 * n, 2)].unsqueeze(2).broadcast_to([P, 2, SLOTS])
                    tt_(pick_w[:, t], pick[:, t].bitcast(F32), w, ALU.mult).then_inc(pick_ready, 1)

            def read_gathered(n, groups):
                for k in groups:
                    dve.wait_ge(gathered, 4 * n + k + 2)
                    tt_(xe[:, 4 * k:4 * k + 4, :], bank(k % 2).rearrange("p (c n) -> p c n", c=4),
                        spread(gffn_c[:, 4 * k:4 * k + 4], 4, P), ALU.mult).then_inc(gather_read, 1)

            def hidden(X):
                dve.wait_ge(silu_done, X + 1)
                tt_(hid.rearrange("p a b -> p (a b)"), silu_g.rearrange("p a b -> p (a b)"), bank(4)[:, T:2 * T],
                    ALU.mult).then_inc(hid_ready, 1)

            def add_scattered(n):
                dve.wait_ge(added, 8 * n + 2)
                for q in range(8):
                    t, j = SCATTER[q]
                    dve.wait_ge(scatter_done, 8 * n + q + 2)
                    y = x_sb[:, t, NB * j:NB * j + NB]
                    tt_(y, y, bank(0 if q % 2 else 7), ALU.add).then_inc(added, 1)

            def pair_in_pipeline(n, first=False, last=False):
                if not first:
                    dve.wait_ge(ws_turned, n)
                weighted_picks(n)
                if not last:
                    dve.wait_ge(gathered, 4 * n + 5)
                    dve.wait_ge(pick_ready, 4 * n + 4)
                    picks(n + 1)
                if not first:
                    add_scattered(n - 1)
                hidden(2 * n)
                if not last:
                    read_gathered(n + 1, (0, 1))
                hidden(2 * n + 1)
                if not last:
                    read_gathered(n + 1, (2, 3))

            def pair_alone(n):
                dve.wait_ge(gathered, 4 * n + 1)
                picks(n)
                dve.wait_ge(ws_turned, n)
                weighted_picks(n)
                read_gathered(n, range(4))
                hidden(2 * n)
                hidden(2 * n + 1)
                add_scattered(n)

            PAIRS = NE // 2
            dve.sem_inc(gather_read, 2)
            dve.sem_inc(added, 2)
            dve.sem_inc(hid_ready, 1)
            picks(0)
            low_part(0, 1)
            low_part(1, 1)
            assert rline.n == LOW_READY
            read_gathered(0, (0, 1))
            finish_routing()
            read_gathered(0, (2, 3))
            pair_in_pipeline(0, first=True)
            with dve.Fori(1, PAIRS - 1) as n:
                pair_in_pipeline(n)
            pair_in_pipeline(PAIRS - 1, last=True)
            add_scattered(PAIRS - 1)
            with dve.If(dve.value_load(over_i[0:1, 0:1], min_val=0, max_val=1) > 0):
                with dve.Fori(PAIRS, ROUNDS * PAIRS) as n:
                    pair_alone(n)
                dve.wait_ge(final_in, 32)
            fline = Line(dve, fin_dve)
            fline(V.memset(over_f, 0.0))
            fline(V.tensor_tensor_reduce(out=junk[1], in0=x_sb[:, 1, :], in1=x_sb[:, 1, :],
                                         scale=1.0, scalar=0.0, op0=ALU.mult, op1=ALU.add, accum_out=fin_ss[:, 1:2]))
            dve.wait_ge(fin_act, 2)
            fline(V.reciprocal(fin_ss, fin_ss))
            dve.wait_ge(final_in, 16)
            for t in range(TT):
                for u in range(2):
                    c = slice(1024 * u, 1024 * u + 1024)
                    fline(stt_(x_sb[:, t, c], x_sb[:, t, c], fin_ss[:, t:t + 1], g_last[:, c], ALU.mult, ALU.mult))
            assert fline.n == FINAL_ROWS


_INS = ["x", "g_mix", "w_in", "conv_w", "a_log", "dt_bias", "gdn_norm_w", "diff_lambda", "diff_norm_w",
        "w_branch_a", "w_branch_d", "w_out", "g_ffn", "w_group", "b_group", "w_router", "b_router",
        "w_exp_gate", "w_exp_up", "w_exp_down", "g_final"]


def kernel(**inputs):
    import numpy as _np
    import concourse.bacc as _bacc
    from concourse import mybir as _mybir
    from concourse.bass_utils import run_bass_kernel_spmd as _run

    nc = _bacc.Bacc("TRN2", target_bir_lowering=False, num_devices=1)
    arrays = {f"in_{name}_dram": _np.ascontiguousarray(inputs[name]) for name in _INS}
    arrays["in_tables_dram"] = constants()
    args = [nc.dram_tensor(name, a.shape, _mybir.dt.from_np(a.dtype), kind="ExternalInput").ap()
            for name, a in arrays.items()]
    args.append(nc.dram_tensor("out_dram", (1, T, D), F32, kind="ExternalOutput").ap())
    encoder(nc, *args)
    r = _run(nc, [arrays], core_ids=[0])
    return r.results[0]["out_dram"]
```
